# Optimizing a Trainium2 kernel written in Bass

```python
import math
import jax, jax.numpy as jnp
from jax import lax
import numpy as np

D_MODEL = 1024
BATCH = 1
SEQ = 256
DEPTH = 1

MEM_LEN = 256
NORM_EPS = 1e-6
SSD_HEAD_DIM = 64
SSD_HEADS = D_MODEL // SSD_HEAD_DIM
SSD_INNER = SSD_HEADS * SSD_HEAD_DIM
SSD_GROUPS = 4
SSD_HEADS_PER_GROUP = SSD_HEADS // SSD_GROUPS
SSD_STATE = 128
SSD_CONV = 4
SSD_CHUNK = 128
SSD_CONV_CH = SSD_INNER + 2 * SSD_GROUPS * SSD_STATE
FOX_HEAD_DIM = 128
FOX_HEADS = D_MODEL // FOX_HEAD_DIM
FOX_INNER = FOX_HEADS * FOX_HEAD_DIM
Q_BLOCK = 128
N_BRANCH = 2
IN_SPLITS = (SSD_INNER, SSD_CONV_CH, SSD_HEADS, FOX_INNER, FOX_INNER, FOX_INNER, FOX_HEADS, N_BRANCH * D_MODEL)
IN_COLS = sum(IN_SPLITS)
X_HEADS = 4
X_HEAD_DIM = D_MODEL // X_HEADS
N_EXPERTS = 32
TOP_K = 4
D_EXPERT = D_MODEL
SWIGLU_ALPHA = 1.702
SWIGLU_LIMIT = 7.0
EXPERT_BLOCK = 128

kernel_name = 'hybrid_ssd_fox_moe_layer'

def rms_norm(x, g):
    xf = x.astype(jnp.float32)
    y = xf * lax.rsqrt(jnp.mean(xf * xf, axis=-1, keepdims=True) + NORM_EPS)
    return (y * g.astype(jnp.float32)).astype(x.dtype)

def causal_depthwise_conv(x, w, b):
    ch = x.shape[-1]
    y = lax.conv_general_dilated(x, w[:, None, :].astype(x.dtype), window_strides=(1,),
                                 padding=[(SSD_CONV - 1, 0)],
                                 dimension_numbers=('NWC', 'WIO', 'NWC'),
                                 feature_group_count=ch)
    return y + b

def ssd_branch(z, xbc, dt_raw, conv_w, conv_b, dt_bias, a_log, d_skip, norm_g):
    Bsz, S, _ = z.shape
    G, E, P, N, Lc = SSD_GROUPS, SSD_HEADS_PER_GROUP, SSD_HEAD_DIM, SSD_STATE, SSD_CHUNK
    nc = S // Lc
    xbc = jax.nn.silu(causal_depthwise_conv(xbc, conv_w, conv_b))
    xs, b_ssm, c_ssm = jnp.split(xbc, [SSD_INNER, SSD_INNER + G * N], axis=-1)
    dt = jax.nn.softplus(dt_raw.astype(jnp.float32) + dt_bias)
    a = -jnp.exp(a_log.astype(jnp.float32)) * dt
    X = xs.reshape(Bsz, nc, Lc, G, E, P)
    Xdt = X * dt.reshape(Bsz, nc, Lc, G, E, 1)
    Bc = b_ssm.reshape(Bsz, nc, Lc, G, N)
    Cc = c_ssm.reshape(Bsz, nc, Lc, G, N)
    a = a.reshape(Bsz, nc, Lc, G, E).transpose(0, 1, 3, 4, 2)
    a_cum = jnp.cumsum(a, axis=-1)
    diff = a_cum[..., :, None] - a_cum[..., None, :]
    causal = jnp.tril(jnp.ones((Lc, Lc), dtype=bool))
    decay_mat = jnp.exp(jnp.where(causal, diff, -jnp.inf))
    cb = jnp.einsum('bclgn,bcsgn->bcgls', Cc, Bc)
    y_diag = jnp.einsum('bcgels,bcsgep->bclgep', cb[:, :, :, None] * decay_mat, Xdt)
    decay_states = jnp.exp(a_cum[..., -1:] - a_cum)
    chunk_states = jnp.einsum('bclgn,bcgel,bclgep->bcgepn', Bc, decay_states, Xdt)
    chunk_decay = jnp.exp(a_cum[..., -1])

    def step(state, inp):
        dec, new = inp
        return dec[..., None, None] * state + new, state

    init = jnp.zeros((Bsz, G, E, P, N), jnp.float32)
    _, states_in = lax.scan(step, init, (chunk_decay.transpose(1, 0, 2, 3),
                                         chunk_states.transpose(1, 0, 2, 3, 4, 5).astype(jnp.float32)))
    states_in = states_in.transpose(1, 0, 2, 3, 4, 5)
    y_off = jnp.einsum('bclgn,bcgepn,bcgel->bclgep', Cc, states_in, jnp.exp(a_cum))
    y = y_diag + y_off + d_skip.reshape(G, E, 1) * X
    y = y.reshape(Bsz, S, G, E * P)
    gated = y * jax.nn.silu(z).reshape(Bsz, S, G, E * P)
    out = rms_norm(gated, norm_g.reshape(G, E * P))
    return out.reshape(Bsz, S, SSD_INNER).astype(z.dtype)

def fox_attention(q, k, v, log_f):
    Bsz, S, H, dh = q.shape
    nb = S // Q_BLOCK
    scale = dh ** -0.5
    c = jnp.cumsum(log_f, axis=1)
    c_keys = c.transpose(0, 2, 1)
    qb = q.reshape(Bsz, nb, Q_BLOCK, H, dh).transpose(1, 0, 2, 3, 4)
    cqb = c.reshape(Bsz, nb, Q_BLOCK, H).transpose(1, 0, 2, 3)
    kpos = jnp.arange(S)

    def block(args):
        qi, ci, i = args
        s = jnp.einsum('bqhd,bkhd->bhqk', qi, k).astype(jnp.float32) * scale
        s = s + ci.transpose(0, 2, 1)[..., None] - c_keys[:, :, None, :]
        qpos = i * Q_BLOCK + jnp.arange(Q_BLOCK)
        s = jnp.where(kpos[None, :] <= qpos[:, None], s, -jnp.inf)
        p = jax.nn.softmax(s, axis=-1)
        return jnp.einsum('bhqk,bkhd->bqhd', p.astype(v.dtype), v)

    out = lax.map(block, (qb, cqb, jnp.arange(nb)))
    return out.transpose(1, 0, 2, 3, 4).reshape(Bsz, S, H * dh)

def memory_cross_attention(u, mem_n, w_q, w_kv, w_o):
    Bsz, S, D = u.shape
    M = mem_n.shape[1]
    q = (u @ w_q).reshape(Bsz, S, X_HEADS, X_HEAD_DIM)
    kv = (mem_n @ w_kv).reshape(Bsz, M, 2, X_HEADS, X_HEAD_DIM)
    k, v = kv[:, :, 0], kv[:, :, 1]
    s = jnp.einsum('bshd,bmhd->bhsm', q, k).astype(jnp.float32) * (X_HEAD_DIM ** -0.5)
    p = jax.nn.softmax(s, axis=-1)
    o = jnp.einsum('bhsm,bmhd->bshd', p.astype(v.dtype), v).reshape(Bsz, S, X_HEADS * X_HEAD_DIM)
    return o @ w_o

def moe_ffn(u, w_router, b_router, w1, b1, w2, b2):
    Bsz, S, D = u.shape
    xf = u.reshape(-1, D)
    n_tok = xf.shape[0]
    logits = (xf @ w_router + b_router).astype(jnp.float32)
    top_vals, top_idx = lax.top_k(logits, TOP_K)
    gates = jax.nn.softmax(top_vals, axis=-1)
    nk = n_tok * TOP_K
    flat_e = top_idx.reshape(-1)
    flat_tok = jnp.arange(nk, dtype=jnp.int32) // TOP_K
    flat_w = gates.reshape(-1)
    order = jnp.argsort(flat_e)
    se = flat_e[order]
    counts = jnp.zeros((N_EXPERTS,), jnp.int32).at[flat_e].add(1)
    padded = (counts + EXPERT_BLOCK - 1) // EXPERT_BLOCK * EXPERT_BLOCK
    start = jnp.cumsum(counts) - counts
    pend = jnp.cumsum(padded)
    pstart = pend - padded
    dest = pstart[se] + (jnp.arange(nk, dtype=jnp.int32) - start[se])
    n_blocks = (nk + EXPERT_BLOCK - 1) // EXPERT_BLOCK + N_EXPERTS
    n_rows = n_blocks * EXPERT_BLOCK
    row_tok = jnp.full((n_rows,), n_tok, jnp.int32).at[dest].set(flat_tok[order])
    row_w = jnp.zeros((n_rows,), jnp.float32).at[dest].set(flat_w[order])
    blk_e = jnp.minimum(jnp.searchsorted(pend, jnp.arange(n_blocks, dtype=jnp.int32) * EXPERT_BLOCK,
                                         side='right'), N_EXPERTS - 1)
    x_pad = jnp.concatenate([xf, jnp.zeros((1, D), xf.dtype)], axis=0)
    x_rows = x_pad[row_tok].reshape(n_blocks, EXPERT_BLOCK, D)

    def expert_block(args):
        xb, e = args
        hgl = xb @ w1[e] + b1[e]
        glu = jnp.minimum(hgl[:, :D_EXPERT], SWIGLU_LIMIT)
        lin = jnp.clip(hgl[:, D_EXPERT:], -SWIGLU_LIMIT, SWIGLU_LIMIT)
        act = glu * jax.nn.sigmoid(SWIGLU_ALPHA * glu) * (lin + 1.0)
        return act @ w2[e] + b2[e]

    y_rows = lax.map(expert_block, (x_rows, blk_e)).reshape(n_rows, D)
    y_rows = y_rows * row_w[:, None].astype(y_rows.dtype)
    out = jax.ops.segment_sum(y_rows, row_tok, num_segments=n_tok + 1)[:n_tok]
    return out.reshape(Bsz, S, D).astype(u.dtype)

def hybrid_layer(h, mem, norm_mix_g, w_in, conv_w, conv_b, dt_bias, a_log, d_skip, ssd_norm_g,
                 w_ssd_branch, b_forget, w_fox_branch, b_gates, w_out, norm_cross_g, norm_mem_g,
                 w_cross_q, w_cross_kv, w_cross_o, norm_ffn_g, w_router, b_router,
                 w_expert_in, b_expert_in, w_expert_out, b_expert_out):
    Bsz, S, D = h.shape
    u = rms_norm(h, norm_mix_g)
    proj = u @ w_in
    cuts = np.cumsum(IN_SPLITS)[:-1].tolist()
    z, xbc, dt_raw, q, k, v, f_logit, gate_logit = jnp.split(proj, cuts, axis=-1)
    y_ssd = ssd_branch(z, xbc, dt_raw, conv_w, conv_b, dt_bias, a_log, d_skip, ssd_norm_g)
    log_f = jax.nn.log_sigmoid((f_logit + b_forget).astype(jnp.float32))
    hs = (Bsz, S, FOX_HEADS, FOX_HEAD_DIM)
    y_fox = fox_attention(q.reshape(hs), k.reshape(hs), v.reshape(hs), log_f)
    gates = jax.nn.sigmoid(gate_logit + b_gates.reshape(-1)).reshape(Bsz, S, N_BRANCH, D)
    merged = gates[:, :, 0] * (y_ssd @ w_ssd_branch) + gates[:, :, 1] * (y_fox @ w_fox_branch)
    h = h + merged @ w_out
    h = h + memory_cross_attention(rms_norm(h, norm_cross_g), rms_norm(mem, norm_mem_g),
                                   w_cross_q, w_cross_kv, w_cross_o)
    h = h + moe_ffn(rms_norm(h, norm_ffn_g), w_router, b_router,
                    w_expert_in, b_expert_in, w_expert_out, b_expert_out)
    return h

def setup_inputs(seed: int = 0) -> dict:
    key = jax.random.key(seed)
    ks = jax.random.split(key, 32)
    f32 = jnp.float32
    L = DEPTH

    def normal(k, shape, scale):
        return jax.random.normal(k, shape, f32) * scale

    def gain(k, shape):
        return 1.0 + 0.05 * jax.random.normal(k, shape, f32)

    dt0 = jnp.exp(jax.random.uniform(ks[6], (L, SSD_HEADS), f32, math.log(1e-3), math.log(1e-1)))
    return {
        'x': normal(ks[0], (BATCH, SEQ, D_MODEL), 1.0),
        'mem': normal(ks[1], (BATCH, MEM_LEN, D_MODEL), 1.0),
        'norm_mix_g': gain(ks[2], (L, D_MODEL)),
        'w_in': normal(ks[3], (L, D_MODEL, IN_COLS), D_MODEL ** -0.5),
        'conv_w': normal(ks[4], (L, SSD_CONV, SSD_CONV_CH), SSD_CONV ** -0.5),
        'conv_b': normal(ks[5], (L, SSD_CONV_CH), 0.02),
        'dt_bias': dt0 + jnp.log(-jnp.expm1(-dt0)),
        'a_log': jnp.log(jax.random.uniform(ks[7], (L, SSD_HEADS), f32, 1.0, 16.0)),
        'd_skip': gain(ks[8], (L, SSD_HEADS)),
        'ssd_norm_g': gain(ks[9], (L, SSD_INNER)),
        'w_ssd_branch': normal(ks[10], (L, SSD_INNER, D_MODEL), SSD_INNER ** -0.5),
        'b_forget': 2.0 + 0.5 * jax.random.normal(ks[11], (L, FOX_HEADS), f32),
        'w_fox_branch': normal(ks[12], (L, FOX_INNER, D_MODEL), FOX_INNER ** -0.5),
        'b_gates': normal(ks[13], (L, N_BRANCH, D_MODEL), 0.02),
        'w_out': normal(ks[14], (L, D_MODEL, D_MODEL), D_MODEL ** -0.5),
        'norm_cross_g': gain(ks[15], (L, D_MODEL)),
        'norm_mem_g': gain(ks[16], (L, D_MODEL)),
        'w_cross_q': normal(ks[17], (L, D_MODEL, X_HEADS * X_HEAD_DIM), D_MODEL ** -0.5),
        'w_cross_kv': normal(ks[18], (L, D_MODEL, 2 * X_HEADS * X_HEAD_DIM), D_MODEL ** -0.5),
        'w_cross_o': normal(ks[19], (L, X_HEADS * X_HEAD_DIM, D_MODEL), D_MODEL ** -0.5),
        'norm_ffn_g': gain(ks[20], (L, D_MODEL)),
        'w_router': normal(ks[21], (L, D_MODEL, N_EXPERTS), D_MODEL ** -0.5),
        'b_router': normal(ks[22], (L, N_EXPERTS), 0.01),
        'w_expert_in': normal(ks[23], (L, N_EXPERTS, D_MODEL, 2 * D_EXPERT), D_MODEL ** -0.5),
        'b_expert_in': normal(ks[24], (L, N_EXPERTS, 2 * D_EXPERT), 0.02),
        'w_expert_out': normal(ks[25], (L, N_EXPERTS, D_EXPERT, D_MODEL), D_EXPERT ** -0.5),
        'b_expert_out': normal(ks[26], (L, N_EXPERTS, D_MODEL), 0.02),
        'norm_final_g': gain(ks[27], (D_MODEL,)),
    }

def reference(x, mem, norm_mix_g, w_in, conv_w, conv_b, dt_bias, a_log, d_skip, ssd_norm_g,
              w_ssd_branch, b_forget, w_fox_branch, b_gates, w_out, norm_cross_g, norm_mem_g,
              w_cross_q, w_cross_kv, w_cross_o, norm_ffn_g, w_router, b_router,
              w_expert_in, b_expert_in, w_expert_out, b_expert_out, norm_final_g):
    h = x
    for l in range(DEPTH):
        h = hybrid_layer(h, mem, norm_mix_g[l], w_in[l], conv_w[l], conv_b[l], dt_bias[l], a_log[l],
                         d_skip[l], ssd_norm_g[l], w_ssd_branch[l], b_forget[l], w_fox_branch[l],
                         b_gates[l], w_out[l], norm_cross_g[l], norm_mem_g[l], w_cross_q[l],
                         w_cross_kv[l], w_cross_o[l], norm_ffn_g[l], w_router[l], b_router[l],
                         w_expert_in[l], b_expert_in[l], w_expert_out[l], b_expert_out[l])
    return rms_norm(h, norm_final_g)


_drawn_inputs = setup_inputs


def setup_inputs(seed=0):
    import zlib

    import numpy as np

    out = dict(_drawn_inputs(seed))
    spreads = {}
    factors = {'norm_cross_g': 3.188, 'b_expert_in': 5.777, 'b_expert_out': 6.636, 'b_gates': 3.649}
    for name, (base, spread) in spreads.items():
        noise = np.random.default_rng([zlib.crc32(name.encode()), seed]).standard_normal(out[name].shape)
        drawn = base * np.exp(spread * noise) if base else spread * noise
        out[name] = __import__('jax').numpy.asarray(drawn.astype(out[name].dtype))
    for name, factor in factors.items():
        out[name] = (out[name] * factor).astype(out[name].dtype)
    return out
```

```python
from contextlib import ExitStack

import numpy as np

import concourse.bass as bass
from concourse import mybir

D = 1024
S = 256
P = 128
KT = D // P
TB = S // P
SSD_H, SSD_P = 16, 64
SSD_G = 4
FOX_H = 8
X_H, X_D = 4, 256
NE, TOPK = 32, 4
DE = 1024
SLOTS = 64
MAX_EXTRA = S // SLOTS - 1
MAX_ITEMS = NE + TOPK * S // SLOTS
NI = 64
EPS = 1e-6
LIMIT, ALPHA = 7.0, 1.702
NO_SLOT = 4096.0
MASKED = -1e30
FOX_SCALE = 128 ** -0.5
X_SCALE = X_D ** -0.5

C_Z, C_XBC, C_DT, C_Q, C_K, C_V, C_F, C_G = 0, 1024, 3072, 3088, 4112, 5136, 6160, 6168


def layer_program(nc, x, mem, norm_mix_g, w_in, conv_w, conv_b, dt_bias, a_log, d_skip, ssd_norm_g,
                  w_ssd, b_forget, w_fox, b_gates, w_out, norm_cross_g, norm_mem_g, w_cq, w_ckv, w_co,
                  norm_ffn_g, w_router, b_router, w_ein, b_ein, w_eout, b_eout, norm_final_g, out):
    f32, i32, u32 = mybir.dt.float32, mybir.dt.int32, mybir.dt.uint32
    ALU = mybir.AluOpType
    ACT = mybir.ActivationFunctionType
    AX = mybir.AxisListType

    groups = []

    def add(name, w, col0, n):
        for j in range(n):
            groups.append((name, w[:, col0 + 512 * j:col0 + 512 * (j + 1)]))

    win = w_in[0]
    add("xbc", win, C_XBC, 4)
    add("z", win, C_Z, 2)
    add("q", win, C_Q, 2)
    add("k", win, C_K, 2)
    add("v", win, C_V, 2)
    add("gate", win, C_G, 4)
    add("ck", w_ckv[0], 0, 2)
    add("cv", w_ckv[0], D, 2)
    add("ssd", w_ssd[0], 0, 2)
    add("fox", w_fox[0], 0, 2)
    add("out", w_out[0], 0, 2)
    add("cq", w_cq[0], 0, 2)
    add("co", w_co[0], 0, 2)
    NG = len(groups)
    FIRST = {}
    for g, (name, _) in enumerate(groups):
        FIRST.setdefault(name, g)
    NUNITS = {name: 2 * sum(n == name for n, _ in groups) for name in FIRST}
    ON_ACT = {"xbc", "z", "q", "gate", "cq"}

    def unit(name, n):
        return 2 * FIRST[name] + n

    def drained(u):
        act = groups[u // 2][0] in ON_ACT
        return act, sum((groups[v // 2][0] in ON_ACT) == act for v in range(u + 1))

    PJ = 3

    with ExitStack() as ctx:
        def sb(name, shape, dt=f32):
            return ctx.enter_context(nc.sbuf_tensor(name, shape, dt))

        def sem(name):
            return ctx.enter_context(nc.semaphore(name))

        ring = sb("ring", [P, 12 * 2048])
        wst = sb("wst", [P, 2 * 4096])
        hT = sb("hT", [P, KT, S])
        uT = sb("uT", [P, KT, S])
        muT = sb("muT", [P, KT, S])
        kxT = sb("kxT", [P, KT, S])
        Vx = sb("Vx", [P, TB, D])
        sq = sb("sq", [P, KT, S])
        merged = sb("merged", [P, KT, S])
        xtok = sb("xtok", [P, TB, D])

        def view(t, at, n):
            return t[:, at:at + n]

        def tiles(ap, n):
            return ap.rearrange("p (c t) -> p c t", c=n)

        xb = tiles(view(ring, 0, 16 * 260), 16)
        yssd = tiles(view(ring, 0, 2048), KT)
        yfox = tiles(view(ring, 2048, 2048), KT)
        xc = tiles(view(ring, 4160, 4096), 16)
        zs = tiles(view(ring, 8256, 2048), KT)
        qT = tiles(view(ring, 10304, 2048), KT)
        kT = tiles(view(ring, 12352, 2048), KT)
        V = tiles(view(ring, 14400, 2048), TB)
        gate = tiles(view(ring, 16448, 4096), 16)
        xdt = tiles(view(ring, 20544, 2048), TB)
        cbm = tiles(view(ring, 22592, 1536), SSD_G)
        PT = view(ring, 22592, 384)
        xflat = xtok[:, :, :].rearrange("p a b -> p (a b)")
        dm = [view(xflat, 384 * j, 384) for j in range(2)]
        negc = view(xflat, 768, 384)
        ft = [view(xflat, 1152 + 384 * j, 384) for j in range(2)]
        mflat = merged[:, :, :].rearrange("p a b -> p (a b)")
        memtok = mflat.rearrange("p (a b) -> p a b", a=TB)
        rsg = view(mflat, 0, 1024)
        ytmp = [view(mflat, 1024 + 256 * j, 256) for j in range(2)]
        mtmp = uT
        xp = [view(mflat, 512 * j, 512) for j in range(2)]
        xPT = view(mflat, 1024, 512)
        qx = muT
        ox = sq

        def w_at(j, n):
            return view(wst, j, n)

        b1 = w_at(0, 2048)
        b2 = w_at(2048, 1024)
        xgs = w_at(3072, 512)
        xgT = w_at(3584, 512)
        glu = w_at(4096, 512)
        sig = w_at(4608, 512)
        lin = w_at(5120, 512)
        actT = w_at(5632, 512)
        ys = w_at(6144, 512)
        sgT = w_at(6656, 256)
        sg = w_at(6912, 256)
        sel = w_at(7168, 128)
        selb = w_at(7296, 64)
        gfin = view(mflat, 0, 1024)
        outsb = muT[:, :, :].rearrange("p a b -> p (a b)").rearrange("p (a b) -> p a b", a=TB)

        ident = sb("ident", [P, P])
        tri = sb("tri", [P, 384])
        fmask = sb("fmask", [P, 384])
        c_d = sb("c_d", [P, P])
        c_g = sb("c_g", [P, P])
        c_s = sb("c_s", [P, P])
        eps = sb("eps", [P, 1])
        prow = sb("prow", [P, P])
        prow2 = sb("prow2", [16, P])
        prm = sb("prm", [P, 144])
        bdf = sb("bdf", [P, 24])
        alog = sb("alog", [P, SSD_H])
        brt = sb("brt", [P, NE])
        dall = sb("dall", [P, SSD_H])
        dsk = sb("dsk", [P, KT])
        wdf = sb("wdf", [P, KT, 24])
        wrt = sb("wrt", [P, KT, NE])
        raw = sb("raw", [P, TB, 24])
        sp = sb("sp", [P, TB, 24])
        dt = sb("dt", [P, TB, SSD_H])
        af = sb("af", [P, TB, 24])
        actok = sb("actok", [P, TB, 24])
        acT = sb("acT", [24, S])
        rs = sb("rs", [P, S])
        mx = sb("mx", [P, 2, 2])
        rsum = sb("rsum", [P, 2, 2])
        rinv = sb("rinv", [P, 2, 2])
        iota = sb("iota", [P, 2, NI])
        iotai = sb("iotai", [P, 2, NI], i32)
        rowi = sb("rowi", [P, 1], i32)
        rowf = sb("rowf", [P, 1])
        kflat = kxT[:, :, :].rearrange("p a b -> p (a b)")
        table_at = iter(range(0, KT * S, 64))

        def table(n, rows=P):
            at = [next(table_at) for _ in range(n)][0]
            return kflat[0:rows, at:at + 64 * n]

        def by_block(ap):
            return ap.rearrange("p (b n) -> p b n", b=TB)

        lg, em, msk, gt, posm = (by_block(table(1)) for _ in range(5))
        v8 = sb("v8", [P, TB, 8])
        i8 = sb("i8", [P, TB, 8], u32)
        i8f = sb("i8f", [P, TB, 8])
        smal = sb("smal", [P, TB, 4])
        posT, gtT = table(4, NE), table(4, NE)
        ec = sb("ec", [NE, 8])
        pe1, pe2, pb2 = table(1, NE), table(1, NE), table(1, NE)
        ipos = by_block(table(2))
        igate = by_block(table(2))
        meta = sb("meta", [1, NI + 1], i32)

        ps = ctx.enter_context(nc.psum_tensor("ps", [P, 8, 512], f32))

        CW, CB, G_MIX, G_CROSS, G_MEM, G_FFN, G_SSD, B_GATE = 0, 64, 80, 88, 96, 104, 112, 120

        ld_x, ld_mem, ld_prm, ld_small = sem("ld_x"), sem("ld_mem"), sem("ld_prm"), sem("ld_small")
        w_loaded = [sem("w_loaded0"), sem("w_loaded1")]
        unit_full = sem("unit_full")
        act_drained, dve_drained = sem("act_drained"), sem("dve_drained")
        consts, ld_skip, dsk_ready = sem("consts"), sem("ld_skip"), sem("dsk_ready")
        pool_chain, dve_chain, act_chain = sem("pool_chain"), sem("dve_chain"), sem("act_chain")
        prm_psum, prm_ready = sem("prm_psum"), sem("prm_ready")
        tr_psum, tr_copied, tr_squared = sem("tr_psum"), sem("tr_copied"), sem("tr_squared")
        squared = sem("squared")
        ms_psum, ms_root, normed = sem("ms_psum"), sem("ms_root"), sem("normed")
        df_psum, df_raw, df_soft, df_ready = sem("df_psum"), sem("df_raw"), sem("df_soft"), sem("df_ready")
        cum_psum, cum_ready = sem("cum_psum"), sem("cum_ready")
        conved, xc_ready = sem("conved"), sem("xc_ready")
        xdt_psum, xdt_ready = sem("xdt_psum"), sem("xdt_ready")
        cb_psum, cb_ready = sem("cb_psum"), sem("cb_ready")
        sb_psum, s_diff, s_exp, s_mt, sy_psum = (sem("sb_psum"), sem("s_diff"), sem("s_exp"),
                                                 sem("s_mt"), sem("sy_psum"))
        y_read, gated, gsq = sem("y_read"), sem("gated"), sem("gsq")
        gms_psum, g_root, yssd_ready = sem("gms_psum"), sem("g_root"), sem("yssd_ready")
        f_psum, f_score, f_exp, f_rinv, f_norm = (sem("f_psum"), sem("f_score"), sem("f_exp"),
                                                  sem("f_rinv"), sem("f_norm"))
        pt_psum, pt_copied, fo_psum, yfox_ready = (sem("pt_psum"), sem("pt_copied"), sem("fo_psum"),
                                                   sem("yfox_ready"))
        gate_sig = sem("gate_sig")
        x_psum, x_max, x_exp, x_rinv, x_norm = (sem("x_psum"), sem("x_max"), sem("x_exp"),
                                                sem("x_rinv"), sem("x_norm"))
        xpt_psum, xpt_copied, xo_psum, ox_ready = (sem("xpt_psum"), sem("xpt_copied"),
                                                   sem("xo_psum"), sem("ox_ready"))
        tok_psum, tok_ready = sem("tok_psum"), sem("tok_ready")
        lg_psum, lg_ready, top_ready, ex_ready, msk_ready = (
            sem("lg_psum"), sem("lg_ready"), sem("top_ready"), sem("ex_ready"), sem("msk_ready"))
        cnt_psum, extra_ready, off_psum, posm_ready, ptr_psum, ptr_ready = (
            sem("cnt_psum"), sem("extra_ready"), sem("off_psum"), sem("posm_ready"),
            sem("ptr_psum"), sem("ptr_ready"))
        table_ready, item_psum, item_ready, meta_ready = (
            sem("table_ready"), sem("item_psum"), sem("item_ready"), sem("meta_ready"))
        ld_b = sem("ld_b")
        ld_g = sem("ld_g")
        e_loaded = [sem(f"e_loaded{s}") for s in range(12)]
        e_used = sem("e_used")
        sel_ready, sg_ready, selb_ready = sem("sel_ready"), sem("sg_ready"), sem("selb_ready")
        h_psum, glu_ready, sig_ready, act_ready = (sem("h_psum"), sem("glu_ready"),
                                                   sem("sig_ready"), sem("act_ready"))
        xg_psum, xg_copied, xgt_psum, xgt_ready = (sem("xg_psum"), sem("xg_copied"),
                                                   sem("xgt_psum"), sem("xgt_ready"))
        sgt_psum, sgt_ready, at_psum, at_ready = (sem("sgt_psum"), sem("sgt_ready"),
                                                  sem("at_psum"), sem("at_ready"))
        y_psum, y_ready = sem("y_psum"), sem("y_ready")
        acc_done, f_sq, f_root, out_ready, stored = (sem("acc_done"), sem("f_sq"), sem("f_root"),
                                                     sem("out_ready"), sem("stored"))

        def e_chunk(expert, s):
            if s < 8:
                return w_ein[0, expert, s * P:(s + 1) * P, :]
            t = s - 8
            return w_eout[0, expert, 2 * t * P:2 * (t + 1) * P, :].rearrange("(c p) n -> p c n", p=P)

        def e_slot(s):
            ap = ring[:, 2048 * s:2048 * (s + 1)]
            return ap if s < 8 else ap.rearrange("p (c n) -> p c n", c=2)

        block = ctx.enter_context(nc.Block())

        @block.sync
        def _(sp_):
            sp_.dma_start(xtok[:, :, :], x[0].rearrange("(b p) d -> p b d", p=P)).then_inc(ld_x, 16)
            for at, src in ((CW, conv_w[0].rearrange("k (c p) -> (k c) p", p=P)),
                            (CB, conv_b[0].rearrange("(c p) -> c p", p=P)),
                            (G_MIX, norm_mix_g[0].rearrange("(c p) -> c p", p=P)),
                            (G_CROSS, norm_cross_g[0].rearrange("(c p) -> c p", p=P)),
                            (G_MEM, norm_mem_g[0].rearrange("(c p) -> c p", p=P)),
                            (G_FFN, norm_ffn_g[0].rearrange("(c p) -> c p", p=P)),
                            (G_SSD, ssd_norm_g[0].rearrange("(c p) -> c p", p=P))):
                sp_.dma_start(prow[at:at + src.shape[0], :], src).then_inc(ld_prm, 16)
            sp_.dma_start(prow2[:, :], b_gates[0].rearrange("b (c p) -> (b c) p", p=P)).then_inc(ld_prm, 16)

            def load_group(g):
                if g >= 2:
                    sp_.wait_ge(unit_full, 2 * (g - 1))
                sp_.dma_start(wst[:, 4096 * (g % 2):4096 * (g % 2 + 1)].rearrange("p (k n) -> p k n", k=KT),
                              groups[g][1].rearrange("(k p) n -> p k n", p=P)).then_inc(w_loaded[g % 2], 16)

            load_group(0)
            sp_.dma_start(memtok, mem[0].rearrange("(b p) d -> p b d", p=P)).then_inc(ld_mem, 16)
            for g in range(1, FIRST["out"] + 2):
                load_group(g)
            sp_.wait_ge(dve_drained, drained(unit("fox", 3))[1])
            s = 0
            for g in range(FIRST["cq"], NG):
                for _ in range(3):
                    sp_.dma_start(e_slot(s), e_chunk(0, s)).then_inc(e_loaded[s], 16)
                    s += 1
                load_group(g)
            sp_.wait_ge(unit_full, 2 * NG)
            sp_.dma_start(b1[0:NE, :], b_ein[0]).then_inc(ld_b, 16)
            sp_.dma_start(b2[0:NE, :], b_eout[0]).then_inc(ld_b, 16)
            sp_.wait_ge(ox_ready, X_H)
            sp_.wait_ge(dve_drained, drained(NG * 2 - 1)[1])
            sp_.dma_start(gfin, norm_final_g.partition_broadcast(P)).then_inc(ld_g, 16)
            with sp_.Fori(1, NE) as i:
                for s in range(12):
                    sp_.wait_ge(e_used, 12 * i + (s - 10))
                    sp_.dma_start(e_slot(s), e_chunk(i, s)).then_inc(e_loaded[s], 16)
            sp_.wait_ge(meta_ready, 1)
            n_items = sp_.value_load(meta[0:1, NI:NI + 1], min_val=NE, max_val=MAX_ITEMS)
            with sp_.If(n_items > NE):
                with sp_.Fori(NE, n_items) as i:
                    e = sp_.value_load(meta[0:1, bass.ds(i, 1)], min_val=0, max_val=NE - 1)
                    for s in range(12):
                        sp_.wait_ge(e_used, 12 * i + (s - 10))
                        sp_.dma_start(e_slot(s), e_chunk(e, s)).then_inc(e_loaded[s], 16)
            for tb in range(TB):
                sp_.wait_ge(out_ready, tb + 1)
                sp_.dma_start(out[0, tb * P:(tb + 1) * P, :], outsb[:, tb, :]).then_inc(stored, 16)
            sp_.wait_ge(stored, 16 * TB)

        @block.gpsimd
        def _(pool):
            done = [0]

            def link(ins):
                done[0] += 1
                ins.then_inc(pool_chain, 1)
                pool.wait_ge(pool_chain, done[0])

            nc.gpsimd.memset(ident[:, :], 0.0).then_inc(pool_chain, 1)
            nc.gpsimd.memset(tri[:, :], 1.0).then_inc(pool_chain, 1)
            nc.gpsimd.memset(fmask[:, :], 0.0).then_inc(pool_chain, 1)
            done[0] = 3
            pool.wait_ge(pool_chain, 3)
            nc.gpsimd.affine_select(out=ident[:, :], in_=ident[:, :], compare_op=ALU.not_equal, fill=1.0,
                                    base=0, pattern=[[-1, P]], channel_multiplier=1).then_inc(consts, 1)
            nc.gpsimd.memset(c_d[:, :], 1.0 / D).then_inc(consts, 1)
            nc.gpsimd.memset(eps[:, :], EPS).then_inc(consts, 1)
            for at in (0, 256):
                nc.gpsimd.affine_select(out=tri[:, at:at + P], in_=tri[:, at:at + P], compare_op=ALU.is_ge,
                                        fill=0.0, base=0, pattern=[[1, P]], channel_multiplier=-1).then_inc(consts, 1)
                nc.gpsimd.affine_select(out=fmask[:, at:at + P], in_=fmask[:, at:at + P], compare_op=ALU.is_ge,
                                        fill=MASKED, base=0, pattern=[[-1, P]], channel_multiplier=1).then_inc(consts, 1)
            nc.gpsimd.memset(c_g[:, :], 1.0 / 256).then_inc(consts, 1)
            nc.gpsimd.memset(c_s[:, :], -float(SLOTS)).then_inc(consts, 1)
            link(nc.gpsimd.iota(iotai[:, :, :], pattern=[[0, 2], [1, NI]], base=0, channel_multiplier=0))
            nc.gpsimd.tensor_copy(iota[:, :, :], iotai[:, :, :]).then_inc(consts, 1)
            link(nc.gpsimd.iota(rowi[:, :], pattern=[[0, 1]], base=0, channel_multiplier=1))
            nc.gpsimd.tensor_copy(rowf[:, :], rowi[:, :]).then_inc(consts, 1)
            nc.gpsimd.memset(xb[:, :, 0:4], 0.0).then_inc(consts, 1)
            pool.dma_start(wdf[:, :, 0:16], win[:, C_DT:C_DT + 16].rearrange("(k p) n -> p k n", p=P)).then_inc(ld_small, 16)
            pool.dma_start(wdf[:, :, 16:24], win[:, C_F:C_F + 8].rearrange("(k p) n -> p k n", p=P)).then_inc(ld_small, 16)
            pool.dma_start(bdf[:, 0:16], dt_bias[0].partition_broadcast(P)).then_inc(ld_small, 16)
            pool.dma_start(bdf[:, 16:24], b_forget[0].partition_broadcast(P)).then_inc(ld_small, 16)
            pool.dma_start(alog[:, :], a_log[0].partition_broadcast(P)).then_inc(ld_small, 16)
            pool.dma_start(brt[:, :], b_router[0].partition_broadcast(P)).then_inc(ld_small, 16)
            pool.dma_start(dall[:, :], d_skip[0].partition_broadcast(P)).then_inc(ld_skip, 16)
            pool.dma_start(wrt[:, :, :], w_router[0].rearrange("(k p) n -> p k n", p=P)).then_inc(ld_small, 16)
            pool.wait_ge(ld_skip, 16)
            pool.wait_ge(consts, 12)
            for j in range(2):
                rows = slice(64 * j, 64 * (j + 1))
                nc.gpsimd.tensor_copy(dsk[rows, :], dall[rows, j:SSD_H:2]).then_inc(dsk_ready, 1)
                pool.wait_ge(dsk_ready, j + 1)
            pool.wait_ge(cb_ready, SSD_G)
            for h in range(SSD_H):
                pool.wait_ge(s_exp, h + 1)
                nc.gpsimd.tensor_tensor(dm[h % 2], dm[h % 2], cbm[:, h // 4, :], ALU.mult).then_inc(s_mt, 1)
            for h in range(FOX_H):
                pool.wait_ge(f_rinv, h + 1)
                nc.gpsimd.tensor_scalar(ft[h % 2][:, 0:P], ft[h % 2][:, 0:P], rinv[:, h % 2, 0:1], None, ALU.mult).then_inc(f_norm, 1)
                nc.gpsimd.tensor_scalar(ft[h % 2][:, P:384], ft[h % 2][:, P:384], rinv[:, h % 2, 1:2], None, ALU.mult).then_inc(f_norm, 1)
            for h in range(X_H):
                pool.wait_ge(x_rinv, h + 1)
                for b in range(TB):
                    t = xp[h % 2][:, S * b:S * (b + 1)]
                    nc.gpsimd.tensor_scalar(t, t, rinv[:, h % 2, b:b + 1], None, ALU.mult).then_inc(x_norm, 1)

        @block.tensor
        def _(pe):
            mm = nc.tensor.matmul
            idn = ident[:, :]

            def transposes(src, n):
                for j in range(4):
                    if n:
                        pe.wait_ge(tr_copied, 4 * (n - 1) + j + 1)
                    for c in (2 * j, 2 * j + 1):
                        for tb in range(TB):
                            at = (c % 2) * S + tb * P
                            last = nc.tensor.transpose(ps[:, 4 + j, at:at + P], src[:, tb, c * P:(c + 1) * P], idn)
                    last.then_inc(tr_psum, 1)

            def mean_square(at):
                for c in range(KT):
                    last = mm(ps[:, 3, at:at + S], c_d[:, :], sq[:, c, :], start=(c == 0), stop=(c == KT - 1))
                last.then_inc(ms_psum, 1)

            def project(name, n, act):
                u = unit(name, n)
                g = u // 2
                if u % 2 == 0:
                    pe.wait_ge(w_loaded[g % 2], 16 * (g // 2 + 1))
                if u >= PJ:
                    on_act, count = drained(u - PJ)
                    pe.wait_ge(act_drained if on_act else dve_drained, count)
                w = wst[:, 4096 * (g % 2):4096 * (g % 2 + 1)].rearrange("p (k n) -> p k n", k=KT)
                for j in range(2):
                    for k in range(KT):
                        cols = (u % 2) * 256
                        if name in ("v", "cv"):
                            lhs, rhs = act[:, k, j * P:(j + 1) * P], w[:, k, cols:cols + 256]
                        else:
                            lhs, rhs = w[:, k, cols + j * P:cols + (j + 1) * P], act[:, k, :]
                        last = mm(ps[:, u % PJ, j * 256:(j + 1) * 256], lhs, rhs,
                                  start=(k == 0), stop=(k == KT - 1))
                last.then_inc(unit_full, 1)

            pe.wait_ge(consts, 2)
            pe.wait_ge(ld_prm, 16 * 8)
            nc.tensor.transpose(ps[:, 3, 0:120], prow[0:120, :], ident[0:120, 0:120])
            nc.tensor.transpose(ps[:, 3, 120:136], prow2[:, :], ident[0:16, 0:16]).then_inc(prm_psum, 1)
            pe.wait_ge(ld_x, 16)
            transposes(xtok, 0)
            pe.wait_ge(prm_ready, 1)
            pe.wait_ge(tr_squared, 4)
            mean_square(256)
            pe.wait_ge(ld_mem, 16)
            transposes(memtok, 1)
            pe.wait_ge(normed, 1)
            for n in range(4):
                project("xbc", n, uT)
            pe.wait_ge(tr_squared, 8)
            mean_square(0)
            for n in range(4, 8):
                project("xbc", n, uT)
            pe.wait_ge(ld_small, 16 * 7)
            pe.wait_ge(ms_root, 2)
            for tb in range(TB):
                for k in range(KT):
                    last = mm(ps[:, 3, 32 * tb:32 * tb + 24], uT[:, k, tb * P:(tb + 1) * P], wdf[:, k, :],
                              start=(k == 0), stop=(k == KT - 1))
            last.then_inc(df_psum, 1)
            for n in range(4):
                project("z", n, uT)
            pe.wait_ge(consts, 11)
            pe.wait_ge(df_ready, 1)
            mm(ps[:, 3, 64:88], tri[:, 0:P], af[:, 0, :], start=True, stop=True)
            mm(ps[:, 3, 96:120], tri[:, P:2 * P], af[:, 0, :], start=True, stop=False)
            mm(ps[:, 3, 96:120], tri[:, 0:P], af[:, 1, :], start=False, stop=True)
            mm(ps[0:24, 3, 256:512], af[:, 0, :], tri[:, 0:S], start=True, stop=False)
            mm(ps[0:24, 3, 256 + P:512], af[:, 1, :], tri[:, 0:P], start=False, stop=True).then_inc(cum_psum, 1)
            for n in range(4):
                project("q", n, uT)
            pe.wait_ge(tr_copied, 8)
            for j in range(4):
                tb, half = j // 2, j % 2
                pe.wait_ge(xc_ready, 4 * (half + 1))
                for c in range(4):
                    last = nc.tensor.transpose(ps[:, 4 + j, c * P:(c + 1) * P],
                                               xc[:, 4 * half + c, tb * P:(tb + 1) * P], idn)
                last.then_inc(xdt_psum, 1)
            for n in range(2):
                project("k", n, uT)
            pe.wait_ge(xc_ready, 16)
            for g in range(SSD_G):
                pe.wait_ge(xdt_ready, g + 1)
                mm(ps[:, 4 + g, 0:S], xc[:, 8 + g, 0:P], xc[:, 12 + g, :], start=True, stop=True)
                mm(ps[:, 4 + g, S:384], xc[:, 8 + g, P:S], xc[:, 12 + g, P:S], start=True, stop=True).then_inc(cb_psum, 1)
            for n in range(2, 4):
                project("k", n, uT)
            fill = [("v", n) for n in range(4)] + [("gate", n) for n in range(8)]
            pe.wait_ge(cum_ready, 2)
            pe.wait_ge(cb_ready, SSD_G)

            def running_sum(bank, r):
                return mm(ps[:, bank, 0:S], ident[0:24, r:r + 1].to_broadcast([24, P]), acT[0:24, :],
                          start=True, stop=True)

            for h in range(SSD_H + 1):
                if h < SSD_H:
                    if h >= 2:
                        pe.wait_ge(s_diff, 2 * (h - 1))
                    running_sum(4 + h % 2, h).then_inc(sb_psum, 1)
                if h >= 1:
                    y, c = h - 1, (h - 1) // 2
                    if y % 2 == 0 and c >= 2:
                        pe.wait_ge(y_read, c - 1)
                    pe.wait_ge(s_mt, y + 1)
                    o = ps[(y % 2) * 64:(y % 2) * 64 + 64, 6 + c % 2, :]
                    mm(o[:, 0:S], xdt[:, 0, y * 64:(y + 1) * 64], dm[y % 2][:, 0:S], start=True, stop=False)
                    mm(o[:, P:S], xdt[:, 1, y * 64:(y + 1) * 64], dm[y % 2][:, S:384],
                       start=False, stop=True).then_inc(sy_psum, 1)
                if h < SSD_H and h % 4 != 0:
                    name, n = fill.pop(0)
                    project(name, n, uT)
            pe.wait_ge(gsq, KT)
            pe.wait_ge(s_diff, 2 * SSD_H)
            for g in range(SSD_G):
                for j in range(2):
                    last = mm(ps[:, 4 + g // 2, (g % 2) * S:(g % 2) * S + S], c_g[:, :], sq[:, 2 * g + j, :],
                              start=(j == 0), stop=(j == 1))
            last.then_inc(gms_psum, 1)
            fill = [("ck", n) for n in range(4)] + [("cv", n) for n in range(4)]
            name, n = fill.pop(0)
            pe.wait_ge(normed, 2)
            project(name, n, muT)
            pe.wait_ge(g_root, 1)
            pe.wait_ge(y_read, 8)
            for h in range(FOX_H + 1):
                if h < FOX_H:
                    if h >= 1:
                        pe.wait_ge(f_score, 4 * h)
                    running_sum(4, SSD_H + h)
                    mm(ps[:, 6 + h % 2, 0:P], qT[:, h, 0:P], kT[:, h, 0:P], start=True, stop=True)
                    mm(ps[:, 6 + h % 2, P:384], qT[:, h, P:S], kT[:, h, :], start=True, stop=True).then_inc(f_psum, 1)
                if h < FOX_H - 1:
                    name, n = fill.pop(0)
                    project(name, n, muT)
                if h >= 1:
                    y = h - 1
                    pe.wait_ge(f_norm, 2 * h)
                    if y >= 1:
                        pe.wait_ge(pt_copied, y)
                    for j in range(3):
                        last = nc.tensor.transpose(ps[:, 3, j * P:(j + 1) * P], ft[y % 2][:, j * P:(j + 1) * P], idn)
                    last.then_inc(pt_psum, 1)
                    pe.wait_ge(pt_copied, y + 1)
                    if y >= 1:
                        pe.wait_ge(yfox_ready, y)
                    o = ps[:, 5, 0:S]
                    mm(o, V[:, 0, y * P:(y + 1) * P], PT[:, 0:S], start=True, stop=False)
                    mm(o[:, P:S], V[:, 1, y * P:(y + 1) * P], PT[:, S:384], start=False, stop=True).then_inc(fo_psum, 1)
            pe.wait_ge(yssd_ready, KT)
            for n in range(4):
                project("ssd", n, yssd)
            pe.wait_ge(yfox_ready, FOX_H)
            for n in range(4):
                project("fox", n, yfox)
            pe.wait_ge(dve_drained, drained(unit("fox", 3))[1])
            for n in range(4):
                project("out", n, merged)
            pe.wait_ge(squared, KT)
            mean_square(0)
            pe.wait_ge(normed, 3)
            for n in range(4):
                project("cq", n, uT)
            pe.wait_ge(act_drained, drained(unit("cq", 3))[1])
            for h in range(X_H + 1):
                if h < X_H:
                    if h >= 2:
                        pe.wait_ge(x_exp, 2 * (h - 1))
                    for b in range(TB):
                        for j in range(2):
                            last = mm(ps[:, 6 + h % 2, b * S:(b + 1) * S], qx[:, 2 * h + j, b * P:(b + 1) * P],
                                      kxT[:, 2 * h + j, :], start=(j == 0), stop=(j == 1))
                    last.then_inc(x_psum, 1)
                if h >= 1:
                    y = h - 1
                    pe.wait_ge(x_norm, 2 * h)
                    if y >= 1:
                        pe.wait_ge(xpt_copied, y)
                    for m in range(TB):
                        for b in range(TB):
                            at = m * S + b * P
                            last = nc.tensor.transpose(ps[:, 3, at:at + P],
                                                       xp[y % 2][:, b * S + m * P:b * S + (m + 1) * P], idn)
                    last.then_inc(xpt_psum, 1)
                    pe.wait_ge(xpt_copied, y + 1)
                    if y >= 2:
                        pe.wait_ge(ox_ready, y - 1)
                    for j in range(2):
                        for m in range(TB):
                            last = mm(ps[:, 4 + y % 2, j * S:(j + 1) * S],
                                      Vx[:, m, (2 * y + j) * P:(2 * y + j + 1) * P],
                                      xPT[:, m * S:(m + 1) * S], start=(m == 0), stop=(m == TB - 1))
                    last.then_inc(xo_psum, 1)
            pe.wait_ge(ox_ready, X_H)
            for n in range(4):
                project("co", n, ox)
            pe.wait_ge(squared, 2 * KT)
            mean_square(0)
            pe.wait_ge(normed, 4)
            for tb in range(TB):
                for k in range(KT):
                    last = mm(ps[:, 3, 256 + NE * tb:256 + NE * (tb + 1)], uT[:, k, tb * P:(tb + 1) * P], wrt[:, k, :],
                              start=(k == 0), stop=(k == KT - 1))
            last.then_inc(lg_psum, 1)
            for j in range(4):
                tb, half = j // 2, j % 2
                for c in range(4):
                    last = nc.tensor.transpose(ps[:, 4 + j, c * P:(c + 1) * P],
                                               uT[:, 4 * half + c, tb * P:(tb + 1) * P], idn)
                last.then_inc(tok_psum, 1)
            pe.wait_ge(msk_ready, TB)
            mm(ps[:, 0, 0:NE], tri[:, 0:P], msk[:, 0, :], start=True, stop=True)
            mm(ps[:, 0, NE:2 * NE], tri[:, P:2 * P], msk[:, 0, :], start=True, stop=False)
            mm(ps[:, 0, NE:2 * NE], tri[:, 0:P], msk[:, 1, :], start=False, stop=True)
            mm(ps[0:NE, 0, 64:65], msk[:, 0, :], tri[:, P:P + 1], start=True, stop=False)
            mm(ps[0:NE, 0, 64:65], msk[:, 1, :], tri[:, P:P + 1], start=False, stop=True).then_inc(cnt_psum, 1)
            pe.wait_ge(extra_ready, 1)
            mm(ps[0:NE, 1, 0:1], tri[0:NE, 0:NE], ec[:, 1:2], start=True, stop=True)
            mm(ps[0:1, 1, 1:2], tri[0:NE, P:P + 1], ec[:, 1:2], start=True, stop=True).then_inc(off_psum, 1)
            pe.wait_ge(posm_ready, 1)
            for tb in range(TB):
                nc.tensor.transpose(ps[0:NE, 2, tb * P:(tb + 1) * P], posm[:, tb, :], idn)
                last = nc.tensor.transpose(ps[0:NE, 2, S + tb * P:S + (tb + 1) * P], gt[:, tb, :], idn)
            last.then_inc(ptr_psum, 1)
            pe.wait_ge(table_ready, 1)
            pe.wait_ge(ptr_ready, 2)
            for tb in range(TB):
                mm(ps[:, 0, 128 + NI * tb:128 + NI * (tb + 1)], posT[:, tb * P:(tb + 1) * P], pe1[:, :], start=True, stop=False)
                mm(ps[:, 0, 128 + NI * tb:128 + NI * (tb + 1)], c_s[0:NE, :], pb2[:, :], start=False, stop=True)
                mm(ps[:, 0, 256 + NI * tb:256 + NI * (tb + 1)], gtT[:, tb * P:(tb + 1) * P], pe1[:, :], start=True, stop=True)
            mm(ps[0:1, 0, 384:384 + NI], rowf[0:NE, :], pe1[:, :], start=True, stop=True).then_inc(item_psum, 1)
            pe.wait_ge(ld_b, 32)
            pe.wait_ge(tok_ready, 4)
            for j in range(4):
                tb, half = j // 2, j % 2
                mm(ps[:, 4 + j, :], gtT[:, tb * P:(tb + 1) * P], b2[0:NE, half * 512:(half + 1) * 512],
                   start=True, stop=False, skip_group_check=True)

            xg_cols = xgT.rearrange("p (m a j) -> p m a j", m=4, a=2)
            at_cols = actT.rearrange("p (m a j) -> p m a j", m=4, a=2)

            def gather(i1):
                pe.wait_ge(sel_ready, 2 * i1)
                for tb in range(TB):
                    for half in range(2):
                        last = mm(ps[64 * half:64 * (half + 1), 2, :], sel[:, 64 * tb:64 * (tb + 1)],
                                  xtok[:, tb, 512 * half:512 * (half + 1)], start=(tb == 0), stop=(tb == TB - 1))
                last.then_inc(xg_psum, 1)

            def gathered_transposes(i1):
                pe.wait_ge(xg_copied, i1)
                for m in range(4):
                    last = nc.tensor.transpose(ps[:, 2, m * P:(m + 1) * P], xgs[:, m * P:(m + 1) * P], idn)
                last.then_inc(xgt_psum, 1)

            def scatter():
                for tb in range(TB):
                    for half in range(2):
                        rows = slice(64 * half, 64 * (half + 1))
                        last = mm(ps[:, 4 + 2 * tb + half, :], sgT[rows, tb * P:(tb + 1) * P], ys[rows, :],
                                  start=False, stop=False, skip_group_check=True)
                return last

            pe.wait_ge(item_ready, 2)
            gather(1)
            gathered_transposes(1)
            pe.wait_ge(meta_ready, 1)
            n_items = pe.value_load(meta[0:1, NI:NI + 1], min_val=NE, max_val=MAX_ITEMS)
            with pe.Fori(0, n_items) as i:
                pe.wait_ge(selb_ready, i + 1)
                pe.wait_ge(xgt_ready, i + 1)
                for b in range(2):
                    for half in range(2):
                        last = mm(ps[64 * half:64 * (half + 1), b, :], selb[0:NE, :],
                                  b1[0:NE, b * DE + 512 * half:b * DE + 512 * (half + 1)], start=True, stop=False)
                last.then_inc(e_used, 1)
                for s in range(8):
                    pe.wait_ge(e_loaded[s], 16 * i + 16)
                    for b in range(2):
                        for half in range(2):
                            last = mm(ps[64 * half:64 * (half + 1), b, :], xg_cols[:, s % 4, s // 4, :],
                                      e_slot(s)[:, b * DE + 512 * half:b * DE + 512 * (half + 1)],
                                      start=False, stop=(s == 7))
                    last.then_inc(e_used if s < 7 else h_psum, 1)
                pe.wait_ge(y_ready, i + 1)
                pe.wait_ge(sgt_ready, i + 1)
                scatter().then_inc(e_used, 1)
                gather(i + 2)
                pe.wait_ge(sg_ready, 2 * i + 2)
                for tb in range(TB):
                    last = nc.tensor.transpose(ps[:, 3, tb * P:(tb + 1) * P], sg[:, tb * P:(tb + 1) * P], idn)
                last.then_inc(sgt_psum, 1)
                gathered_transposes(i + 2)
                pe.wait_ge(act_ready, i + 1)
                for m in range(4):
                    last = nc.tensor.transpose(ps[:, 0, m * P:(m + 1) * P], lin[:, m * P:(m + 1) * P], idn)
                last.then_inc(at_psum, 1)
                pe.wait_ge(at_ready, i + 1)
                pe.wait_ge(sgt_ready, i + 2)
                for s in range(8, 12):
                    pe.wait_ge(e_loaded[s], 16 * i + 16)
                    for c in range(2):
                        k = 2 * (s - 8) + c
                        for half in range(2):
                            last = mm(ps[64 * half:64 * (half + 1), 3, :], at_cols[:, k % 4, k // 4, :],
                                      e_slot(s)[:, c, 512 * half:512 * (half + 1)],
                                      start=(k == 0), stop=(k == 7))
                    last.then_inc(e_used if s < 11 else y_psum, 1)
            pe.wait_ge(y_ready, n_items + 1)
            scatter()
            for j in range(4):
                tb, half = j // 2, j % 2
                for c in range(4):
                    last = mm(ps[:, 4 + j, c * P:(c + 1) * P], hT[:, 4 * half + c, tb * P:(tb + 1) * P], idn,
                              start=False, stop=(c == 3), skip_group_check=True)
            last.then_inc(acc_done, 1)

        @block.scalar
        def _(act):
            A = nc.scalar.activation
            done = [0]

            def link(ins):
                done[0] += 1
                ins.then_inc(act_chain, 1)
                act.wait_ge(act_chain, done[0])

            def squares(n, src):
                for j in range(4):
                    act.wait_ge(tr_copied, 4 * n + j + 1)
                    A(sq[:, 2 * j:2 * j + 2, :], src[:, 2 * j:2 * j + 2, :], ACT.Square).then_inc(tr_squared, 1)

            def root(n, at):
                act.wait_ge(ms_psum, n + 1)
                if n:
                    act.wait_ge(normed, n)
                A(rs[:, :], ps[:, 3, at:at + S], ACT.Sqrt, bias=eps[:, :]).then_inc(ms_root, 1)

            def drain(name, n):
                u = unit(name, n)
                act.wait_ge(unit_full, u + 1)
                bank = ps[:, u % PJ, :]
                two = bank.rearrange("p (a b) -> p a b", a=2)
                if name == "xbc":
                    ins = A(xb[:, 2 * n:2 * n + 2, 4:4 + S], two, ACT.Copy)
                elif name == "z":
                    ins = A(zs[:, 2 * n:2 * n + 2, :], two, ACT.Silu)
                elif name == "q":
                    ins = A(qT[:, 2 * n:2 * n + 2, :], two, ACT.Copy, scale=FOX_SCALE)
                elif name == "cq":
                    ins = A(qx[:, 2 * n:2 * n + 2, :], two, ACT.Copy, scale=X_SCALE)
                else:
                    for j in range(2):
                        c = 2 * n + j
                        ins = A(gate[:, c, :], bank[:, j * S:(j + 1) * S], ACT.Identity,
                                bias=prm[:, B_GATE + c:B_GATE + c + 1])
                ins.then_inc(act_drained, 1)

            act.wait_ge(consts, 3)
            squares(0, hT)
            root(0, 256)
            act.wait_ge(ms_psum, 1)
            squares(1, muT)
            act.wait_ge(consts, 12)
            for n in range(4):
                drain("xbc", n)
            root(1, 0)
            for n in range(4, 8):
                drain("xbc", n)
            for c in range(16):
                act.wait_ge(conved, c + 1)
                A(xc[:, c, :], xc[:, c, :], ACT.Silu, bias=prm[:, CB + c:CB + c + 1]).then_inc(xc_ready, 1)
                if c % 4 == 3:
                    drain("z", c // 4)
            act.wait_ge(df_raw, 1)
            link(A(sp[:, :, :], raw[:, :, :], ACT.Abs))
            link(A(sp[:, :, :], sp[:, :, :], ACT.Exp, scale=-1.0))
            A(alog[:, :], alog[:, :], ACT.Exp).then_inc(df_soft, 1)
            A(sp[:, :, :], sp[:, :, :], ACT.Ln, bias=1.0).then_inc(df_soft, 1)
            for n in range(4):
                drain("q", n)
            fill = [("v", n) for n in range(4)] + [("gate", n) for n in range(8)]
            for h in range(SSD_H + 2):
                if h < SSD_H:
                    act.wait_ge(s_diff, 2 * h + 2)
                    A(dm[h % 2], dm[h % 2], ACT.Exp).then_inc(s_exp, 1)
                if h < SSD_H and h % 4 != 0:
                    name, n = fill.pop(0)
                    if name in ON_ACT:
                        drain(name, n)
                if h >= 2 and h % 2 == 0:
                    c = h // 2 - 1
                    act.wait_ge(gated, c + 1)
                    A(sq[:, c, :], zs[:, c, :], ACT.Square).then_inc(gsq, 1)
            act.wait_ge(gms_psum, 1)
            A(rsg, ps[:, 4:6, :].rearrange("p a b -> p (a b)"), ACT.Sqrt, bias=eps[:, :]).then_inc(g_root, 1)
            for h in range(FOX_H + 1):
                if h < FOX_H:
                    act.wait_ge(f_score, 4 * h + 4)
                    t = ft[h % 2]
                    A(t[:, 0:P], t[:, 0:P], ACT.Exp, bias=mx[:, h % 2, 0:1], accum_out=rsum[:, h % 2, 0:1]).then_inc(f_exp, 1)
                    A(t[:, P:384], t[:, P:384], ACT.Exp, bias=mx[:, h % 2, 1:2], accum_out=rsum[:, h % 2, 1:2]).then_inc(f_exp, 1)
                if h >= 1:
                    y = h - 1
                    act.wait_ge(pt_psum, y + 1)
                    if y >= 1:
                        act.wait_ge(fo_psum, y)
                    A(PT, ps[:, 3, 0:384], ACT.Copy).then_inc(pt_copied, 1)
                    act.wait_ge(fo_psum, y + 1)
                    A(yfox[:, y, :], ps[:, 5, 0:S], ACT.Copy).then_inc(yfox_ready, 1)
            act.wait_ge(act_drained, drained(unit("gate", 7))[1])
            A(gate[:, :, :], gate[:, :, :], ACT.Sigmoid).then_inc(gate_sig, 1)

            def norm_squares(first):
                for c in range(KT):
                    if c % 2 == 0:
                        act.wait_ge(dve_drained, first + c // 2)
                    A(sq[:, c, :], hT[:, c, :], ACT.Square).then_inc(squared, 1)

            norm_squares(drained(unit("out", 0))[1])
            root(2, 0)
            for n in range(4):
                drain("cq", n)
            for h in range(X_H + 1):
                if h < X_H:
                    act.wait_ge(x_max, h + 1)
                    if h >= 2:
                        act.wait_ge(xpt_psum, h - 1)
                    for b in range(TB):
                        A(xp[h % 2][:, S * b:S * (b + 1)], ps[:, 6 + h % 2, S * b:S * (b + 1)], ACT.Exp,
                          bias=mx[:, h % 2, b:b + 1], accum_out=rsum[:, h % 2, b:b + 1]).then_inc(x_exp, 1)
                if h >= 1:
                    y = h - 1
                    act.wait_ge(xpt_psum, y + 1)
                    if y >= 1:
                        act.wait_ge(xo_psum, y)
                    A(xPT, ps[:, 3, :], ACT.Copy).then_inc(xpt_copied, 1)
                    act.wait_ge(xo_psum, y + 1)
                    A(ox[:, 2 * y:2 * y + 2, :].rearrange("p a b -> p (a b)"), ps[:, 4 + y % 2, :], ACT.Copy).then_inc(ox_ready, 1)
            act.wait_ge(unit_full, 2 * NG)
            norm_squares(drained(unit("co", 0))[1])
            root(3, 0)
            for j in range(4):
                act.wait_ge(tok_psum, j + 1)
                A(xtok[:, j // 2, 512 * (j % 2):512 * (j % 2 + 1)], ps[:, 4 + j, :], ACT.Copy).then_inc(tok_ready, 1)
            act.wait_ge(top_ready, 1)
            for tb in range(TB):
                A(em[:, tb, :], lg[:, tb, :], ACT.Exp, bias=smal[:, tb, 0:1]).then_inc(ex_ready, 1)
            act.wait_ge(ptr_psum, 1)
            A(posT[:, :], ps[0:NE, 2, 0:S], ACT.Copy).then_inc(ptr_ready, 1)
            A(gtT[:, :], ps[0:NE, 2, S:2 * S], ACT.Copy).then_inc(ptr_ready, 1)

            def gathered_copy(i1):
                act.wait_ge(xg_psum, i1)
                A(xgs, ps[:, 2, :], ACT.Copy).then_inc(xg_copied, 1)

            gathered_copy(1)
            act.wait_ge(meta_ready, 1)
            n_items = act.value_load(meta[0:1, NI:NI + 1], min_val=NE, max_val=MAX_ITEMS)
            with act.Fori(0, n_items) as i:
                act.wait_ge(glu_ready, i + 1)
                A(sig, glu, ACT.Sigmoid, scale=ALPHA).then_inc(sig_ready, 1)
                gathered_copy(i + 2)
                act.wait_ge(sgt_psum, i + 1)
                A(sgT, ps[:, 3, 0:S], ACT.Copy).then_inc(sgt_ready, 1)
                act.wait_ge(at_psum, i + 1)
                A(actT, ps[:, 0, :], ACT.Copy).then_inc(at_ready, 1)
                act.wait_ge(y_psum, i + 1)
                A(ys, ps[:, 3, :], ACT.Copy).then_inc(y_ready, 1)
            act.wait_ge(acc_done, 1)
            for tb in range(TB):
                A(outsb[:, tb, :], ps[:, 4 + 2 * tb:6 + 2 * tb, :].rearrange("p a b -> p (a b)"), ACT.Square,
                  accum_out=smal[:, tb, 2:3]).then_inc(f_sq, 1)
            act.wait_ge(f_sq, 2)
            A(smal[:, :, 3], smal[:, :, 2], ACT.Sqrt, scale=1.0 / D, bias=eps[:, :]).then_inc(f_root, 1)

        @block.vector
        def _(dve):
            V_ = nc.vector
            done = [0]

            def link(ins):
                done[0] += 1
                ins.then_inc(dve_chain, 1)
                dve.wait_ge(dve_chain, done[0])

            def apply_norm(n, src, dst, gain):
                dve.wait_ge(ms_root, n + 1)
                link(V_.reciprocal(rs[:, :], rs[:, :]))
                for c in range(KT):
                    last = V_.scalar_tensor_tensor(out=dst[:, c, :], in0=src[:, c, :],
                                                   scalar=prm[:, gain + c:gain + c + 1], in1=rs[:, :],
                                                   op0=ALU.mult, op1=ALU.mult)
                last.then_inc(normed, 1)

            def copies(n, dst):
                for j in range(4):
                    dve.wait_ge(tr_psum, 4 * n + j + 1)
                    V_.tensor_copy(dst[:, 2 * j:2 * j + 2, :].rearrange("p a b -> p (a b)"), ps[:, 4 + j, :]).then_inc(tr_copied, 1)

            def drain(name, n):
                u = unit(name, n)
                dve.wait_ge(unit_full, u + 1)
                bank = ps[:, u % PJ, :]
                two = bank.rearrange("p (a b) -> p a b", a=2)
                pair = slice(2 * n, 2 * n + 2)
                if name == "k":
                    ins = V_.tensor_copy(kT[:, pair, :], two)
                elif name == "ck":
                    ins = V_.tensor_copy(kxT[:, pair, :], two)
                elif name == "v":
                    ins = V_.tensor_copy(V[:, :, 256 * n:256 * (n + 1)], two)
                elif name == "cv":
                    ins = V_.tensor_copy(Vx[:, :, 256 * n:256 * (n + 1)], two)
                elif name == "ssd":
                    ins = V_.tensor_tensor(merged[:, pair, :], two, gate[:, pair, :], ALU.mult)
                elif name == "fox":
                    link(V_.tensor_tensor(mtmp[:, pair, :], two, gate[:, 8 + 2 * n:10 + 2 * n, :], ALU.mult))
                    ins = V_.tensor_tensor(merged[:, pair, :], merged[:, pair, :], mtmp[:, pair, :], ALU.add)
                else:
                    ins = V_.tensor_tensor(hT[:, pair, :], hT[:, pair, :], two, ALU.add)
                ins.then_inc(dve_drained, 1)

            dve.wait_ge(prm_psum, 1)
            V_.tensor_copy(prm[:, 0:136], ps[:, 3, 0:136]).then_inc(prm_ready, 1)
            dve.wait_ge(prm_ready, 1)
            copies(0, hT)
            dve.wait_ge(tr_copied, 4)
            apply_norm(0, hT, uT, G_MIX)
            copies(1, muT)
            for q in range(4):
                dve.wait_ge(act_drained, 2 * q + 2)
                for tap in range(4):
                    for c in range(4 * q, 4 * q + 4):
                        src = xb[:, c, 1 + tap:1 + tap + S]
                        w = prm[:, CW + 16 * tap + c:CW + 16 * tap + c + 1]
                        if tap == 0:
                            ins = V_.tensor_scalar(xc[:, c, :], src, w, None, ALU.mult)
                        else:
                            dve.wait_ge(dve_chain, done[0] - 3)
                            ins = V_.scalar_tensor_tensor(out=xc[:, c, :], in0=src, scalar=w, in1=xc[:, c, :],
                                                          op0=ALU.mult, op1=ALU.add)
                        if tap < 3:
                            ins.then_inc(dve_chain, 1)
                            done[0] += 1
                        else:
                            ins.then_inc(conved, 1)
                            if c < 4 * q + 3:
                                dve.wait_ge(dve_chain, done[0])
                if q == 1:
                    apply_norm(1, muT, muT, G_MEM)
            dve.wait_ge(df_psum, 1)
            for tb in range(TB):
                last = V_.tensor_tensor(raw[:, tb, :], ps[:, 3, 32 * tb:32 * tb + 24], bdf[:, :], ALU.add)
            last.then_inc(df_raw, 1)
            dve.wait_ge(df_raw, 1)
            dve.wait_ge(df_soft, 2)
            link(V_.scalar_tensor_tensor(out=dt[:, :, :], in0=raw[:, :, 0:16], scalar=0.0, in1=sp[:, :, 0:16],
                                         op0=ALU.max, op1=ALU.add))
            for tb in range(TB):
                V_.scalar_tensor_tensor(out=af[:, tb, 0:16], in0=dt[:, tb, :], scalar=-1.0, in1=alog[:, :],
                                        op0=ALU.mult, op1=ALU.mult)
            V_.scalar_tensor_tensor(out=af[:, :, 16:24], in0=raw[:, :, 16:24], scalar=0.0, in1=sp[:, :, 16:24],
                                    op0=ALU.min, op1=ALU.subtract).then_inc(df_ready, 1)
            dve.wait_ge(cum_psum, 1)
            V_.tensor_copy(actok[:, :, :], ps[:, 3, 64:128].rearrange("p (a b) -> p a b", a=2)[:, :, 0:24]).then_inc(cum_ready, 1)
            V_.tensor_copy(acT[:, :], ps[0:24, 3, 256:512]).then_inc(cum_ready, 1)
            for j in range(4):
                tb, half = j // 2, j % 2
                dve.wait_ge(xdt_psum, j + 1)
                V_.tensor_tensor(xdt[:, tb, 512 * half:512 * (half + 1)].rearrange("p (h e) -> p h e", e=64),
                                 ps[:, 4 + j, :].rearrange("p (h e) -> p h e", e=64),
                                 dt[:, tb, 8 * half:8 * half + 8].unsqueeze(2).to_broadcast([P, 8, 64]),
                                 ALU.mult).then_inc(xdt_ready, 1)
            for n in range(2):
                drain("k", n)
            for g in range(SSD_G):
                dve.wait_ge(cb_psum, g + 1)
                V_.tensor_tensor(cbm[:, g, :], ps[:, 4 + g, 0:384], tri[:, :], ALU.mult).then_inc(cb_ready, 1)
            for n in range(2, 4):
                drain("k", n)
            dve.wait_ge(cum_ready, 2)
            dve.wait_ge(dsk_ready, 2)
            fill = [("v", n) for n in range(4)] + [("gate", n) for n in range(8)]
            for h in range(SSD_H + 2):
                if h < SSD_H:
                    dve.wait_ge(sb_psum, h + 1)
                    if h >= 2:
                        dve.wait_ge(sy_psum, h - 1)
                    V_.tensor_scalar(dm[h % 2][:, 0:S], ps[:, 4 + h % 2, 0:S], actok[:, 0, h:h + 1], 0.0,
                                     ALU.subtract, ALU.min).then_inc(s_diff, 1)
                    V_.tensor_scalar(dm[h % 2][:, S:384], ps[:, 4 + h % 2, P:S], actok[:, 1, h:h + 1], 0.0,
                                     ALU.subtract, ALU.min).then_inc(s_diff, 1)
                if h < SSD_H and h % 4 != 0:
                    name, n = fill.pop(0)
                    if name not in ON_ACT:
                        drain(name, n)
                if h >= 2 and h % 2 == 0:
                    c = h // 2 - 1
                    dve.wait_ge(sy_psum, 2 * c + 2)
                    V_.scalar_tensor_tensor(out=ytmp[c % 2], in0=xc[:, c, :], scalar=dsk[:, c:c + 1],
                                            in1=ps[:, 6 + c % 2, 0:S], op0=ALU.mult, op1=ALU.add).then_inc(y_read, 1)
                    dve.wait_ge(y_read, c + 1)
                    V_.tensor_tensor(zs[:, c, :], ytmp[c % 2], zs[:, c, :], ALU.mult).then_inc(gated, 1)
            fill = [("ck", n) for n in range(4)] + [("cv", n) for n in range(4)]
            name, n = fill.pop(0)
            drain(name, n)
            dve.wait_ge(g_root, 1)
            link(V_.reciprocal(rsg, rsg))
            for c in range(KT):
                V_.scalar_tensor_tensor(out=yssd[:, c, :], in0=zs[:, c, :], scalar=prm[:, G_SSD + c:G_SSD + c + 1],
                                        in1=rsg[:, (c // 2) * S:(c // 2 + 1) * S], op0=ALU.mult, op1=ALU.mult).then_inc(yssd_ready, 1)
            for h in range(FOX_H + 1):
                if h < FOX_H:
                    cp, sc, t = ps[:, 4, :], ps[:, 6 + h % 2, :], ft[h % 2]
                    dve.wait_ge(f_psum, h + 1)
                    if h >= 2:
                        dve.wait_ge(pt_psum, h - 1)
                    V_.scalar_tensor_tensor(out=negc[:, 0:P], in0=cp[:, 0:P], scalar=-1.0, in1=fmask[:, 0:P],
                                            op0=ALU.mult, op1=ALU.add)
                    link(V_.scalar_tensor_tensor(out=negc[:, P:384], in0=cp[:, 0:S], scalar=-1.0, in1=fmask[:, P:384],
                                                 op0=ALU.mult, op1=ALU.add))
                    r = SSD_H + h
                    V_.scalar_tensor_tensor(out=t[:, 0:P], in0=sc[:, 0:P], scalar=actok[:, 0, r:r + 1], in1=negc[:, 0:P],
                                            op0=ALU.add, op1=ALU.add).then_inc(f_score, 1)
                    V_.scalar_tensor_tensor(out=t[:, P:384], in0=sc[:, P:384], scalar=actok[:, 1, r:r + 1],
                                            in1=negc[:, P:384], op0=ALU.add, op1=ALU.add).then_inc(f_score, 1)
                    dve.wait_ge(f_score, 4 * h + 2)
                    V_.reduce_max(mx[:, h % 2, 0:1], t[:, 0:P], AX.X, negate=True).then_inc(f_score, 1)
                    V_.reduce_max(mx[:, h % 2, 1:2], t[:, P:384], AX.X, negate=True).then_inc(f_score, 1)
                if h < FOX_H - 1:
                    name, n = fill.pop(0)
                    drain(name, n)
                if h < FOX_H:
                    dve.wait_ge(f_exp, 2 * h + 2)
                    V_.reciprocal(rinv[:, h % 2, :], rsum[:, h % 2, :]).then_inc(f_rinv, 1)
            dve.wait_ge(gate_sig, 1)
            for n in range(4):
                drain("ssd", n)
            for n in range(4):
                drain("fox", n)
            for n in range(4):
                drain("out", n)
            apply_norm(2, hT, uT, G_CROSS)
            for h in range(X_H):
                dve.wait_ge(x_psum, h + 1)
                V_.tensor_reduce(mx[:, h % 2, :], ps[:, 6 + h % 2, :].rearrange("p (a b) -> p a b", a=2), AX.X,
                                 ALU.max, negate=True).then_inc(x_max, 1)
                dve.wait_ge(x_exp, 2 * h + 2)
                V_.reciprocal(rinv[:, h % 2, :], rsum[:, h % 2, :]).then_inc(x_rinv, 1)
            for n in range(4):
                drain("co", n)
            apply_norm(3, hT, uT, G_FFN)
            dve.wait_ge(lg_psum, 1)
            for tb in range(TB):
                last = V_.tensor_tensor(lg[:, tb, :], ps[:, 3, 256 + NE * tb:256 + NE * (tb + 1)], brt[:, :], ALU.add)
            link(last)
            for tb in range(TB):
                link(V_.max(v8[:, tb, :], lg[:, tb, :]))
                link(V_.max_index(i8[:, tb, :], v8[:, tb, :], lg[:, tb, :]))
            V_.tensor_scalar(smal[:, :, 0], v8[:, :, 0], -1.0, None, ALU.mult).then_inc(top_ready, 1)
            link(V_.tensor_copy(i8f[:, :, :], i8[:, :, :]))
            for tb in range(TB):
                link(V_.tensor_scalar(msk[:, tb, :], iota[:, 0, 0:NE], i8f[:, tb, 0:1], None, ALU.is_equal))
                for k in range(1, TOPK):
                    ins = V_.scalar_tensor_tensor(out=msk[:, tb, :], in0=iota[:, 0, 0:NE], scalar=i8f[:, tb, k:k + 1],
                                                  in1=msk[:, tb, :], op0=ALU.is_equal, op1=ALU.add)
                    if k < TOPK - 1:
                        link(ins)
                ins.then_inc(msk_ready, 1)
            dve.wait_ge(msk_ready, 2)
            dve.wait_ge(ex_ready, 2)
            for tb in range(TB):
                link(V_.scalar_tensor_tensor(out=gt[:, tb, :], in0=em[:, tb, :], scalar=1.0, in1=msk[:, tb, :],
                                             op0=ALU.mult, op1=ALU.mult, accum_out=smal[:, tb, 1:2]))
            link(V_.reciprocal(smal[:, :, 1], smal[:, :, 1]))
            for tb in range(TB):
                V_.tensor_scalar(gt[:, tb, :], gt[:, tb, :], smal[:, tb, 1:2], None, ALU.mult)
            link(V_.tensor_scalar(posm[:, :, :], msk[:, :, :], -(NO_SLOT + 1.0), NO_SLOT, ALU.mult, ALU.add))
            dve.wait_ge(cnt_psum, 1)
            V_.tensor_tensor(posm[:, :, :], posm[:, :, :], ps[:, 0, 0:2 * NE].rearrange("p (a b) -> p a b", a=2),
                             ALU.add).then_inc(posm_ready, 1)
            link(V_.tensor_copy(ec[:, 0:1], ps[0:NE, 0, 64:65]))
            link(V_.tensor_scalar(ec[:, 1:2], ec[:, 0:1], float(SLOTS), None, ALU.is_gt))
            for b in range(2, MAX_EXTRA + 1):
                ins = V_.scalar_tensor_tensor(out=ec[:, 1:2], in0=ec[:, 0:1], scalar=float(SLOTS * b), in1=ec[:, 1:2],
                                              op0=ALU.is_gt, op1=ALU.add)
                if b < MAX_EXTRA:
                    link(ins)
            ins.then_inc(extra_ready, 1)
            dve.wait_ge(extra_ready, 1)
            dve.wait_ge(off_psum, 1)
            link(V_.tensor_scalar(ec[:, 3:4], ps[0:NE, 1, 0:1], float(NE), None, ALU.add))
            link(V_.tensor_tensor(ec[:, 2:3], ec[:, 3:4], ec[:, 1:2], ALU.subtract))
            link(V_.tensor_scalar(ec[:, 4:5], ec[:, 2:3], -1.0, None, ALU.add))
            link(V_.tensor_scalar(pe2[:, :], iota[0:NE, 0, :], ec[:, 3:4], None, ALU.is_lt))
            link(V_.scalar_tensor_tensor(out=pe2[:, :], in0=iota[0:NE, 0, :], scalar=ec[:, 2:3], in1=pe2[:, :],
                                         op0=ALU.is_ge, op1=ALU.mult))
            V_.scalar_tensor_tensor(out=pb2[:, :], in0=iota[0:NE, 0, :], scalar=ec[:, 4:5], in1=pe2[:, :],
                                    op0=ALU.subtract, op1=ALU.mult)
            V_.tensor_scalar(meta[0:1, NI:NI + 1], ps[0:1, 1, 1:2], float(NE), None, ALU.add)
            V_.tensor_tensor(pe1[:, :], pe2[:, :], ident[0:NE, 0:NI], ALU.add).then_inc(table_ready, 1)
            dve.wait_ge(item_psum, 1)
            V_.tensor_copy(ipos[:, :, :], ps[:, 0, 128:256].rearrange("p (a b) -> p a b", a=2)).then_inc(item_ready, 1)
            V_.tensor_copy(igate[:, :, :], ps[:, 0, 256:384].rearrange("p (a b) -> p a b", a=2)).then_inc(item_ready, 1)
            V_.tensor_copy(meta[0:1, 0:NI], ps[0:1, 0, 384:384 + NI]).then_inc(meta_ready, 1)
            dve.wait_ge(meta_ready, 1)
            dve.wait_ge(unit_full, 2 * NG)
            dve.wait_ge(table_ready, 1)

            def selection(i, i1):
                for tb in range(TB):
                    V_.tensor_scalar(sel[:, 64 * tb:64 * (tb + 1)], iota[:, 0, :], ipos[:, tb, bass.ds(i, 1)], None,
                                     ALU.is_equal).then_inc(sel_ready, 1)

            def bias_row(i):
                V_.tensor_copy(selb[0:NE, :], pe1[:, bass.ds(i, 1)].to_broadcast([NE, SLOTS])).then_inc(selb_ready, 1)

            def gathered_columns(i1):
                dve.wait_ge(xgt_psum, i1)
                V_.tensor_copy(xgT, ps[:, 2, :]).then_inc(xgt_ready, 1)

            selection(0, 1)
            bias_row(0)
            V_.memset(ys, 0.0).then_inc(y_ready, 1)
            V_.memset(sgT, 0.0).then_inc(sgt_ready, 1)
            gathered_columns(1)
            n_items = dve.value_load(meta[0:1, NI:NI + 1], min_val=NE, max_val=MAX_ITEMS)
            with dve.Fori(0, n_items) as i:
                dve.wait_ge(xg_psum, i + 1)
                selection(i + 1, i + 2)
                for tb in range(TB):
                    V_.tensor_scalar(sg[:, P * tb:P * (tb + 1)], iota[:, :, :].rearrange("p a b -> p (a b)"),
                                     ipos[:, tb, bass.ds(i, 1)], igate[:, tb, bass.ds(i, 1)],
                                     ALU.is_equal, ALU.mult).then_inc(sg_ready, 1)
                dve.wait_ge(h_psum, i + 1)
                V_.tensor_scalar(glu, ps[:, 0, :], LIMIT, None, ALU.min).then_inc(glu_ready, 1)
                V_.tensor_scalar(lin, ps[:, 1, :], LIMIT, -LIMIT, ALU.min, ALU.max).then_inc(dve_chain, 1)
                dve.wait_ge(dve_chain, 2 * i + (done[0] + 1))
                V_.scalar_tensor_tensor(out=lin, in0=lin, scalar=1.0, in1=glu, op0=ALU.add, op1=ALU.mult).then_inc(dve_chain, 1)
                dve.wait_ge(dve_chain, 2 * i + (done[0] + 2))
                dve.wait_ge(sig_ready, i + 1)
                V_.tensor_tensor(lin, lin, sig, ALU.mult).then_inc(act_ready, 1)
                bias_row(i + 1)
                gathered_columns(i + 2)
            dve.wait_ge(ld_g, 16)
            dve.wait_ge(f_root, 1)
            V_.reciprocal(smal[:, :, 1], smal[:, :, 3]).then_inc(f_root, 1)
            dve.wait_ge(f_root, 2)
            for tb in range(TB):
                V_.scalar_tensor_tensor(out=outsb[:, tb, :], in0=ps[:, 4 + 2 * tb:6 + 2 * tb, :].rearrange("p a b -> p (a b)"),
                                        scalar=smal[:, tb, 1:2], in1=gfin, op0=ALU.mult, op1=ALU.mult).then_inc(out_ready, 1)


INPUTS = ["x", "mem", "norm_mix_g", "w_in", "conv_w", "conv_b", "dt_bias", "a_log", "d_skip", "ssd_norm_g",
          "w_ssd_branch", "b_forget", "w_fox_branch", "b_gates", "w_out", "norm_cross_g", "norm_mem_g",
          "w_cross_q", "w_cross_kv", "w_cross_o", "norm_ffn_g", "w_router", "b_router", "w_expert_in",
          "b_expert_in", "w_expert_out", "b_expert_out", "norm_final_g"]


def kernel(**inputs):
    import concourse.bacc as bacc
    from concourse.bass_utils import run_bass_kernel_spmd

    nc = bacc.Bacc("TRN2", target_bir_lowering=False, num_devices=1)
    arrays, args = {}, []
    for name in INPUTS:
        a = np.ascontiguousarray(inputs[name])
        arrays[f"in_{name}"] = a
        args.append(nc.dram_tensor(f"in_{name}", a.shape, mybir.dt.from_np(a.dtype), kind="ExternalInput").ap())
    args.append(nc.dram_tensor("out_h", (1, S, D), mybir.dt.float32, kind="ExternalOutput").ap())
    layer_program(nc, *args)
    result = run_bass_kernel_spmd(nc, [arrays], core_ids=[0])
    return result.results[0]["out_h"]
```

```python
from contextlib import ExitStack

import numpy as np

import concourse.bass as bass
from concourse import mybir

D = 1024
S = 256
P = 128
KT = D // P
TB = S // P
SSD_H, SSD_P = 16, 64
SSD_G = 4
FOX_H = 8
X_H, X_D = 4, 256
NE, TOPK = 32, 4
DE = 1024
SLOTS = 64
MAX_EXTRA = S // SLOTS - 1
MAX_ITEMS = NE + TOPK * S // SLOTS
NI = 64
EPS = 1e-6
LIMIT, ALPHA = 7.0, 1.702
NO_SLOT = 4096.0
MASKED = -1e30
FOX_SCALE = 128 ** -0.5
X_SCALE = X_D ** -0.5

C_Z, C_XBC, C_DT, C_Q, C_K, C_V, C_F, C_G = 0, 1024, 3072, 3088, 4112, 5136, 6160, 6168


def layer_program(nc, x, mem, norm_mix_g, w_in, conv_w, conv_b, dt_bias, a_log, d_skip, ssd_norm_g,
                  w_ssd, b_forget, w_fox, b_gates, w_out, norm_cross_g, norm_mem_g, w_cq, w_ckv, w_co,
                  norm_ffn_g, w_router, b_router, w_ein, b_ein, w_eout, b_eout, norm_final_g, out):
    f32, f32r, i32, u32 = mybir.dt.float32, mybir.dt.float32r, mybir.dt.int32, mybir.dt.uint32
    ALU = mybir.AluOpType
    ACT = mybir.ActivationFunctionType
    AX = mybir.AxisListType

    units = []

    def add(name, w, col0, *numbers):
        for n in numbers:
            units.append((name, n, w[:, col0 + 256 * n:col0 + 256 * (n + 1)]))

    win = w_in[0]
    add("xbc", win, C_XBC, *range(8))
    add("z", win, C_Z, *range(4))
    add("q", win, C_Q, *range(4))
    add("k", win, C_K, *range(4))
    add("v", win, C_V, *range(4))
    add("gate", win, C_G, *range(8))
    add("ssd", w_ssd[0], 0, *range(4))
    add("fox", w_fox[0], 0, *range(4))
    add("ck", w_ckv[0], 0, 0)
    add("out", w_out[0], 0, *range(4))
    add("ck", w_ckv[0], 0, 1, 2, 3)
    add("cq", w_cq[0], 0, *range(4))
    add("cv", w_ckv[0], D, *range(4))
    add("co", w_co[0], 0, *range(4))
    NU = len(units)
    ON_ACT = {"xbc", "z", "q", "gate", "cq"}
    BY_TOKEN = {"v", "cv"}

    def unit(name, n):
        return next(u for u, (a, b, _) in enumerate(units) if (a, b) == (name, n))

    def drained(u):
        act = units[u][0] in ON_ACT
        return act, sum((units[v][0] in ON_ACT) == act for v in range(u + 1))

    SPLIT = {"u": 0, "yssd": 4, "merged": 8, "mu": 12, "u2": 16}
    SSD_FILL = {}
    for h_, n_ in zip((0, 1, 3, 4, 5, 7, 8, 9, 11, 12, 13, 15), range(12)):
        SSD_FILL[h_] = (("q", "k", "v")[n_ // 4], n_ % 4)

    PJ = 3

    with ExitStack() as ctx:
        def sb(name, shape, dt=f32):
            return ctx.enter_context(nc.sbuf_tensor(name, shape, dt))

        def sem(name):
            return ctx.enter_context(nc.semaphore(name))

        PAGE = 2048
        arena = sb("arena", [P, 24 * PAGE])
        arena_at = nc.sbuf_base - 4 * 24 * PAGE

        def page(n, count=PAGE, at=0):
            return arena[:, n * PAGE + at:n * PAGE + at + count]

        def tiles(ap, n):
            return ap.rearrange("p (c t) -> p c t", c=n)

        def rounded(name, first, shape):
            return nc.alloc_sbuf_tensor_at(name, shape, f32r, offset=arena_at + 4 * PAGE * first)

        xin = tiles(page(0), TB)
        memin = tiles(page(1), TB)
        xb = tiles(page(2, 16 * 260), 16)
        cbm = tiles(page(4, 1536, 64), SSD_G)
        PT = page(4, 384, 64)
        xc = tiles(page(5, 2 * PAGE), 16)
        zs = tiles(page(8), KT)
        xdt = tiles(page(9), TB)
        qT, kT, V = tiles(page(0), KT), tiles(page(1), KT), tiles(page(7), TB)
        dm = [page(2, 384, 384 * j) for j in range(3)]
        ytmp = [page(3, 256, 256 * j) for j in range(2)]
        gate = tiles(page(2, 2 * PAGE), 16)
        merged = tiles(page(5), KT)
        mtmp = tiles(page(0), KT)
        negc = page(21, 384, 1600)
        ft = [page(21, 384, 384 * j) for j in range(2)]
        kxT, Vx, qx = tiles(page(6), KT), tiles(page(7), TB), tiles(page(20), KT)
        xp = [page(21, 512, 512 * j) for j in range(2)]
        xPT = page(21, 512, 1024)
        w_raw = nc.alloc_sbuf_tensor_at("w_raw", [P, 2, KT, 256], f32, offset=arena_at + 4 * PAGE * 14)
        raw_w = [w_raw[:, j, :, :] for j in range(2)]
        w_hi = rounded("w_hi", 12, [P, 4, KT, P])
        w_lo = rounded("w_lo", 10, [P, 4, KT, P])
        splits = {}
        for name, first in (("A", 16), ("B", 18), ("C", 8)):
            splits[name] = [rounded(f"{name}_{part}", first + j, [P, KT, S]) for j, part in enumerate(("hi", "lo"))]
        A_, B_, C_ = splits["A"], splits["B"], splits["C"]
        muT = tiles(page(20), KT)
        sq = tiles(page(21), KT)
        xtok = tiles(page(21), TB)
        uT = tiles(page(22), KT)
        outsb = tiles(page(22), TB)
        hT = tiles(page(23), KT)
        def w_at(at, n):
            return page(12, n, at)

        b1 = w_at(0, 2048)
        b2 = w_at(2048, 1024)
        xgs = w_at(3072, 512)
        xgT = w_at(3584, 512)
        glu = w_at(4096, 512)
        sig = w_at(4608, 512)
        lin = w_at(5120, 512)
        actT = w_at(5632, 512)
        ys = w_at(6144, 512)
        sgT = w_at(6656, 256)
        sg = w_at(6912, 256)
        sel = w_at(7168, 128)
        selb = w_at(7296, 64)
        gfin = page(0, D)

        ident = sb("ident", [P, P])
        tri = sb("tri", [P, 384])
        fmask = sb("fmask", [P, 384])
        c_d = sb("c_d", [P, P])
        c_g = sb("c_g", [P, P])
        c_s = sb("c_s", [P, P])
        eps = sb("eps", [P, 1])
        prow = sb("prow", [P, P])
        prow2 = sb("prow2", [16, P])
        prm = sb("prm", [P, 144])
        bdf = sb("bdf", [P, 24])
        alog = sb("alog", [P, SSD_H])
        brt = sb("brt", [P, NE])
        dall = sb("dall", [P, SSD_H])
        dsk = sb("dsk", [P, KT])
        wdf = sb("wdf", [P, KT, 24])
        wrt = sb("wrt", [P, KT, NE])
        raw = sb("raw", [P, TB, 24])
        sp = sb("sp", [P, TB, 24])
        dt = sb("dt", [P, TB, SSD_H])
        af = sb("af", [P, TB, 24])
        actok = sb("actok", [P, TB, 24])
        acT = sb("acT", [24, S])
        st = sb("st", [P, TB])
        gst = sb("gst", [P, TB, SSD_G])
        mx = sb("mx", [P, 2, 2])
        rsum = sb("rsum", [P, 2, 2])
        rinv = sb("rinv", [P, 2, 2])
        iota = sb("iota", [P, 2, NI])
        iotai = sb("iotai", [P, 2, NI], i32)
        rowi = sb("rowi", [P, 1], i32)
        rowf = sb("rowf", [P, 1])
        table_at = iter(range(0, PAGE, 64))

        def table(n, rows=P):
            at = [next(table_at) for _ in range(n)][0]
            return page(20, 64 * n, at)[0:rows, :]

        def by_block(ap):
            return ap.rearrange("p (b n) -> p b n", b=TB)

        lg, em, msk, gt, posm = (by_block(table(1)) for _ in range(5))
        v8 = sb("v8", [P, TB, 8])
        i8 = sb("i8", [P, TB, 8], u32)
        i8f = sb("i8f", [P, TB, 8])
        smal = sb("smal", [P, TB, 4])
        posT, gtT = table(4, NE), table(4, NE)
        ec = sb("ec", [NE, 8])
        pe1, pe2, pb2 = table(1, NE), table(1, NE), table(1, NE)
        ipos = by_block(table(2))
        igate = by_block(table(2))
        meta = sb("meta", [1, NI + 1], i32)

        ps = ctx.enter_context(nc.psum_tensor("ps", [P, 8, 512], f32))

        CW, CB, G_MIX, G_CROSS, G_MEM, G_FFN, G_SSD, B_GATE = 0, 64, 80, 88, 96, 104, 112, 120

        ld_x, ld_mem, ld_prm, ld_small = sem("ld_x"), sem("ld_mem"), sem("ld_prm"), sem("ld_small")
        w_loaded = [sem("w_loaded0"), sem("w_loaded1")]
        w_hi_ready, w_lo_ready = sem("w_hi_ready"), sem("w_lo_ready")
        w_done = sem("w_done")
        a_hi_ready, a_lo_ready = sem("a_hi_ready"), sem("a_lo_ready")
        act_drained, dve_drained = sem("act_drained"), sem("dve_drained")
        consts, ld_skip, dsk_ready = sem("consts"), sem("ld_skip"), sem("dsk_ready")
        pool_chain, dve_chain, act_chain = sem("pool_chain"), sem("dve_chain"), sem("act_chain")
        prm_psum, prm_ready = sem("prm_psum"), sem("prm_ready")
        tr_psum, tr_copied, tr_squared = sem("tr_psum"), sem("tr_copied"), sem("tr_squared")
        squared = sem("squared")
        ms_psum, ms_root, st_ready, ms_rows, normed, normed_tiles = (sem("ms_psum"), sem("ms_root"), sem("st_ready"),
                                                       sem("ms_rows"), sem("normed"), sem("normed_tiles"))
        df_psum, df_raw, df_soft, df_ready = sem("df_psum"), sem("df_raw"), sem("df_soft"), sem("df_ready")
        cum_psum, cum_ready = sem("cum_psum"), sem("cum_ready")
        conved, xc_ready = sem("conved"), sem("xc_ready")
        xdt_psum, xdt_ready = sem("xdt_psum"), sem("xdt_ready")
        cb_psum, cb_ready = sem("cb_psum"), sem("cb_ready")
        sb_psum, s_diff, s_exp, s_mt, sy_psum = (sem("sb_psum"), sem("s_diff"), sem("s_exp"),
                                                 sem("s_mt"), sem("sy_psum"))
        y_read, gated, gsq = sem("y_read"), sem("gated"), sem("gsq")
        gms_psum, g_root, gst_ready, g_rows, y_normed = (sem("gms_psum"), sem("g_root"), sem("gst_ready"),
                                                         sem("g_rows"), sem("y_normed"))
        merge_made = sem("merge_made")
        f_psum, f_score, f_exp, f_rinv, f_norm = (sem("f_psum"), sem("f_score"), sem("f_exp"),
                                                  sem("f_rinv"), sem("f_norm"))
        pt_psum, pt_copied, fo_psum, yf_hi, yf_lo = (sem("pt_psum"), sem("pt_copied"), sem("fo_psum"),
                                                     sem("yf_hi"), sem("yf_lo"))
        gate_sig = sem("gate_sig")
        x_psum, x_max, x_exp, x_rinv, x_norm = (sem("x_psum"), sem("x_max"), sem("x_exp"),
                                                sem("x_rinv"), sem("x_norm"))
        xpt_psum, xpt_copied, xo_psum, ox_hi, ox_lo = (sem("xpt_psum"), sem("xpt_copied"),
                                                       sem("xo_psum"), sem("ox_hi"), sem("ox_lo"))
        tok_psum, tok_ready = sem("tok_psum"), sem("tok_ready")
        lg_psum, lg_ready, top_ready, ex_ready, msk_ready = (
            sem("lg_psum"), sem("lg_ready"), sem("top_ready"), sem("ex_ready"), sem("msk_ready"))
        cnt_psum, extra_ready, off_psum, posm_ready, ptr_psum, ptr_ready = (
            sem("cnt_psum"), sem("extra_ready"), sem("off_psum"), sem("posm_ready"),
            sem("ptr_psum"), sem("ptr_ready"))
        table_ready, item_psum, item_ready, meta_ready = (
            sem("table_ready"), sem("item_psum"), sem("item_ready"), sem("meta_ready"))
        ld_b = sem("ld_b")
        ld_g = sem("ld_g")
        e_loaded = [sem(f"e_loaded{s}") for s in range(12)]
        x_loaded = [sem(f"x_loaded{s}") for s in range(4)]
        e_used = sem("e_used")
        sel_ready, sg_ready, selb_ready = sem("sel_ready"), sem("sg_ready"), sem("selb_ready")
        h_psum, glu_ready, sig_ready, act_ready = (sem("h_psum"), sem("glu_ready"),
                                                   sem("sig_ready"), sem("act_ready"))
        xg_psum, xg_copied, xgt_psum, xgt_ready = (sem("xg_psum"), sem("xg_copied"),
                                                   sem("xgt_psum"), sem("xgt_ready"))
        sgt_psum, sgt_ready, at_psum, at_ready = (sem("sgt_psum"), sem("sgt_ready"),
                                                  sem("at_psum"), sem("at_ready"))
        y_psum, y_ready = sem("y_psum"), sem("y_ready")
        acc_done, f_sq, f_root, out_ready, stored = (sem("acc_done"), sem("f_sq"), sem("f_root"),
                                                     sem("out_ready"), sem("stored"))

        def e_chunk(expert, s):
            if s < 8:
                return w_ein[0, expert, s * P:(s + 1) * P, :]
            t = s - 8
            return w_eout[0, expert, 2 * t * P:2 * (t + 1) * P, :].rearrange("(c p) n -> p c n", p=P)

        def e_slot(s, first=False):
            ap = page(16 + s) if first and s < 4 else page(s)
            return ap if s < 8 else ap.rearrange("p (c n) -> p c n", c=2)

        block = ctx.enter_context(nc.Block())

        @block.sync
        def _(sp_):
            sp_.dma_start(xin, x[0].rearrange("(b p) d -> p b d", p=P)).then_inc(ld_x, 16)
            for at, src in ((CW, conv_w[0].rearrange("k (c p) -> (k c) p", p=P)),
                            (CB, conv_b[0].rearrange("(c p) -> c p", p=P)),
                            (G_MIX, norm_mix_g[0].rearrange("(c p) -> c p", p=P)),
                            (G_CROSS, norm_cross_g[0].rearrange("(c p) -> c p", p=P)),
                            (G_MEM, norm_mem_g[0].rearrange("(c p) -> c p", p=P)),
                            (G_FFN, norm_ffn_g[0].rearrange("(c p) -> c p", p=P)),
                            (G_SSD, ssd_norm_g[0].rearrange("(c p) -> c p", p=P))):
                sp_.dma_start(prow[at:at + src.shape[0], :], src).then_inc(ld_prm, 16)
            sp_.dma_start(prow2[:, :], b_gates[0].rearrange("b (c p) -> (b c) p", p=P)).then_inc(ld_prm, 16)

            def load(u):
                if u >= 2:
                    sp_.wait_ge(w_lo_ready, 2 * (u - 1))
                sp_.dma_start(raw_w[u % 2], units[u][2].rearrange("(k p) n -> p k n", p=P)).then_inc(w_loaded[u % 2], 16)

            def chunk(item, s):
                if item == 0 and s < 4:
                    sp_.dma_start(e_slot(s, True), e_chunk(0, s)).then_inc(x_loaded[s], 16)
                else:
                    sp_.dma_start(e_slot(s), e_chunk(item, s)).then_inc(e_loaded[s], 16)

            load(0)
            load(1)
            sp_.dma_start(memin, mem[0].rearrange("(b p) d -> p b d", p=P)).then_inc(ld_mem, 16)
            for u in range(2, unit("out", 3)):
                load(u)
            sp_.wait_ge(a_lo_ready, SPLIT["merged"] + 4)
            ahead = [(0, 4), (0, 5), (1, 0), (1, 1), (1, 2), (1, 3)]
            for u in range(unit("out", 3), unit("cv", 1)):
                load(u)
                if ahead:
                    chunk(*ahead.pop(0))
            load(unit("cv", 1))
            sp_.wait_ge(w_done, 2 * unit("cq", 3) + 2)
            chunk(0, 8)
            load(unit("cv", 2))
            chunk(0, 9)
            for u in range(unit("cv", 3), unit("co", 2)):
                load(u)
            sp_.wait_ge(xo_psum, X_H)
            load(unit("co", 2))
            chunk(0, 6)
            load(unit("co", 3))
            for item, s in ((0, 7), (0, 2), (0, 3)):
                chunk(item, s)
            sp_.wait_ge(w_done, 2 * NU)
            sp_.dma_start(b1[0:NE, :], b_ein[0]).then_inc(ld_b, 16)
            sp_.dma_start(b2[0:NE, :], b_eout[0]).then_inc(ld_b, 16)
            for item, s in ((0, 0), (0, 1), (0, 10), (0, 11)):
                chunk(item, s)
            for s in range(4, 12):
                sp_.wait_ge(e_used, s + 2)
                chunk(1, s)
            with sp_.Fori(2, NE) as i:
                for s in range(12):
                    sp_.wait_ge(e_used, 12 * i + (s - 10))
                    sp_.dma_start(e_slot(s), e_chunk(i, s)).then_inc(e_loaded[s], 16)
            sp_.wait_ge(meta_ready, 1)
            n_items = sp_.value_load(meta[0:1, NI:NI + 1], min_val=NE, max_val=MAX_ITEMS)
            with sp_.If(n_items > NE):
                with sp_.Fori(NE, n_items) as i:
                    e = sp_.value_load(meta[0:1, bass.ds(i, 1)], min_val=0, max_val=NE - 1)
                    for s in range(12):
                        sp_.wait_ge(e_used, 12 * i + (s - 10))
                        sp_.dma_start(e_slot(s), e_chunk(e, s)).then_inc(e_loaded[s], 16)
            sp_.wait_ge(e_used, 12 * n_items)
            sp_.dma_start(gfin, norm_final_g.partition_broadcast(P)).then_inc(ld_g, 16)
            for tb in range(TB):
                sp_.wait_ge(out_ready, tb + 1)
                sp_.dma_start(out[0, tb * P:(tb + 1) * P, :], outsb[:, tb, :]).then_inc(stored, 16)
            sp_.wait_ge(stored, 16 * TB)

        @block.gpsimd
        def _(pool):
            done = [0]

            def link(ins):
                done[0] += 1
                ins.then_inc(pool_chain, 1)
                pool.wait_ge(pool_chain, done[0])

            nc.gpsimd.memset(ident[:, :], 0.0).then_inc(pool_chain, 1)
            nc.gpsimd.memset(tri[:, :], 1.0).then_inc(pool_chain, 1)
            nc.gpsimd.memset(fmask[:, :], 0.0).then_inc(pool_chain, 1)
            done[0] = 3
            pool.wait_ge(pool_chain, 3)
            nc.gpsimd.affine_select(out=ident[:, :], in_=ident[:, :], compare_op=ALU.not_equal, fill=1.0,
                                    base=0, pattern=[[-1, P]], channel_multiplier=1).then_inc(consts, 1)
            nc.gpsimd.memset(c_d[:, :], 1.0 / D).then_inc(consts, 1)
            nc.gpsimd.memset(eps[:, :], EPS).then_inc(consts, 1)
            for at in (0, 256):
                nc.gpsimd.affine_select(out=tri[:, at:at + P], in_=tri[:, at:at + P], compare_op=ALU.is_ge,
                                        fill=0.0, base=0, pattern=[[1, P]], channel_multiplier=-1).then_inc(consts, 1)
                nc.gpsimd.affine_select(out=fmask[:, at:at + P], in_=fmask[:, at:at + P], compare_op=ALU.is_ge,
                                        fill=MASKED, base=0, pattern=[[-1, P]], channel_multiplier=1).then_inc(consts, 1)
            nc.gpsimd.memset(c_g[:, :], 1.0 / 256).then_inc(consts, 1)
            nc.gpsimd.memset(c_s[:, :], -float(SLOTS)).then_inc(consts, 1)
            link(nc.gpsimd.iota(iotai[:, :, :], pattern=[[0, 2], [1, NI]], base=0, channel_multiplier=0))
            nc.gpsimd.tensor_copy(iota[:, :, :], iotai[:, :, :]).then_inc(consts, 1)
            link(nc.gpsimd.iota(rowi[:, :], pattern=[[0, 1]], base=0, channel_multiplier=1))
            nc.gpsimd.tensor_copy(rowf[:, :], rowi[:, :]).then_inc(consts, 1)
            nc.gpsimd.memset(xb[:, :, 0:4], 0.0).then_inc(consts, 1)
            pool.dma_start(wdf[:, :, 0:16], win[:, C_DT:C_DT + 16].rearrange("(k p) n -> p k n", p=P)).then_inc(ld_small, 16)
            pool.dma_start(wdf[:, :, 16:24], win[:, C_F:C_F + 8].rearrange("(k p) n -> p k n", p=P)).then_inc(ld_small, 16)
            pool.dma_start(bdf[:, 0:16], dt_bias[0].partition_broadcast(P)).then_inc(ld_small, 16)
            pool.dma_start(bdf[:, 16:24], b_forget[0].partition_broadcast(P)).then_inc(ld_small, 16)
            pool.dma_start(alog[:, :], a_log[0].partition_broadcast(P)).then_inc(ld_small, 16)
            pool.dma_start(brt[:, :], b_router[0].partition_broadcast(P)).then_inc(ld_small, 16)
            pool.dma_start(dall[:, :], d_skip[0].partition_broadcast(P)).then_inc(ld_skip, 16)
            pool.dma_start(wrt[:, :, :], w_router[0].rearrange("(k p) n -> p k n", p=P)).then_inc(ld_small, 16)
            pool.wait_ge(ld_skip, 16)
            pool.wait_ge(consts, 12)
            for j in range(2):
                rows = slice(64 * j, 64 * (j + 1))
                nc.gpsimd.tensor_copy(dsk[rows, :], dall[rows, j:SSD_H:2]).then_inc(dsk_ready, 1)
                pool.wait_ge(dsk_ready, j + 1)
            pool.wait_ge(cb_ready, SSD_G)
            for h in range(SSD_H):
                pool.wait_ge(s_exp, h + 1)
                nc.gpsimd.tensor_tensor(dm[h % 3], dm[h % 3], cbm[:, h // 4, :], ALU.mult).then_inc(s_mt, 1)
            for h in range(FOX_H):
                pool.wait_ge(f_rinv, h + 1)
                nc.gpsimd.tensor_scalar(ft[h % 2][:, 0:P], ft[h % 2][:, 0:P], rinv[:, h % 2, 0:1], None, ALU.mult).then_inc(f_norm, 1)
                nc.gpsimd.tensor_scalar(ft[h % 2][:, P:384], ft[h % 2][:, P:384], rinv[:, h % 2, 1:2], None, ALU.mult).then_inc(f_norm, 1)
            for h in range(X_H):
                pool.wait_ge(x_rinv, h + 1)
                for b in range(TB):
                    t = xp[h % 2][:, S * b:S * (b + 1)]
                    nc.gpsimd.tensor_scalar(t, t, rinv[:, h % 2, b:b + 1], None, ALU.mult).then_inc(x_norm, 1)

        @block.tensor
        def _(pe):
            mm = nc.tensor.matmul
            idn = ident[:, :]

            def transposes(src, n):
                for j in range(4):
                    if n:
                        pe.wait_ge(tr_copied, 4 * (n - 1) + j + 1)
                    for c in (2 * j, 2 * j + 1):
                        for tb in range(TB):
                            at = (c % 2) * S + tb * P
                            last = nc.tensor.transpose(ps[:, 4 + j, at:at + P], src[:, tb, c * P:(c + 1) * P], idn)
                    last.then_inc(tr_psum, 1)

            def mean_squares(squares, count):
                for tb in range(TB):
                    for c in range(KT):
                        if tb == 0 and c % 2 == 0:
                            pe.wait_ge(squares, count + c // 2 + 1)
                        last = mm(ps[:, 3, 508 + tb:509 + tb], sq[:, c, tb * P:(tb + 1) * P], c_d[:, 0:1],
                                  start=(c == 0), stop=(c == KT - 1))
                last.then_inc(ms_psum, 1)

            def inverse_rows(n):
                pe.wait_ge(st_ready, n + 1)
                for tb in range(TB):
                    last = mm(ps[:, 3, tb * P:(tb + 1) * P], st[:, tb:tb + 1].to_broadcast([P, P]), idn,
                              start=True, stop=True)
                last.then_inc(ms_rows, 1)

            def project(name, n, act, ready=None):
                u = unit(name, n)
                a_hi, a_lo = act
                if u >= PJ:
                    on_act, count = drained(u - PJ)
                    pe.wait_ge(act_drained if on_act else dve_drained, count)

                def tile_ready(k):
                    if ready and k % ready[2] == 0:
                        pe.wait_ge(ready[0], ready[1] + k // ready[2] + 1)

                for j in range(2):
                    o = ps[:, u % PJ, j * 256:(j + 1) * 256]
                    if name in BY_TOKEN:
                        pe.wait_ge(w_lo_ready, 2 * u + 2)
                        slots, rows = slice(2 * (u % 2), 2 * (u % 2) + 2), slice(j * P, (j + 1) * P)
                        for k in range(KT):
                            wh, wl = w_hi[:, slots, k, :], w_lo[:, slots, k, :]
                            mm(o, a_hi[:, k, rows], wh, start=(k == 0), stop=False)
                            mm(o, a_hi[:, k, rows], wl, start=False, stop=False)
                            last = mm(o, a_lo[:, k, rows], wh, start=False, stop=(k == KT - 1))
                    else:
                        pe.wait_ge(w_lo_ready, 2 * u + j + 1)
                        s = (2 * u + j) % 4
                        for k in range(KT):
                            if j == 0:
                                tile_ready(k)
                            mm(o, w_hi[:, s, k, :], a_hi[:, k, :], start=(k == 0), stop=False)
                            mm(o, w_hi[:, s, k, :], a_lo[:, k, :], start=False, stop=False)
                            last = mm(o, w_lo[:, s, k, :], a_hi[:, k, :], start=False, stop=(k == KT - 1))
                        if j == 0:
                            last.then_inc(w_done, 1)
                last.then_inc(w_done, 2 if name in BY_TOKEN else 1)

            pe.wait_ge(consts, 2)
            pe.wait_ge(ld_prm, 16 * 8)
            nc.tensor.transpose(ps[:, 3, 0:120], prow[0:120, :], ident[0:120, 0:120])
            nc.tensor.transpose(ps[:, 3, 120:136], prow2[:, :], ident[0:16, 0:16]).then_inc(prm_psum, 1)
            pe.wait_ge(ld_x, 16)
            transposes(xin, 0)
            pe.wait_ge(prm_ready, 1)
            mean_squares(tr_squared, 0)
            pe.wait_ge(ld_mem, 16)
            transposes(memin, 1)
            inverse_rows(0)
            project("xbc", 0, A_, (a_lo_ready, SPLIT["u"], 2))
            for n in range(1, 4):
                project("xbc", n, A_)
            pe.wait_ge(normed, 1)
            mean_squares(tr_squared, 4)
            project("xbc", 4, A_)
            inverse_rows(1)
            for n in range(5, 8):
                project("xbc", n, A_)
            pe.wait_ge(ld_small, 16 * 7)
            pe.wait_ge(normed, 2)
            for tb in range(TB):
                for k in range(KT):
                    last = mm(ps[:, 3, 32 * tb:32 * tb + 24], uT[:, k, tb * P:(tb + 1) * P], wdf[:, k, :],
                              start=(k == 0), stop=(k == KT - 1))
            last.then_inc(df_psum, 1)
            for n in range(4):
                project("z", n, A_)
            pe.wait_ge(consts, 11)
            pe.wait_ge(df_ready, 1)
            mm(ps[:, 3, 64:88], tri[:, 0:P], af[:, 0, :], start=True, stop=True)
            mm(ps[:, 3, 96:120], tri[:, P:2 * P], af[:, 0, :], start=True, stop=False)
            mm(ps[:, 3, 96:120], tri[:, 0:P], af[:, 1, :], start=False, stop=True)
            mm(ps[0:24, 3, 256:512], af[:, 0, :], tri[:, 0:S], start=True, stop=False)
            mm(ps[0:24, 3, 256 + P:512], af[:, 1, :], tri[:, 0:P], start=False, stop=True).then_inc(cum_psum, 1)
            pe.wait_ge(tr_copied, 8)
            for j in range(4):
                tb, half = j // 2, j % 2
                pe.wait_ge(xc_ready, 4 * (half + 1))
                for c in range(4):
                    last = nc.tensor.transpose(ps[:, 4 + j, c * P:(c + 1) * P],
                                               xc[:, 4 * half + c, tb * P:(tb + 1) * P], idn)
                last.then_inc(xdt_psum, 1)
            pe.wait_ge(xc_ready, 16)
            for g in range(SSD_G):
                pe.wait_ge(xdt_ready, g + 1)
                mm(ps[:, 4 + g, 0:S], xc[:, 8 + g, 0:P], xc[:, 12 + g, :], start=True, stop=True)
                mm(ps[:, 4 + g, S:384], xc[:, 8 + g, P:S], xc[:, 12 + g, P:S], start=True, stop=True).then_inc(cb_psum, 1)
            pe.wait_ge(cum_ready, 2)

            def running_sum(bank, r):
                return mm(ps[:, bank, 0:S], ident[0:24, r:r + 1].to_broadcast([24, P]), acT[0:24, :],
                          start=True, stop=True)

            for h in range(SSD_H + 2):
                if h < SSD_H:
                    if h < 2:
                        pe.wait_ge(cb_ready, h + 1)
                    else:
                        pe.wait_ge(s_diff, 2 * (h - 1))
                    running_sum(4 + h % 2, h).then_inc(sb_psum, 1)
                if h in SSD_FILL:
                    project(*SSD_FILL[h], A_)
                if h >= 2:
                    y, c = h - 2, (h - 2) // 2
                    if y % 2 == 0:
                        if c < 2:
                            pe.wait_ge(cb_ready, SSD_G)
                        else:
                            pe.wait_ge(y_read, c - 1)
                    pe.wait_ge(s_mt, y + 1)
                    o = ps[(y % 2) * 64:(y % 2) * 64 + 64, 6 + c % 2, :]
                    mm(o[:, 0:S], xdt[:, 0, y * 64:(y + 1) * 64], dm[y % 3][:, 0:S], start=True, stop=False)
                    mm(o[:, P:S], xdt[:, 1, y * 64:(y + 1) * 64], dm[y % 3][:, S:384],
                       start=False, stop=True).then_inc(sy_psum, 1)

            def scores(h):
                if h >= 1:
                    pe.wait_ge(f_score, 4 * h)
                running_sum(4, SSD_H + h)
                mm(ps[:, 6 + h % 2, 0:P], qT[:, h, 0:P], kT[:, h, 0:P], start=True, stop=True)
                mm(ps[:, 6 + h % 2, P:384], qT[:, h, P:S], kT[:, h, :], start=True, stop=True).then_inc(f_psum, 1)

            pe.wait_ge(s_diff, 2 * SSD_H)
            pe.wait_ge(y_read, 7)
            on_act, count = drained(unit("k", 3))
            pe.wait_ge(dve_drained, count)
            pe.wait_ge(act_drained, drained(unit("q", 3))[1])
            scores(0)
            project("gate", 0, A_)
            pe.wait_ge(gsq, KT)
            for tb in range(TB):
                for g in range(SSD_G):
                    for j in range(2):
                        last = mm(ps[:, 5, 4 * tb + g:4 * tb + g + 1], sq[:, 2 * g + j, tb * P:(tb + 1) * P],
                                  c_g[:, 0:1], start=(j == 0), stop=(j == 1))
            last.then_inc(gms_psum, 1)
            project("gate", 1, A_)
            pe.wait_ge(gst_ready, 1)
            for g in range(SSD_G):
                for tb in range(TB):
                    at = (g % 2) * S + tb * P
                    last = mm(ps[:, 3 + 2 * (g // 2), at:at + P], gst[:, tb, g:g + 1].to_broadcast([P, P]), idn,
                              start=True, stop=True)
            last.then_inc(g_rows, 1)
            pe.wait_ge(y_read, 8)
            for h in range(1, FOX_H + 1):
                if h < FOX_H:
                    scores(h)
                if h == 1:
                    project("gate", 2, A_)
                    pe.wait_ge(y_normed, KT)
                y = h - 1
                pe.wait_ge(f_norm, 2 * h)
                for j in range(3):
                    last = nc.tensor.transpose(ps[:, 3, j * P:(j + 1) * P], ft[y % 2][:, j * P:(j + 1) * P], idn)
                last.then_inc(pt_psum, 1)
                if 1 < h < 7:
                    project("gate", h + 1, A_)
                pe.wait_ge(pt_copied, y + 1)
                if y >= 1:
                    pe.wait_ge(yf_lo, y)
                o = ps[:, 5, 0:S]
                mm(o, V[:, 0, y * P:(y + 1) * P], PT[:, 0:S], start=True, stop=False)
                mm(o[:, P:S], V[:, 1, y * P:(y + 1) * P], PT[:, S:384], start=False, stop=True).then_inc(fo_psum, 1)
            project("ssd", 0, B_, (a_lo_ready, SPLIT["yssd"], 2))
            for n in range(1, 4):
                project("ssd", n, B_)
            project("fox", 0, C_, (yf_lo, 0, 1))
            for n in range(1, 4):
                project("fox", n, C_)
            project("ck", 0, B_, (a_lo_ready, SPLIT["mu"], 2))
            project("out", 0, A_, (a_lo_ready, SPLIT["merged"], 2))
            for n in range(1, 4):
                project("out", n, A_)
            project("ck", 1, B_)
            mean_squares(squared, 0)
            project("ck", 2, B_)
            inverse_rows(2)
            project("ck", 3, B_)
            project("cq", 0, C_, (a_lo_ready, SPLIT["u2"], 2))
            for n in range(1, 4):
                project("cq", n, C_)
            for h in range(X_H + 1):
                if h < X_H:
                    if h == 0:
                        pe.wait_ge(dve_drained, drained(unit("ck", 3))[1])
                    if h >= 2:
                        pe.wait_ge(x_exp, 2 * (h - 1))
                    pe.wait_ge(act_drained, drained(unit("cq", h))[1])
                    for b in range(TB):
                        for j in range(2):
                            last = mm(ps[:, 6 + h % 2, b * S:(b + 1) * S], qx[:, 2 * h + j, b * P:(b + 1) * P],
                                      kxT[:, 2 * h + j, :], start=(j == 0), stop=(j == 1))
                    last.then_inc(x_psum, 1)
                y = h - 1
                if h >= 1:
                    pe.wait_ge(x_norm, 2 * h)
                    for m in range(TB):
                        for b in range(TB):
                            at = m * S + b * P
                            last = nc.tensor.transpose(ps[:, 3, at:at + P],
                                                       xp[y % 2][:, b * S + m * P:b * S + (m + 1) * P], idn)
                    last.then_inc(xpt_psum, 1)
                if h < X_H:
                    project("cv", h, B_)
                if h >= 1:
                    pe.wait_ge(dve_drained, drained(unit("cv", y))[1])
                    pe.wait_ge(xpt_copied, y + 1)
                    if y >= 2:
                        pe.wait_ge(ox_lo, y - 1)
                    for j in range(2):
                        for m in range(TB):
                            last = mm(ps[:, 4 + y % 2, j * S:(j + 1) * S],
                                      Vx[:, m, (2 * y + j) * P:(2 * y + j + 1) * P],
                                      xPT[:, m * S:(m + 1) * S], start=(m == 0), stop=(m == TB - 1))
                    last.then_inc(xo_psum, 1)
            project("co", 0, A_, (ox_lo, 0, 2))
            for n in range(1, 4):
                project("co", n, A_)
            mean_squares(squared, 4)
            inverse_rows(3)
            pe.wait_ge(normed, 4)
            for tb in range(TB):
                for k in range(KT):
                    last = mm(ps[:, 3, 256 + NE * tb:256 + NE * (tb + 1)], uT[:, k, tb * P:(tb + 1) * P], wrt[:, k, :],
                              start=(k == 0), stop=(k == KT - 1))
            last.then_inc(lg_psum, 1)
            for j in range(4):
                tb, half = j // 2, j % 2
                for c in range(4):
                    last = nc.tensor.transpose(ps[:, 4 + j, c * P:(c + 1) * P],
                                               uT[:, 4 * half + c, tb * P:(tb + 1) * P], idn)
                last.then_inc(tok_psum, 1)
            pe.wait_ge(msk_ready, TB)
            mm(ps[:, 0, 0:NE], tri[:, 0:P], msk[:, 0, :], start=True, stop=True)
            mm(ps[:, 0, NE:2 * NE], tri[:, P:2 * P], msk[:, 0, :], start=True, stop=False)
            mm(ps[:, 0, NE:2 * NE], tri[:, 0:P], msk[:, 1, :], start=False, stop=True)
            mm(ps[0:NE, 0, 64:65], msk[:, 0, :], tri[:, P:P + 1], start=True, stop=False)
            mm(ps[0:NE, 0, 64:65], msk[:, 1, :], tri[:, P:P + 1], start=False, stop=True).then_inc(cnt_psum, 1)
            pe.wait_ge(extra_ready, 1)
            mm(ps[0:NE, 1, 0:1], tri[0:NE, 0:NE], ec[:, 1:2], start=True, stop=True)
            mm(ps[0:1, 1, 1:2], tri[0:NE, P:P + 1], ec[:, 1:2], start=True, stop=True).then_inc(off_psum, 1)
            pe.wait_ge(posm_ready, 1)
            for tb in range(TB):
                nc.tensor.transpose(ps[0:NE, 2, tb * P:(tb + 1) * P], posm[:, tb, :], idn)
                last = nc.tensor.transpose(ps[0:NE, 2, S + tb * P:S + (tb + 1) * P], gt[:, tb, :], idn)
            last.then_inc(ptr_psum, 1)
            pe.wait_ge(table_ready, 1)
            pe.wait_ge(ptr_ready, 2)
            for tb in range(TB):
                mm(ps[:, 0, 128 + NI * tb:128 + NI * (tb + 1)], posT[:, tb * P:(tb + 1) * P], pe1[:, :], start=True, stop=False)
                mm(ps[:, 0, 128 + NI * tb:128 + NI * (tb + 1)], c_s[0:NE, :], pb2[:, :], start=False, stop=True)
                mm(ps[:, 0, 256 + NI * tb:256 + NI * (tb + 1)], gtT[:, tb * P:(tb + 1) * P], pe1[:, :], start=True, stop=True)
            mm(ps[0:1, 0, 384:384 + NI], rowf[0:NE, :], pe1[:, :], start=True, stop=True).then_inc(item_psum, 1)
            pe.wait_ge(ld_b, 32)
            pe.wait_ge(tok_ready, 4)
            for j in range(4):
                tb, half = j // 2, j % 2
                mm(ps[:, 4 + j, :], gtT[:, tb * P:(tb + 1) * P], b2[0:NE, half * 512:(half + 1) * 512],
                   start=True, stop=False, skip_group_check=True)

            xg_cols = xgT.rearrange("p (m a j) -> p m a j", m=4, a=2)
            at_cols = actT.rearrange("p (m a j) -> p m a j", m=4, a=2)

            def gather(i1):
                pe.wait_ge(sel_ready, 2 * i1)
                for tb in range(TB):
                    for half in range(2):
                        last = mm(ps[64 * half:64 * (half + 1), 2, :], sel[:, 64 * tb:64 * (tb + 1)],
                                  xtok[:, tb, 512 * half:512 * (half + 1)], start=(tb == 0), stop=(tb == TB - 1))
                last.then_inc(xg_psum, 1)

            def gathered_transposes(i1):
                pe.wait_ge(xg_copied, i1)
                for m in range(4):
                    last = nc.tensor.transpose(ps[:, 2, m * P:(m + 1) * P], xgs[:, m * P:(m + 1) * P], idn)
                last.then_inc(xgt_psum, 1)

            def scatter():
                for tb in range(TB):
                    for half in range(2):
                        rows = slice(64 * half, 64 * (half + 1))
                        last = mm(ps[:, 4 + 2 * tb + half, :], sgT[rows, tb * P:(tb + 1) * P], ys[rows, :],
                                  start=False, stop=False, skip_group_check=True)
                return last

            pe.wait_ge(item_ready, 2)
            gather(1)
            gathered_transposes(1)
            pe.wait_ge(meta_ready, 1)
            n_items = pe.value_load(meta[0:1, NI:NI + 1], min_val=NE, max_val=MAX_ITEMS)

            def item(i, first=False):
                pe.wait_ge(selb_ready, i + 1)
                pe.wait_ge(xgt_ready, i + 1)
                for b in range(2):
                    for half in range(2):
                        last = mm(ps[64 * half:64 * (half + 1), b, :], selb[0:NE, :],
                                  b1[0:NE, b * DE + 512 * half:b * DE + 512 * (half + 1)], start=True, stop=False)
                last.then_inc(e_used, 1)
                for s in range(8):
                    if s < 4:
                        pe.wait_ge(x_loaded[s] if first else e_loaded[s], 16 if first else 16 * i)
                    else:
                        pe.wait_ge(e_loaded[s], 16 * i + 16)
                    for b in range(2):
                        for half in range(2):
                            last = mm(ps[64 * half:64 * (half + 1), b, :], xg_cols[:, s % 4, s // 4, :],
                                      e_slot(s, first)[:, b * DE + 512 * half:b * DE + 512 * (half + 1)],
                                      start=False, stop=(s == 7))
                    last.then_inc(e_used if s < 7 else h_psum, 1)
                pe.wait_ge(y_ready, i + 1)
                pe.wait_ge(sgt_ready, i + 1)
                scatter().then_inc(e_used, 1)
                gather(i + 2)
                pe.wait_ge(sg_ready, 2 * i + 2)
                for tb in range(TB):
                    last = nc.tensor.transpose(ps[:, 3, tb * P:(tb + 1) * P], sg[:, tb * P:(tb + 1) * P], idn)
                last.then_inc(sgt_psum, 1)
                gathered_transposes(i + 2)
                pe.wait_ge(act_ready, i + 1)
                for m in range(4):
                    last = nc.tensor.transpose(ps[:, 0, m * P:(m + 1) * P], lin[:, m * P:(m + 1) * P], idn)
                last.then_inc(at_psum, 1)
                pe.wait_ge(at_ready, i + 1)
                pe.wait_ge(sgt_ready, i + 2)
                for s in range(8, 12):
                    pe.wait_ge(e_loaded[s], 16 * i + 16)
                    for c in range(2):
                        k = 2 * (s - 8) + c
                        for half in range(2):
                            last = mm(ps[64 * half:64 * (half + 1), 3, :], at_cols[:, k % 4, k // 4, :],
                                      e_slot(s)[:, c, 512 * half:512 * (half + 1)],
                                      start=(k == 0), stop=(k == 7))
                    last.then_inc(e_used if s < 11 else y_psum, 1)

            item(0, first=True)
            with pe.Fori(1, n_items) as i:
                item(i)
            pe.wait_ge(y_ready, n_items + 1)
            scatter()
            for j in range(4):
                tb, half = j // 2, j % 2
                for c in range(4):
                    last = mm(ps[:, 4 + j, c * P:(c + 1) * P], hT[:, 4 * half + c, tb * P:(tb + 1) * P], idn,
                              start=False, stop=(c == 3), skip_group_check=True)
            last.then_inc(acc_done, 1)

        @block.scalar
        def _(act):
            A = nc.scalar.activation
            done = [0]

            def link(ins):
                done[0] += 1
                ins.then_inc(act_chain, 1)
                act.wait_ge(act_chain, done[0])

            def squares(n, src):
                for j in range(4):
                    act.wait_ge(tr_copied, 4 * n + j + 1)
                    A(sq[:, 2 * j:2 * j + 2, :], src[:, 2 * j:2 * j + 2, :], ACT.Square).then_inc(tr_squared, 1)

            def root(n):
                act.wait_ge(ms_psum, n + 1)
                if n:
                    act.wait_ge(st_ready, n)
                    act.wait_ge(ms_rows, n)
                A(st[:, :], ps[:, 3, 508:508 + TB], ACT.Sqrt, bias=eps[:, :]).then_inc(ms_root, 1)

            def split_weights(u):
                if u == NU:
                    return
                act.wait_ge(w_loaded[u % 2], 16 * (u // 2 + 1))
                for j in range(2):
                    p = 2 * u + j
                    if p >= 4:
                        act.wait_ge(w_done, p - 3)
                    A(w_hi[:, p % 4, :, :], raw_w[u % 2][:, :, j * P:(j + 1) * P], ACT.Copy).then_inc(w_hi_ready, 1)

            def split_act(name, src, dst, ready, count, step):
                for j in range(4):
                    act.wait_ge(ready, count + step * (j + 1))
                    A(dst[0][:, 2 * j:2 * j + 2, :], src[:, 2 * j:2 * j + 2, :], ACT.Copy).then_inc(a_hi_ready, 1)

            def step(name, n):
                u = unit(name, n)
                split_weights(u + 1)
                if name not in ON_ACT:
                    return
                act.wait_ge(w_done, 2 * u + 2)
                bank = ps[:, u % PJ, :]
                two = bank.rearrange("p (a b) -> p a b", a=2)
                if name == "xbc":
                    ins = A(xb[:, 2 * n:2 * n + 2, 4:4 + S], two, ACT.Copy)
                elif name == "z":
                    ins = A(zs[:, 2 * n:2 * n + 2, :], two, ACT.Silu)
                elif name == "q":
                    ins = A(qT[:, 2 * n:2 * n + 2, :], two, ACT.Copy, scale=FOX_SCALE)
                elif name == "cq":
                    ins = A(qx[:, 2 * n:2 * n + 2, :], two, ACT.Copy, scale=X_SCALE)
                else:
                    for j in range(2):
                        c = 2 * n + j
                        ins = A(gate[:, c, :], bank[:, j * S:(j + 1) * S], ACT.Identity,
                                bias=prm[:, B_GATE + c:B_GATE + c + 1])
                ins.then_inc(act_drained, 1)

            act.wait_ge(consts, 3)
            squares(0, hT)
            split_weights(0)
            root(0)
            act.wait_ge(ms_psum, 1)
            split_act("u", uT, A_, normed_tiles, 0, 1)
            squares(1, muT)
            act.wait_ge(consts, 12)
            for n in range(4):
                step("xbc", n)
            root(1)
            for n in range(4, 8):
                step("xbc", n)
            for c in range(16):
                act.wait_ge(conved, c + 1)
                A(xc[:, c, :], xc[:, c, :], ACT.Silu, bias=prm[:, CB + c:CB + c + 1]).then_inc(xc_ready, 1)
                if c % 4 == 3:
                    step("z", c // 4)
            act.wait_ge(df_raw, 1)
            link(A(sp[:, :, :], raw[:, :, :], ACT.Abs))
            link(A(sp[:, :, :], sp[:, :, :], ACT.Exp, scale=-1.0))
            A(alog[:, :], alog[:, :], ACT.Exp).then_inc(df_soft, 1)
            A(sp[:, :, :], sp[:, :, :], ACT.Ln, bias=1.0).then_inc(df_soft, 1)
            for h in range(SSD_H + 3):
                if h < SSD_H:
                    act.wait_ge(s_diff, 2 * h + 2)
                    A(dm[h % 3], dm[h % 3], ACT.Exp).then_inc(s_exp, 1)
                if h in SSD_FILL:
                    step(*SSD_FILL[h])
                if h >= 3 and h % 2 == 1:
                    c = (h - 3) // 2
                    act.wait_ge(gated, c + 1)
                    A(sq[:, c, :], zs[:, c, :], ACT.Square).then_inc(gsq, 1)

            def exps(h):
                act.wait_ge(f_score, 4 * h + 4)
                t = ft[h % 2]
                A(t[:, 0:P], t[:, 0:P], ACT.Exp, bias=mx[:, h % 2, 0:1], accum_out=rsum[:, h % 2, 0:1]).then_inc(f_exp, 1)
                A(t[:, P:384], t[:, P:384], ACT.Exp, bias=mx[:, h % 2, 1:2], accum_out=rsum[:, h % 2, 1:2]).then_inc(f_exp, 1)

            exps(0)
            step("gate", 0)
            act.wait_ge(gms_psum, 1)
            A(gst[:, :, :], ps[:, 5, 0:TB * SSD_G].rearrange("p (a b) -> p a b", a=TB), ACT.Sqrt, bias=eps[:, :]).then_inc(g_root, 1)
            step("gate", 1)
            for h in range(1, FOX_H + 1):
                if h == 1:
                    split_act("yssd", zs, B_, y_normed, 0, 2)
                    exps(1)
                    step("gate", 2)
                y = h - 1
                act.wait_ge(pt_psum, y + 1)
                if y >= 1:
                    act.wait_ge(fo_psum, y)
                A(PT, ps[:, 3, 0:384], ACT.Copy).then_inc(pt_copied, 1)
                if 1 < h < FOX_H:
                    exps(h)
                if 1 < h < 7:
                    step("gate", h + 1)
                act.wait_ge(fo_psum, y + 1)
                if y == 0:
                    act.wait_ge(a_lo_ready, SPLIT["yssd"] + 4)
                A(C_[0][:, y, :], ps[:, 5, 0:S], ACT.Copy).then_inc(yf_hi, 1)
            act.wait_ge(act_drained, drained(unit("gate", 7))[1])
            A(gate[:, :, :], gate[:, :, :], ACT.Sigmoid).then_inc(gate_sig, 1)
            for n in range(4):
                step("ssd", n)
            act.wait_ge(w_done, 2 * unit("ssd", 3) + 2)
            for n in range(4):
                step("fox", n)
                act.wait_ge(merge_made, n + 1)
                A(A_[0][:, 2 * n:2 * n + 2, :], merged[:, 2 * n:2 * n + 2, :], ACT.Copy).then_inc(a_hi_ready, 1)
            split_act("mu", muT, B_, normed, 2, 0)
            step("ck", 0)
            for n in range(4):
                step("out", n)

            def norm_squares(name):
                for n in range(4):
                    act.wait_ge(dve_drained, drained(unit(name, n))[1])
                    A(sq[:, 2 * n:2 * n + 2, :], hT[:, 2 * n:2 * n + 2, :], ACT.Square).then_inc(squared, 1)

            norm_squares("out")
            step("ck", 1)
            root(2)
            step("ck", 2)
            split_act("u2", uT, C_, normed_tiles, 4, 1)
            step("ck", 3)
            for n in range(4):
                step("cq", n)
            for h in range(X_H + 1):
                y = h - 1
                if h < X_H:
                    act.wait_ge(x_max, h + 1)
                    if h >= 2:
                        act.wait_ge(xpt_psum, h - 1)
                    for b in range(TB):
                        A(xp[h % 2][:, S * b:S * (b + 1)], ps[:, 6 + h % 2, S * b:S * (b + 1)], ACT.Exp,
                          bias=mx[:, h % 2, b:b + 1], accum_out=rsum[:, h % 2, b:b + 1]).then_inc(x_exp, 1)
                if h >= 1:
                    act.wait_ge(xpt_psum, y + 1)
                    if y >= 1:
                        act.wait_ge(xo_psum, y)
                    A(xPT, ps[:, 3, :], ACT.Copy).then_inc(xpt_copied, 1)
                if h < X_H:
                    step("cv", h)
                if h >= 1:
                    act.wait_ge(xo_psum, y + 1)
                    A(A_[0][:, 2 * y:2 * y + 2, :].rearrange("p a b -> p (a b)"), ps[:, 4 + y % 2, :], ACT.Copy).then_inc(ox_hi, 1)
            for n in range(4):
                step("co", n)
            norm_squares("co")
            root(3)
            for j in range(4):
                act.wait_ge(tok_psum, j + 1)
                A(xtok[:, j // 2, 512 * (j % 2):512 * (j % 2 + 1)], ps[:, 4 + j, :], ACT.Copy).then_inc(tok_ready, 1)
            act.wait_ge(top_ready, 1)
            for tb in range(TB):
                A(em[:, tb, :], lg[:, tb, :], ACT.Exp, bias=smal[:, tb, 0:1]).then_inc(ex_ready, 1)
            act.wait_ge(ptr_psum, 1)
            A(posT[:, :], ps[0:NE, 2, 0:S], ACT.Copy).then_inc(ptr_ready, 1)
            A(gtT[:, :], ps[0:NE, 2, S:2 * S], ACT.Copy).then_inc(ptr_ready, 1)

            def gathered_copy(i1):
                act.wait_ge(xg_psum, i1)
                A(xgs, ps[:, 2, :], ACT.Copy).then_inc(xg_copied, 1)

            gathered_copy(1)
            act.wait_ge(meta_ready, 1)
            n_items = act.value_load(meta[0:1, NI:NI + 1], min_val=NE, max_val=MAX_ITEMS)
            with act.Fori(0, n_items) as i:
                act.wait_ge(glu_ready, i + 1)
                A(sig, glu, ACT.Sigmoid, scale=ALPHA).then_inc(sig_ready, 1)
                gathered_copy(i + 2)
                act.wait_ge(sgt_psum, i + 1)
                A(sgT, ps[:, 3, 0:S], ACT.Copy).then_inc(sgt_ready, 1)
                act.wait_ge(at_psum, i + 1)
                A(actT, ps[:, 0, :], ACT.Copy).then_inc(at_ready, 1)
                act.wait_ge(y_psum, i + 1)
                A(ys, ps[:, 3, :], ACT.Copy).then_inc(y_ready, 1)
            act.wait_ge(acc_done, 1)
            for tb in range(TB):
                A(outsb[:, tb, :], ps[:, 4 + 2 * tb:6 + 2 * tb, :].rearrange("p a b -> p (a b)"), ACT.Square,
                  accum_out=smal[:, tb, 2:3]).then_inc(f_sq, 1)
            act.wait_ge(f_sq, 2)
            A(smal[:, :, 3], smal[:, :, 2], ACT.Sqrt, scale=1.0 / D, bias=eps[:, :]).then_inc(f_root, 1)

        @block.vector
        def _(dve):
            V_ = nc.vector
            done = [0]

            def link(ins):
                done[0] += 1
                ins.then_inc(dve_chain, 1)
                dve.wait_ge(dve_chain, done[0])

            def inverse(n):
                dve.wait_ge(ms_root, n + 1)
                V_.reciprocal(st[:, :], st[:, :]).then_inc(st_ready, 1)

            def split_act(name, src, dst, j):
                dve.wait_ge(a_hi_ready, SPLIT[name] + j + 1)
                pair = slice(2 * j, 2 * j + 2)
                V_.tensor_tensor(dst[1][:, pair, :], src[:, pair, :], dst[0][:, pair, :].bitcast(f32),
                                 ALU.subtract).then_inc(a_lo_ready, 1)

            def apply_norm(n, src, dst, gain, name=None, pair=None):
                dve.wait_ge(ms_rows, n + 1)
                for c in range(KT):
                    ins = V_.scalar_tensor_tensor(out=dst[:, c, :], in0=src[:, c, :],
                                                  scalar=prm[:, gain + c:gain + c + 1], in1=ps[:, 3, 0:S],
                                                  op0=ALU.mult, op1=ALU.mult)
                    if name and c % 2 == 1 and c < KT - 1:
                        ins.then_inc(normed_tiles, 1)
                        if c >= 3:
                            split_act(name, dst, pair, c // 2 - 1)
                ins.then_inc(normed, 1)
                if name:
                    dve.wait_ge(normed, n + 1)
                    V_.engine_nop().then_inc(normed_tiles, 1)
                    split_act(name, dst, pair, 2)
                    split_act(name, dst, pair, 3)

            def copies(n, dst):
                for j in range(4):
                    dve.wait_ge(tr_psum, 4 * n + j + 1)
                    V_.tensor_copy(dst[:, 2 * j:2 * j + 2, :].rearrange("p a b -> p (a b)"), ps[:, 4 + j, :]).then_inc(tr_copied, 1)

            def split_weights(u):
                if u == NU:
                    return
                for j in range(2):
                    p = 2 * u + j
                    dve.wait_ge(w_hi_ready, p + 1)
                    V_.tensor_tensor(w_lo[:, p % 4, :, :], raw_w[u % 2][:, :, j * P:(j + 1) * P],
                                     w_hi[:, p % 4, :, :].bitcast(f32), ALU.subtract).then_inc(w_lo_ready, 1)

            def step(name, n):
                u = unit(name, n)
                split_weights(u + 1)
                if name in ON_ACT:
                    return
                dve.wait_ge(w_done, 2 * u + 2)
                bank = ps[:, u % PJ, :]
                two = bank.rearrange("p (a b) -> p a b", a=2)
                pair = slice(2 * n, 2 * n + 2)
                if name == "k":
                    ins = V_.tensor_copy(kT[:, pair, :], two)
                elif name == "ck":
                    ins = V_.tensor_copy(kxT[:, pair, :], two)
                elif name == "v":
                    ins = V_.tensor_copy(V[:, :, 256 * n:256 * (n + 1)], two)
                elif name == "cv":
                    ins = V_.tensor_copy(Vx[:, :, 256 * n:256 * (n + 1)], two)
                elif name == "ssd":
                    ins = V_.tensor_tensor(merged[:, pair, :], two, gate[:, pair, :], ALU.mult)
                elif name == "fox":
                    link(V_.tensor_tensor(mtmp[:, pair, :], two, gate[:, 8 + 2 * n:10 + 2 * n, :], ALU.mult))
                    ins = V_.tensor_tensor(merged[:, pair, :], merged[:, pair, :], mtmp[:, pair, :], ALU.add)
                else:
                    ins = V_.tensor_tensor(hT[:, pair, :], hT[:, pair, :], two, ALU.add)
                ins.then_inc(dve_drained, 1)
                if name == "fox":
                    dve.wait_ge(dve_drained, drained(u)[1])
                    V_.engine_nop().then_inc(merge_made, 1)

            dve.wait_ge(prm_psum, 1)
            V_.tensor_copy(prm[:, 0:136], ps[:, 3, 0:136]).then_inc(prm_ready, 1)
            dve.wait_ge(prm_ready, 1)
            copies(0, hT)
            dve.wait_ge(tr_copied, 4)
            split_weights(0)
            inverse(0)
            copies(1, muT)
            apply_norm(0, hT, uT, G_MIX, "u", A_)
            for n in range(2):
                step("xbc", n)
            for q in range(4):
                dve.wait_ge(act_drained, 2 * q + 2)
                for tap in range(4):
                    for c in range(4 * q, 4 * q + 4):
                        src = xb[:, c, 1 + tap:1 + tap + S]
                        w = prm[:, CW + 16 * tap + c:CW + 16 * tap + c + 1]
                        if tap == 0:
                            ins = V_.tensor_scalar(xc[:, c, :], src, w, None, ALU.mult)
                        else:
                            dve.wait_ge(dve_chain, done[0] - 3)
                            ins = V_.scalar_tensor_tensor(out=xc[:, c, :], in0=src, scalar=w, in1=xc[:, c, :],
                                                          op0=ALU.mult, op1=ALU.add)
                        if tap < 3:
                            ins.then_inc(dve_chain, 1)
                            done[0] += 1
                        else:
                            ins.then_inc(conved, 1)
                            if c < 4 * q + 3:
                                dve.wait_ge(dve_chain, done[0])
                if q == 1:
                    inverse(1)
                if q < 3:
                    for n in (2 * q + 2, 2 * q + 3):
                        step("xbc", n)
                if q == 2:
                    apply_norm(1, muT, muT, G_MEM)
            for n in range(4):
                step("z", n)
            dve.wait_ge(df_psum, 1)
            for tb in range(TB):
                last = V_.tensor_tensor(raw[:, tb, :], ps[:, 3, 32 * tb:32 * tb + 24], bdf[:, :], ALU.add)
            last.then_inc(df_raw, 1)
            dve.wait_ge(df_raw, 1)
            dve.wait_ge(df_soft, 2)
            link(V_.scalar_tensor_tensor(out=dt[:, :, :], in0=raw[:, :, 0:16], scalar=0.0, in1=sp[:, :, 0:16],
                                         op0=ALU.max, op1=ALU.add))
            for tb in range(TB):
                V_.scalar_tensor_tensor(out=af[:, tb, 0:16], in0=dt[:, tb, :], scalar=-1.0, in1=alog[:, :],
                                        op0=ALU.mult, op1=ALU.mult)
            V_.scalar_tensor_tensor(out=af[:, :, 16:24], in0=raw[:, :, 16:24], scalar=0.0, in1=sp[:, :, 16:24],
                                    op0=ALU.min, op1=ALU.subtract).then_inc(df_ready, 1)
            dve.wait_ge(cum_psum, 1)
            V_.tensor_copy(actok[:, :, :], ps[:, 3, 64:128].rearrange("p (a b) -> p a b", a=2)[:, :, 0:24]).then_inc(cum_ready, 1)
            V_.tensor_copy(acT[:, :], ps[0:24, 3, 256:512]).then_inc(cum_ready, 1)
            for j in range(4):
                tb, half = j // 2, j % 2
                dve.wait_ge(xdt_psum, j + 1)
                V_.tensor_tensor(xdt[:, tb, 512 * half:512 * (half + 1)].rearrange("p (h e) -> p h e", e=64),
                                 ps[:, 4 + j, :].rearrange("p (h e) -> p h e", e=64),
                                 dt[:, tb, 8 * half:8 * half + 8].unsqueeze(2).to_broadcast([P, 8, 64]),
                                 ALU.mult).then_inc(xdt_ready, 1)
            for g in range(SSD_G):
                dve.wait_ge(cb_psum, g + 1)
                V_.tensor_tensor(cbm[:, g, :], ps[:, 4 + g, 0:384], tri[:, :], ALU.mult).then_inc(cb_ready, 1)
            dve.wait_ge(cum_ready, 2)
            dve.wait_ge(dsk_ready, 2)
            for h in range(SSD_H + 3):
                if h < SSD_H:
                    dve.wait_ge(sb_psum, h + 1)
                    if h >= 3:
                        dve.wait_ge(sy_psum, h - 2)
                    V_.tensor_scalar(dm[h % 3][:, 0:S], ps[:, 4 + h % 2, 0:S], actok[:, 0, h:h + 1], 0.0,
                                     ALU.subtract, ALU.min).then_inc(s_diff, 1)
                    V_.tensor_scalar(dm[h % 3][:, S:384], ps[:, 4 + h % 2, P:S], actok[:, 1, h:h + 1], 0.0,
                                     ALU.subtract, ALU.min).then_inc(s_diff, 1)
                if h in SSD_FILL:
                    step(*SSD_FILL[h])
                if h >= 3 and h % 2 == 1:
                    c = (h - 3) // 2
                    dve.wait_ge(sy_psum, 2 * c + 2)
                    V_.scalar_tensor_tensor(out=ytmp[c % 2], in0=xc[:, c, :], scalar=dsk[:, c:c + 1],
                                            in1=ps[:, 6 + c % 2, 0:S], op0=ALU.mult, op1=ALU.add).then_inc(y_read, 1)
                    dve.wait_ge(y_read, c + 1)
                    V_.tensor_tensor(zs[:, c, :], ytmp[c % 2], zs[:, c, :], ALU.mult).then_inc(gated, 1)

            def scores(h):
                cp, sc, t = ps[:, 4, :], ps[:, 6 + h % 2, :], ft[h % 2]
                dve.wait_ge(f_psum, h + 1)
                if h >= 2:
                    dve.wait_ge(pt_psum, h - 1)
                V_.scalar_tensor_tensor(out=negc[:, 0:P], in0=cp[:, 0:P], scalar=-1.0, in1=fmask[:, 0:P],
                                        op0=ALU.mult, op1=ALU.add)
                link(V_.scalar_tensor_tensor(out=negc[:, P:384], in0=cp[:, 0:S], scalar=-1.0, in1=fmask[:, P:384],
                                             op0=ALU.mult, op1=ALU.add))
                r = SSD_H + h
                V_.scalar_tensor_tensor(out=t[:, 0:P], in0=sc[:, 0:P], scalar=actok[:, 0, r:r + 1], in1=negc[:, 0:P],
                                        op0=ALU.add, op1=ALU.add).then_inc(f_score, 1)
                V_.scalar_tensor_tensor(out=t[:, P:384], in0=sc[:, P:384], scalar=actok[:, 1, r:r + 1],
                                        in1=negc[:, P:384], op0=ALU.add, op1=ALU.add).then_inc(f_score, 1)
                dve.wait_ge(f_score, 4 * h + 2)
                V_.reduce_max(mx[:, h % 2, 0:1], t[:, 0:P], AX.X, negate=True).then_inc(f_score, 1)
                V_.reduce_max(mx[:, h % 2, 1:2], t[:, P:384], AX.X, negate=True).then_inc(f_score, 1)

            def sums_inverse(h):
                dve.wait_ge(f_exp, 2 * h + 2)
                V_.reciprocal(rinv[:, h % 2, :], rsum[:, h % 2, :]).then_inc(f_rinv, 1)

            dve.wait_ge(gms_psum, 1)
            scores(0)
            step("gate", 0)
            sums_inverse(0)
            dve.wait_ge(g_root, 1)
            V_.reciprocal(gst[:, :, :], gst[:, :, :]).then_inc(gst_ready, 1)
            step("gate", 1)
            dve.wait_ge(g_rows, 1)
            for c in range(KT):
                g = c // 2
                V_.scalar_tensor_tensor(out=zs[:, c, :], in0=zs[:, c, :], scalar=prm[:, G_SSD + c:G_SSD + c + 1],
                                        in1=ps[:, 3 + 2 * (g // 2), (g % 2) * S:(g % 2) * S + S],
                                        op0=ALU.mult, op1=ALU.mult).then_inc(y_normed, 1)
            for h in range(1, FOX_H + 1):
                if h < FOX_H:
                    scores(h)
                if h == 1:
                    step("gate", 2)
                    for j in range(4):
                        split_act("yssd", zs, B_, j)
                if 1 < h < 7:
                    step("gate", h + 1)
                if h < FOX_H:
                    sums_inverse(h)
                y = h - 1
                dve.wait_ge(yf_hi, h)
                V_.tensor_tensor(C_[1][:, y, :], ps[:, 5, 0:S], C_[0][:, y, :].bitcast(f32), ALU.subtract).then_inc(yf_lo, 1)
            dve.wait_ge(gate_sig, 1)
            for n in range(4):
                step("ssd", n)
            for n in range(4):
                step("fox", n)
                if n:
                    split_act("merged", merged, A_, n - 1)
            split_act("merged", merged, A_, 3)
            for j in range(4):
                split_act("mu", muT, B_, j)
            step("ck", 0)
            for n in range(4):
                step("out", n)
            step("ck", 1)
            inverse(2)
            step("ck", 2)
            apply_norm(2, hT, uT, G_CROSS, "u2", C_)
            step("ck", 3)
            for n in range(4):
                step("cq", n)
            for h in range(X_H + 1):
                if h < X_H:
                    dve.wait_ge(x_psum, h + 1)
                    V_.tensor_reduce(mx[:, h % 2, :], ps[:, 6 + h % 2, :].rearrange("p (a b) -> p a b", a=2), AX.X,
                                     ALU.max, negate=True).then_inc(x_max, 1)
                    dve.wait_ge(x_exp, 2 * h + 2)
                    V_.reciprocal(rinv[:, h % 2, :], rsum[:, h % 2, :]).then_inc(x_rinv, 1)
                    step("cv", h)
                if h >= 1:
                    y = h - 1
                    dve.wait_ge(ox_hi, h)
                    V_.tensor_tensor(A_[1][:, 2 * y:2 * y + 2, :].rearrange("p a b -> p (a b)"), ps[:, 4 + y % 2, :],
                                     A_[0][:, 2 * y:2 * y + 2, :].rearrange("p a b -> p (a b)").bitcast(f32),
                                     ALU.subtract).then_inc(ox_lo, 1)
            for n in range(4):
                step("co", n)
            inverse(3)
            apply_norm(3, hT, uT, G_FFN)
            dve.wait_ge(lg_psum, 1)
            for tb in range(TB):
                last = V_.tensor_tensor(lg[:, tb, :], ps[:, 3, 256 + NE * tb:256 + NE * (tb + 1)], brt[:, :], ALU.add)
            link(last)
            for tb in range(TB):
                link(V_.max(v8[:, tb, :], lg[:, tb, :]))
                link(V_.max_index(i8[:, tb, :], v8[:, tb, :], lg[:, tb, :]))
            V_.tensor_scalar(smal[:, :, 0], v8[:, :, 0], -1.0, None, ALU.mult).then_inc(top_ready, 1)
            link(V_.tensor_copy(i8f[:, :, :], i8[:, :, :]))
            for tb in range(TB):
                link(V_.tensor_scalar(msk[:, tb, :], iota[:, 0, 0:NE], i8f[:, tb, 0:1], None, ALU.is_equal))
                for k in range(1, TOPK):
                    ins = V_.scalar_tensor_tensor(out=msk[:, tb, :], in0=iota[:, 0, 0:NE], scalar=i8f[:, tb, k:k + 1],
                                                  in1=msk[:, tb, :], op0=ALU.is_equal, op1=ALU.add)
                    if k < TOPK - 1:
                        link(ins)
                ins.then_inc(msk_ready, 1)
            dve.wait_ge(msk_ready, 2)
            dve.wait_ge(ex_ready, 2)
            for tb in range(TB):
                link(V_.scalar_tensor_tensor(out=gt[:, tb, :], in0=em[:, tb, :], scalar=1.0, in1=msk[:, tb, :],
                                             op0=ALU.mult, op1=ALU.mult, accum_out=smal[:, tb, 1:2]))
            link(V_.reciprocal(smal[:, :, 1], smal[:, :, 1]))
            for tb in range(TB):
                V_.tensor_scalar(gt[:, tb, :], gt[:, tb, :], smal[:, tb, 1:2], None, ALU.mult)
            link(V_.tensor_scalar(posm[:, :, :], msk[:, :, :], -(NO_SLOT + 1.0), NO_SLOT, ALU.mult, ALU.add))
            dve.wait_ge(cnt_psum, 1)
            V_.tensor_tensor(posm[:, :, :], posm[:, :, :], ps[:, 0, 0:2 * NE].rearrange("p (a b) -> p a b", a=2),
                             ALU.add).then_inc(posm_ready, 1)
            link(V_.tensor_copy(ec[:, 0:1], ps[0:NE, 0, 64:65]))
            link(V_.tensor_scalar(ec[:, 1:2], ec[:, 0:1], float(SLOTS), None, ALU.is_gt))
            for b in range(2, MAX_EXTRA + 1):
                ins = V_.scalar_tensor_tensor(out=ec[:, 1:2], in0=ec[:, 0:1], scalar=float(SLOTS * b), in1=ec[:, 1:2],
                                              op0=ALU.is_gt, op1=ALU.add)
                if b < MAX_EXTRA:
                    link(ins)
            ins.then_inc(extra_ready, 1)
            dve.wait_ge(extra_ready, 1)
            dve.wait_ge(off_psum, 1)
            link(V_.tensor_scalar(ec[:, 3:4], ps[0:NE, 1, 0:1], float(NE), None, ALU.add))
            link(V_.tensor_tensor(ec[:, 2:3], ec[:, 3:4], ec[:, 1:2], ALU.subtract))
            link(V_.tensor_scalar(ec[:, 4:5], ec[:, 2:3], -1.0, None, ALU.add))
            link(V_.tensor_scalar(pe2[:, :], iota[0:NE, 0, :], ec[:, 3:4], None, ALU.is_lt))
            link(V_.scalar_tensor_tensor(out=pe2[:, :], in0=iota[0:NE, 0, :], scalar=ec[:, 2:3], in1=pe2[:, :],
                                         op0=ALU.is_ge, op1=ALU.mult))
            V_.scalar_tensor_tensor(out=pb2[:, :], in0=iota[0:NE, 0, :], scalar=ec[:, 4:5], in1=pe2[:, :],
                                    op0=ALU.subtract, op1=ALU.mult)
            V_.tensor_scalar(meta[0:1, NI:NI + 1], ps[0:1, 1, 1:2], float(NE), None, ALU.add)
            V_.tensor_tensor(pe1[:, :], pe2[:, :], ident[0:NE, 0:NI], ALU.add).then_inc(table_ready, 1)
            dve.wait_ge(item_psum, 1)
            V_.tensor_copy(ipos[:, :, :], ps[:, 0, 128:256].rearrange("p (a b) -> p a b", a=2)).then_inc(item_ready, 1)
            V_.tensor_copy(igate[:, :, :], ps[:, 0, 256:384].rearrange("p (a b) -> p a b", a=2)).then_inc(item_ready, 1)
            V_.tensor_copy(meta[0:1, 0:NI], ps[0:1, 0, 384:384 + NI]).then_inc(meta_ready, 1)
            dve.wait_ge(meta_ready, 1)
            dve.wait_ge(w_done, 2 * NU)
            dve.wait_ge(table_ready, 1)

            def selection(i, i1):
                for tb in range(TB):
                    V_.tensor_scalar(sel[:, 64 * tb:64 * (tb + 1)], iota[:, 0, :], ipos[:, tb, bass.ds(i, 1)], None,
                                     ALU.is_equal).then_inc(sel_ready, 1)

            def bias_row(i):
                V_.tensor_copy(selb[0:NE, :], pe1[:, bass.ds(i, 1)].to_broadcast([NE, SLOTS])).then_inc(selb_ready, 1)

            def gathered_columns(i1):
                dve.wait_ge(xgt_psum, i1)
                V_.tensor_copy(xgT, ps[:, 2, :]).then_inc(xgt_ready, 1)

            selection(0, 1)
            bias_row(0)
            V_.memset(ys, 0.0).then_inc(y_ready, 1)
            V_.memset(sgT, 0.0).then_inc(sgt_ready, 1)
            gathered_columns(1)
            n_items = dve.value_load(meta[0:1, NI:NI + 1], min_val=NE, max_val=MAX_ITEMS)
            with dve.Fori(0, n_items) as i:
                dve.wait_ge(xg_psum, i + 1)
                selection(i + 1, i + 2)
                for tb in range(TB):
                    V_.tensor_scalar(sg[:, P * tb:P * (tb + 1)], iota[:, :, :].rearrange("p a b -> p (a b)"),
                                     ipos[:, tb, bass.ds(i, 1)], igate[:, tb, bass.ds(i, 1)],
                                     ALU.is_equal, ALU.mult).then_inc(sg_ready, 1)
                dve.wait_ge(h_psum, i + 1)
                V_.tensor_scalar(glu, ps[:, 0, :], LIMIT, None, ALU.min).then_inc(glu_ready, 1)
                V_.tensor_scalar(lin, ps[:, 1, :], LIMIT, -LIMIT, ALU.min, ALU.max).then_inc(dve_chain, 1)
                dve.wait_ge(dve_chain, 2 * i + (done[0] + 1))
                V_.scalar_tensor_tensor(out=lin, in0=lin, scalar=1.0, in1=glu, op0=ALU.add, op1=ALU.mult).then_inc(dve_chain, 1)
                dve.wait_ge(dve_chain, 2 * i + (done[0] + 2))
                dve.wait_ge(sig_ready, i + 1)
                V_.tensor_tensor(lin, lin, sig, ALU.mult).then_inc(act_ready, 1)
                bias_row(i + 1)
                gathered_columns(i + 2)
            dve.wait_ge(ld_g, 16)
            dve.wait_ge(f_root, 1)
            V_.reciprocal(smal[:, :, 1], smal[:, :, 3]).then_inc(f_root, 1)
            dve.wait_ge(f_root, 2)
            for tb in range(TB):
                V_.scalar_tensor_tensor(out=outsb[:, tb, :], in0=ps[:, 4 + 2 * tb:6 + 2 * tb, :].rearrange("p a b -> p (a b)"),
                                        scalar=smal[:, tb, 1:2], in1=gfin, op0=ALU.mult, op1=ALU.mult).then_inc(out_ready, 1)


INPUTS = ["x", "mem", "norm_mix_g", "w_in", "conv_w", "conv_b", "dt_bias", "a_log", "d_skip", "ssd_norm_g",
          "w_ssd_branch", "b_forget", "w_fox_branch", "b_gates", "w_out", "norm_cross_g", "norm_mem_g",
          "w_cross_q", "w_cross_kv", "w_cross_o", "norm_ffn_g", "w_router", "b_router", "w_expert_in",
          "b_expert_in", "w_expert_out", "b_expert_out", "norm_final_g"]


def kernel(**inputs):
    import concourse.bacc as bacc
    from concourse.bass_utils import run_bass_kernel_spmd

    nc = bacc.Bacc("TRN2", target_bir_lowering=False, num_devices=1)
    arrays, args = {}, []
    for name in INPUTS:
        a = np.ascontiguousarray(inputs[name])
        arrays[f"in_{name}"] = a
        args.append(nc.dram_tensor(f"in_{name}", a.shape, mybir.dt.from_np(a.dtype), kind="ExternalInput").ap())
    args.append(nc.dram_tensor("out_h", (1, S, D), mybir.dt.float32, kind="ExternalOutput").ap())
    layer_program(nc, *args)
    result = run_bass_kernel_spmd(nc, [arrays], core_ids=[0])
    return result.results[0]["out_h"]
```

```python
from contextlib import ExitStack

import numpy as np

import concourse.bass as bass
from concourse import mybir

D = 1024
S = 256
P = 128
KT = D // P
TB = S // P
SSD_H, SSD_P = 16, 64
SSD_G = 4
FOX_H = 8
X_H, X_D = 4, 256
NE, TOPK = 32, 4
DE = 1024
SLOTS = 64
MAX_EXTRA = S // SLOTS - 1
MAX_ITEMS = NE + TOPK * S // SLOTS
NI = 64
EARLY = 5
EPS = 1e-6
LIMIT, ALPHA = 7.0, 1.702
NO_SLOT = 4096.0
MASKED = -1e30
FOX_SCALE = 128 ** -0.5
X_SCALE = X_D ** -0.5

C_Z, C_XBC, C_DT, C_Q, C_K, C_V, C_F, C_G = 0, 1024, 3072, 3088, 4112, 5136, 6160, 6168


def layer_program(nc, x, mem, norm_mix_g, w_in, conv_w, conv_b, dt_bias, a_log, d_skip, ssd_norm_g,
                  w_ssd, b_forget, w_fox, b_gates, w_out, norm_cross_g, norm_mem_g, w_cq, w_ckv, w_co,
                  norm_ffn_g, w_router, b_router, w_ein, b_ein, w_eout, b_eout, norm_final_g, out):
    f32, f32r, i32, u32 = mybir.dt.float32, mybir.dt.float32r, mybir.dt.int32, mybir.dt.uint32
    ALU = mybir.AluOpType
    ACT = mybir.ActivationFunctionType
    AX = mybir.AxisListType

    units = []

    def add(name, w, col0, *numbers):
        for n in numbers:
            units.append((name, n, w[:, col0 + 256 * n:col0 + 256 * (n + 1)]))

    win = w_in[0]
    add("xbc", win, C_XBC, *range(8))
    add("z", win, C_Z, *range(4))
    add("q", win, C_Q, *range(4))
    add("k", win, C_K, *range(4))
    add("v", win, C_V, *range(4))
    add("gate", win, C_G, *range(8))
    add("ssd", w_ssd[0], 0, *range(4))
    add("fox", w_fox[0], 0, *range(4))
    add("ck", w_ckv[0], 0, 0)
    add("out", w_out[0], 0, *range(4))
    add("ck", w_ckv[0], 0, 1, 2, 3)
    add("cq", w_cq[0], 0, *range(4))
    add("cv", w_ckv[0], D, *range(4))
    add("co", w_co[0], 0, *range(4))
    NU = len(units)
    ON_ACT = {"xbc", "z", "q", "gate", "cq"}
    BY_TOKEN = {"v", "cv"}

    def unit(name, n):
        return next(u for u, (a, b, _) in enumerate(units) if (a, b) == (name, n))

    def drained(u):
        act = units[u][0] in ON_ACT
        return act, sum((units[v][0] in ON_ACT) == act for v in range(u + 1))

    SPLIT = {"u": 0, "yssd": 4, "mu": 8, "merged": 12, "u2": 16}
    SSD_FILL = {}
    for h_, n_ in zip((0, 1, 3, 4, 5, 7, 8, 9, 11, 12, 13, 15), range(12)):
        SSD_FILL[h_] = (("q", "k", "v")[n_ // 4], n_ % 4)

    FOX_FILL = {h_: ("gate", h_ + 1) for h_ in range(1, 7)} | {7: ("ssd", 0), 8: ("ssd", 1)}

    PJ = 3

    with ExitStack() as ctx:
        def sb(name, shape, dt=f32):
            return ctx.enter_context(nc.sbuf_tensor(name, shape, dt))

        def sem(name):
            return ctx.enter_context(nc.semaphore(name))

        PAGE = 2048
        arena = sb("arena", [P, 24 * PAGE])
        arena_at = nc.sbuf_base - 4 * 24 * PAGE

        def page(n, count=PAGE, at=0):
            return arena[:, n * PAGE + at:n * PAGE + at + count]

        def tiles(ap, n):
            return ap.rearrange("p (c t) -> p c t", c=n)

        def rounded(name, first, shape):
            return nc.alloc_sbuf_tensor_at(name, shape, f32r, offset=arena_at + 4 * PAGE * first)

        xin = tiles(page(0), TB)
        memin = tiles(page(1), TB)
        xb = tiles(page(2, 16 * 260), 16)
        cbm = tiles(page(4, 1536, 64), SSD_G)
        PT = page(4, 384, 64)
        xc = tiles(page(5, 2 * PAGE), 16)
        zs = tiles(page(8), KT)
        xdt = tiles(page(9), TB)
        qT, kT, V = tiles(page(0), KT), tiles(page(1), KT), tiles(page(7), TB)
        dm = [page(2, 384, 384 * j) for j in range(4)]
        ytmp = [page(3, 256, 256 * j) for j in range(2)]
        gate = tiles(page(2, 2 * PAGE), 16)
        merged = tiles(page(5), KT)
        mtmp = tiles(page(0), KT)
        ft = [page(4, 384, 448 + 384 * j) for j in range(2)]
        negc = page(4, 384, 1216)
        kxT, Vx, qx = tiles(page(6), KT), tiles(page(7), TB), tiles(page(20), KT)
        xp = [page(21, 512, 512 * j) for j in range(2)]
        xPT = page(21, 512, 1024)
        w_raw = nc.alloc_sbuf_tensor_at("w_raw", [P, 2, KT, 256], f32, offset=arena_at + 4 * PAGE * 14)
        raw_w = [w_raw[:, j, :, :] for j in range(2)]
        w_hi = rounded("w_hi", 12, [P, 4, KT, P])
        w_lo = rounded("w_lo", 10, [P, 4, KT, P])
        splits = {}
        for name, first in (("A", 16), ("B", 18), ("C", 8)):
            splits[name] = [rounded(f"{name}_{part}", first + j, [P, KT, S]) for j, part in enumerate(("hi", "lo"))]
        A_, B_, C_ = splits["A"], splits["B"], splits["C"]
        muT = tiles(page(20), KT)
        sq = tiles(page(21), KT)
        xtok = tiles(page(21), TB)
        uT = tiles(page(22), KT)
        hT = tiles(page(23), KT)
        def w_at(at, n):
            return page(12, n, at)

        xgs, xgT, glu, sig, lin, actT, ys = (w_at(512 * j, 512) for j in range(7))
        sgT, sg = w_at(3584, 256), w_at(3840, 256)
        b1 = page(22)
        outsb = tiles(page(1), TB)

        late = sb("late", [P, PAGE])
        fmask = late[:, 0:384]
        c_g = late[:, 384:512]
        late_at = nc.sbuf_base - 4 * PAGE
        acT = [nc.alloc_sbuf_tensor_at(f"acT_{part}", [24, S], f32r, offset=late_at + 4 * at)
               for part, at in (("hi", 512), ("lo", 1792))]
        dfT = late[0:24, 1536:1792]
        wdf = late[:, 768:960].rearrange("p (k n) -> p k n", k=KT)
        prow = late[:, 1024:1152]
        prow2 = late[0:16, 1152:1280]
        raw, sp, af = (tiles(late[:, at:at + 48], TB) for at in (1280, 1328, 1376))
        dt = tiles(late[:, 1424:1456], TB)
        alog, dall = late[:, 1456:1472], late[:, 1472:1488]
        dsk, bdf = late[:, 1488:1496], late[:, 1496:1520]
        OUTSIDE = [late[:, :], page(18), page(19), page(14), page(15), page(16), page(17),
                   page(23)]
        XN = len(OUTSIDE)
        gfin = late[:, 0:D]

        ident = sb("ident", [P, P])
        ident_r = sb("ident_r", [24, 24], f32r)
        tri = sb("tri", [P, 384])
        c_d = sb("c_d", [P, P])
        c_s = sb("c_s", [P, P])
        eps = sb("eps", [P, 1])
        prm = sb("prm", [P, 144])
        brt = sb("brt", [P, NE])
        wrt = sb("wrt", [P, KT, NE])
        actok = sb("actok", [P, TB, 24])
        st = sb("st", [P, TB])
        gst = sb("gst", [P, TB, SSD_G])
        mx = sb("mx", [P, 2, 2])
        warm = st[:, 0:1]
        rsum = sb("rsum", [P, 2, 2])
        rinv = sb("rinv", [P, 2, 2])
        iota = sb("iota", [P, 2, NI])
        iotai = sb("iotai", [P, 2, NI], i32)
        islot = sb("islot", [P, 2, NI])
        ifurther = sb("ifurther", [NE, 2, NI])
        fulls = sb("fulls", [NE, MAX_EXTRA])
        rowi = sb("rowi", [P, 1], i32)
        rowf = sb("rowf", [P, 1])
        table_at = iter(range(0, PAGE, 64))

        def table(n, rows=P):
            at = [next(table_at) for _ in range(n)][0]
            return page(20, 64 * n, at)[0:rows, :]

        def by_block(ap):
            return ap.rearrange("p (b n) -> p b n", b=TB)

        lg, em, msk, gt, posm = (by_block(table(1)) for _ in range(5))
        chosen_at = table(4)
        chosen = chosen_at.rearrange("p (b k e) -> p b k e", b=TB, k=TOPK)
        posT, lgT = chosen_at[0:NE, :], table(4, NE)
        pe2, pb2 = table(1, NE), table(1, NE)
        table(1)
        b2 = page(20, 16 * 64)
        gtT, pe1 = table(4, NE), table(1, NE)
        ipos = by_block(table(2))
        igate = by_block(table(2))
        sel, selb = table(2), table(1)
        v8 = sb("v8", [P, TB, 8])
        i8 = sb("i8", [P, TB, 8], u32)
        i8f = sb("i8f", [P, TB, 8])
        smal = sb("smal", [P, TB, 4])
        ec = sb("ec", [NE, 8])
        meta = sb("meta", [1, NI + 1], i32)

        ps = ctx.enter_context(nc.psum_tensor("ps", [P, 8, 512], f32))

        CW, CB, G_MIX, G_CROSS, G_MEM, G_FFN, G_SSD, B_GATE = 0, 64, 80, 88, 96, 104, 112, 120

        ld_xs = [sem("ld_x0"), sem("ld_x1")]
        ld_mem, ld_prm, ld_small = sem("ld_mem"), sem("ld_prm"), sem("ld_small")
        w_loaded = [sem("w_loaded0"), sem("w_loaded1")]
        w_hi_ready, w_lo_ready = sem("w_hi_ready"), sem("w_lo_ready")
        w_done = sem("w_done")
        a_hi_ready, a_lo_ready = sem("a_hi_ready"), sem("a_lo_ready")
        act_drained, dve_drained = sem("act_drained"), sem("dve_drained")
        consts, ld_skip, dsk_ready = sem("consts"), sem("ld_skip"), sem("dsk_ready")
        pool_chain, dve_chain, act_chain = sem("pool_chain"), sem("dve_chain"), sem("act_chain")
        prm_psum, prm_ready = sem("prm_psum"), sem("prm_ready")
        tr_psum, tr_copied, tr_squared = sem("tr_psum"), sem("tr_copied"), sem("tr_squared")
        squared = sem("squared")
        sq_summed = sem("sq_summed")
        ms_psum, ms_root, st_ready, ms_rows, normed, normed_tiles = (sem("ms_psum"), sem("ms_root"), sem("st_ready"),
                                                       sem("ms_rows"), sem("normed"), sem("normed_tiles"))
        df_psum, df_raw, df_soft, df_ready = sem("df_psum"), sem("df_raw"), sem("df_soft"), sem("df_ready")
        cum_psum, cum_ready = sem("cum_psum"), sem("cum_ready")
        conv_begun, conved, xc_ready = sem("conv_begun"), sem("conved"), sem("xc_ready")
        dft_psum, dft_ready = sem("dft_psum"), sem("dft_ready")
        xdt_psum, xdt_ready = sem("xdt_psum"), sem("xdt_ready")
        cb_psum, cb_ready = sem("cb_psum"), sem("cb_ready")
        sb_psum, s_diff, s_exp, s_mt, sy_psum = (sem("sb_psum"), sem("s_diff"), sem("s_exp"),
                                                 sem("s_mt"), sem("sy_psum"))
        y_read, gated, gsq = sem("y_read"), sem("gated"), sem("gsq")
        gms_psum, g_root, gst_ready, g_rows, y_normed = (sem("gms_psum"), sem("g_root"), sem("gst_ready"),
                                                         sem("g_rows"), sem("y_normed"))
        merge_made = sem("merge_made")
        f_psum, f_score, f_exp, f_norm = sem("f_psum"), sem("f_score"), sem("f_exp"), sem("f_norm")
        pt_psum, pt_copied, fo_psum, yf_hi, yf_lo = (sem("pt_psum"), sem("pt_copied"), sem("fo_psum"),
                                                     sem("yf_hi"), sem("yf_lo"))
        gate_sig = sem("gate_sig")
        x_psum, x_max, x_exp, x_norm = sem("x_psum"), sem("x_max"), sem("x_exp"), sem("x_norm")
        xpt_psum, xpt_copied, xo_psum, ox_hi, ox_lo = (sem("xpt_psum"), sem("xpt_copied"),
                                                       sem("xo_psum"), sem("ox_hi"), sem("ox_lo"))
        tok_psum, tok_ready = sem("tok_psum"), sem("tok_ready")
        wrt_ready, lgt_psum, lgt_ready, pos_psum, gt_ready = (
            sem("wrt_ready"), sem("lgt_psum"), sem("lgt_ready"), sem("pos_psum"), sem("gt_ready"))
        lg_psum, top_ready, ex_ready, msk_ready = (
            sem("lg_psum"), sem("top_ready"), sem("ex_ready"), sem("msk_ready"))
        cnt_psum, extra_ready, off_psum, posm_ready, ptr_psum, ptr_ready = (
            sem("cnt_psum"), sem("extra_ready"), sem("off_psum"), sem("posm_ready"),
            sem("ptr_psum"), sem("ptr_ready"))
        table_ready, item_psum, item_ready, meta_ready = (
            sem("table_ready"), sem("item_psum"), sem("item_ready"), sem("meta_ready"))
        ld_b1, ld_b2 = sem("ld_b1"), sem("ld_b2")
        ld_g = sem("ld_g")
        e_loaded = [sem(f"e_loaded{s}") for s in range(12)]
        x_loaded = [sem(f"x_loaded{s}") for s in range(XN)]
        e_used = sem("e_used")
        sel_ready, sg_ready, selb_ready = sem("sel_ready"), sem("sg_ready"), sem("selb_ready")
        h_psum, glu_ready, sig_ready, act_ready = (sem("h_psum"), sem("glu_ready"),
                                                   sem("sig_ready"), sem("act_ready"))
        xg_psum, xg_copied, xgt_psum, xgt_ready = (sem("xg_psum"), sem("xg_copied"),
                                                   sem("xgt_psum"), sem("xgt_ready"))
        sgt_psum, sgt_ready, at_psum, at_ready = (sem("sgt_psum"), sem("sgt_ready"),
                                                  sem("at_psum"), sem("at_ready"))
        y_psum, y_ready = sem("y_psum"), sem("y_ready")
        f_inverse = sem("f_inverse")
        acc_done, f_sq, f_root, out_ready, stored = (sem("acc_done"), sem("f_sq"), sem("f_root"),
                                                     sem("out_ready"), sem("stored"))

        def e_chunk(expert, s):
            if s < 8:
                return w_ein[0, expert, s * P:(s + 1) * P, :]
            t = s - 8
            return w_eout[0, expert, 2 * t * P:2 * (t + 1) * P, :].rearrange("(c p) n -> p c n", p=P)

        def e_slot(s, outside=False):
            ap = OUTSIDE[s] if outside and s < XN else page(s)
            return ap if s < 8 else ap.rearrange("p (c n) -> p c n", c=2)

        block = ctx.enter_context(nc.Block())

        @block.sync
        def _(sp_):
            for half in range(2):
                cols = slice(512 * half, 512 * (half + 1))
                sp_.dma_start(xin[:, :, cols], x[0][:, cols].rearrange("(b p) d -> p b d", p=P)).then_inc(ld_xs[half], 16)
            def load(u):
                if u >= 2:
                    sp_.wait_ge(w_lo_ready, 2 * (u - 1))
                sp_.dma_start(raw_w[u % 2], units[u][2].rearrange("(k p) n -> p k n", p=P)).then_inc(w_loaded[u % 2], 16)

            def chunk(item, s):
                if item == 1 and s < XN:
                    sp_.dma_start(e_slot(s, True), e_chunk(1, s)).then_inc(x_loaded[s], 16)
                else:
                    sp_.dma_start(e_slot(s), e_chunk(item, s)).then_inc(e_loaded[s], 16)

            load(0)
            for at, src in ((CW, conv_w[0].rearrange("k (c p) -> (k c) p", p=P)),
                            (CB, conv_b[0].rearrange("(c p) -> c p", p=P)),
                            (G_MIX, norm_mix_g[0].rearrange("(c p) -> c p", p=P)),
                            (G_CROSS, norm_cross_g[0].rearrange("(c p) -> c p", p=P)),
                            (G_MEM, norm_mem_g[0].rearrange("(c p) -> c p", p=P)),
                            (G_FFN, norm_ffn_g[0].rearrange("(c p) -> c p", p=P)),
                            (G_SSD, ssd_norm_g[0].rearrange("(c p) -> c p", p=P))):
                sp_.dma_start(prow[at:at + src.shape[0], :], src).then_inc(ld_prm, 16)
            sp_.dma_start(prow2[:, :], b_gates[0].rearrange("b (c p) -> (b c) p", p=P)).then_inc(ld_prm, 16)

            load(1)
            sp_.dma_start(memin, mem[0].rearrange("(b p) d -> p b d", p=P)).then_inc(ld_mem, 16)
            for u in range(2, unit("out", 3)):
                load(u)
            sp_.wait_ge(a_lo_ready, SPLIT["merged"] + 4)
            ahead = [(0, 0), (0, 1), (0, 2), (0, 3), (0, 4), (0, 5), (1, 0)]
            for u in range(unit("out", 3), unit("cv", 1)):
                load(u)
                if ahead:
                    chunk(*ahead.pop(0))
            load(unit("cv", 1))
            sp_.wait_ge(w_done, 2 * unit("cq", 3) + 2)
            chunk(0, 8)
            sp_.dma_start(b1[0:NE, :], b_ein[0]).then_inc(ld_b1, 16)
            load(unit("cv", 2))
            chunk(0, 9)
            for u in range(unit("cv", 3), unit("co", 2)):
                load(u)
            sp_.wait_ge(xo_psum, X_H)
            load(unit("co", 2))
            chunk(0, 6)
            load(unit("co", 3))
            chunk(0, 7)
            for s in (1, 2):
                chunk(1, s)
            for page_, s in ((0, 3), (1, 4)):
                sp_.wait_ge(w_lo_ready, 2 * (NU - 1 + page_))
                chunk(1, s)
            sp_.wait_ge(w_done, 2 * NU)
            for item, s in ((0, 10), (0, 11), (1, 5), (1, 6)):
                chunk(item, s)
            sp_.wait_ge(tok_psum, 4)
            chunk(1, 7)
            sp_.wait_ge(item_psum, 2)
            sp_.dma_start(b2[0:NE, :], b_eout[0]).then_inc(ld_b2, 16)
            def first_chunks(i, outside, slots=range(XN)):
                for s in slots:
                    sp_.wait_ge(e_used, 12 * i + (s + 2))
                    sp_.dma_start(e_slot(s, outside), e_chunk(i + 2, s)).then_inc((x_loaded if outside else e_loaded)[s], 16)

            def last_chunks(i):
                for s in range(XN, 12):
                    sp_.wait_ge(e_used, 12 * i + (s + 2))
                    sp_.dma_start(e_slot(s), e_chunk(i + 1, s)).then_inc(e_loaded[s], 16)

            with sp_.Fori(0, EARLY) as pair:
                first_chunks(2 * pair, False)
                last_chunks(2 * pair)
                first_chunks(2 * pair + 1, True)
                last_chunks(2 * pair + 1)
            first_chunks(2 * EARLY, False, range(3))
            last_chunks(2 * EARLY)
            first_chunks(2 * EARLY, False, range(3, XN))
            last_chunks(2 * EARLY + 1)
            first_chunks(2 * EARLY + 1, True)
            with sp_.Fori(EARLY + 1, NE // 2 - 1) as pair:
                last_chunks(2 * pair)
                first_chunks(2 * pair, False)
                last_chunks(2 * pair + 1)
                first_chunks(2 * pair + 1, True)
            last_chunks(NE - 2)
            sp_.wait_ge(e_used, 12 * (NE - 1) + 2)
            sp_.dma_start(gfin, norm_final_g.partition_broadcast(P)).then_inc(ld_g, 16)
            sp_.wait_ge(meta_ready, 1)
            n_items = sp_.value_load(meta[0:1, NI:NI + 1], min_val=NE, max_val=MAX_ITEMS)
            with sp_.If(n_items > NE):
                with sp_.Fori(NE, n_items) as i:
                    e = sp_.value_load(meta[0:1, bass.ds(i, 1)], min_val=0, max_val=NE - 1)
                    for s in range(12):
                        sp_.wait_ge(e_used, 12 * i + (s - 10))
                        sp_.dma_start(e_slot(s), e_chunk(e, s)).then_inc(e_loaded[s], 16)
            for tb in range(TB):
                for half in range(2):
                    cols = slice(512 * half, 512 * (half + 1))
                    sp_.wait_ge(out_ready, 2 * tb + half + 1)
                    sp_.dma_start(out[0, tb * P:(tb + 1) * P, cols], outsb[:, tb, cols]).then_inc(stored, 16)
            sp_.wait_ge(stored, 16 * 2 * TB)

        @block.gpsimd
        def _(pool):
            done = [0]

            def link(ins):
                done[0] += 1
                ins.then_inc(pool_chain, 1)
                pool.wait_ge(pool_chain, done[0])

            nc.gpsimd.memset(ident[:, :], 0.0).then_inc(pool_chain, 1)
            nc.gpsimd.memset(tri[:, :], 1.0).then_inc(pool_chain, 1)
            nc.gpsimd.memset(fmask[:, :], 0.0).then_inc(pool_chain, 1)
            done[0] = 3
            pool.wait_ge(pool_chain, 3)
            nc.gpsimd.affine_select(out=ident[:, :], in_=ident[:, :], compare_op=ALU.not_equal, fill=1.0,
                                    base=0, pattern=[[-1, P]], channel_multiplier=1).then_inc(consts, 1)
            nc.gpsimd.memset(c_d[:, :], 1.0 / D).then_inc(consts, 1)
            nc.gpsimd.memset(eps[:, :], EPS).then_inc(consts, 1)
            for at in (0, 256):
                nc.gpsimd.affine_select(out=tri[:, at:at + P], in_=tri[:, at:at + P], compare_op=ALU.is_ge,
                                        fill=0.0, base=0, pattern=[[1, P]], channel_multiplier=-1).then_inc(consts, 1)
                nc.gpsimd.affine_select(out=fmask[:, at:at + P], in_=fmask[:, at:at + P], compare_op=ALU.is_ge,
                                        fill=MASKED, base=0, pattern=[[-1, P]], channel_multiplier=1).then_inc(consts, 1)
            nc.gpsimd.memset(c_g[:, :], 1.0 / 256).then_inc(consts, 1)
            nc.gpsimd.memset(c_s[:, :], -float(SLOTS)).then_inc(consts, 1)
            link(nc.gpsimd.iota(iotai[:, :, :], pattern=[[0, 2], [1, NI]], base=0, channel_multiplier=0))
            nc.gpsimd.tensor_copy(iota[:, :, :], iotai[:, :, :]).then_inc(consts, 1)
            link(nc.gpsimd.iota(rowi[:, :], pattern=[[0, 1]], base=0, channel_multiplier=1))
            nc.gpsimd.tensor_copy(rowf[:, :], rowi[:, :]).then_inc(consts, 1)
            nc.gpsimd.memset(xb[:, :, 0:4], 0.0).then_inc(consts, 1)
            pool.wait_ge(consts, 12)
            nc.gpsimd.tensor_scalar(islot[:, :, :], iota[:, :, :], -NO_SLOT, None, ALU.add).then_inc(pool_chain, 1)
            for b in range(2):
                nc.gpsimd.tensor_scalar(ifurther[:, b, :], iota[0:NE, 0, :], float(b - NE), None, ALU.add).then_inc(pool_chain, 1)
            for b in range(MAX_EXTRA):
                nc.gpsimd.memset(fulls[:, b:b + 1], float(SLOTS * (b + 1))).then_inc(pool_chain, 1)
            done[0] += 3 + MAX_EXTRA
            pool.wait_ge(pool_chain, done[0])
            pool.dma_start(wdf[:, :, 0:16], win[:, C_DT:C_DT + 16].rearrange("(k p) n -> p k n", p=P)).then_inc(ld_small, 16)
            pool.dma_start(wdf[:, :, 16:24], win[:, C_F:C_F + 8].rearrange("(k p) n -> p k n", p=P)).then_inc(ld_small, 16)
            pool.dma_start(bdf[:, 0:16], dt_bias[0].partition_broadcast(P)).then_inc(ld_small, 16)
            pool.dma_start(bdf[:, 16:24], b_forget[0].partition_broadcast(P)).then_inc(ld_small, 16)
            pool.dma_start(alog[:, :], a_log[0].partition_broadcast(P)).then_inc(ld_small, 16)
            pool.dma_start(brt[:, :], b_router[0].partition_broadcast(P)).then_inc(ld_small, 16)
            pool.dma_start(dall[:, :], d_skip[0].partition_broadcast(P)).then_inc(ld_skip, 16)
            pool.dma_start(wrt[:, :, :], w_router[0].rearrange("(k p) n -> p k n", p=P)).then_inc(ld_small, 16)
            pool.wait_ge(ld_skip, 16)
            for j in range(2):
                rows = slice(64 * j, 64 * (j + 1))
                nc.gpsimd.tensor_copy(dsk[rows, :], dall[rows, j:SSD_H:2]).then_inc(dsk_ready, 1)
                pool.wait_ge(dsk_ready, j + 1)
            pool.wait_ge(ld_small, 16 * 7)
            pool.wait_ge(prm_ready, 1)
            nc.gpsimd.tensor_tensor(wrt[:, :, :], wrt[:, :, :],
                                    prm[:, G_FFN:G_FFN + KT].unsqueeze(2).to_broadcast([P, KT, NE]),
                                    ALU.mult).then_inc(wrt_ready, 1)
            pool.wait_ge(cb_ready, SSD_G)
            for h in range(SSD_H):
                pool.wait_ge(s_exp, h + 1)
                nc.gpsimd.tensor_tensor(dm[h % 4], dm[h % 4], cbm[:, h // 4, :], ALU.mult).then_inc(s_mt, 1)
            for n in range(2):
                for pair in (1, 2):
                    pool.wait_ge(squared, 4 * n + pair + 1)
                    link(nc.gpsimd.tensor_tensor(sq[:, 0:2, :], sq[:, 0:2, :], sq[:, 2 * pair:2 * pair + 2, :], ALU.add))
                nc.gpsimd.tensor_tensor(sq[:, 0, :], sq[:, 0, :], sq[:, 1, :], ALU.add).then_inc(sq_summed, 1)
            pool.wait_ge(w_done, 2 * NU)
            nc.gpsimd.memset(ys, 0.0).then_inc(y_ready, 1)
            nc.gpsimd.memset(sgT, 0.0).then_inc(sgt_ready, 1)

        @block.tensor
        def _(pe):
            mm = nc.tensor.matmul
            idn = ident[:, :]

            def transposes(src, n):
                for j in range(4):
                    if n:
                        pe.wait_ge(tr_copied, 4 * (n - 1) + j + 1)
                    elif j % 2 == 0:
                        pe.wait_ge(ld_xs[j // 2], 16)
                    for c in (2 * j, 2 * j + 1):
                        for tb in range(TB):
                            at = (c % 2) * S + tb * P
                            last = nc.tensor.transpose(ps[:, 4 + j, at:at + P], src[:, tb, c * P:(c + 1) * P], idn)
                    last.then_inc(tr_psum, 1)

            def mean_squares(squares, count, summed=0):
                for c in range(KT):
                    if summed and 1 <= c <= 5:
                        continue
                    if summed and c == 0:
                        pe.wait_ge(sq_summed, summed)
                    elif c % 2 == 0:
                        pe.wait_ge(squares, count + c // 2 + 1)
                    for tb in range(TB):
                        last = mm(ps[:, 3, 508 + tb:509 + tb], sq[:, c, tb * P:(tb + 1) * P], c_d[:, 0:1],
                                  start=(c == 0 and tb == 0), stop=(c == KT - 1), skip_group_check=True)
                last.then_inc(ms_psum, 1)

            def inverse_rows(n):
                pe.wait_ge(st_ready, n + 1)
                for tb in range(TB):
                    last = mm(ps[:, 3, tb * P:(tb + 1) * P], st[:, tb:tb + 1].to_broadcast([P, P]), idn,
                              start=True, stop=True)
                last.then_inc(ms_rows, 1)

            def project(name, n, act, ready=None, between=None):
                u = unit(name, n)
                a_hi, a_lo = act
                if u >= PJ:
                    on_act, count = drained(u - PJ)
                    pe.wait_ge(act_drained if on_act else dve_drained, count)

                def tile_ready(k):
                    if ready and k % ready[2] == 0:
                        pe.wait_ge(ready[0], ready[1] + k // ready[2] + 1)

                for j in range(2):
                    o = ps[:, u % PJ, j * 256:(j + 1) * 256]
                    if name in BY_TOKEN:
                        pe.wait_ge(w_lo_ready, 2 * u + 2)
                        slots, rows = slice(2 * (u % 2), 2 * (u % 2) + 2), slice(j * P, (j + 1) * P)
                        for k in range(KT):
                            wh, wl = w_hi[:, slots, k, :], w_lo[:, slots, k, :]
                            mm(o, a_hi[:, k, rows], wh, start=(k == 0), stop=False)
                            mm(o, a_hi[:, k, rows], wl, start=False, stop=False)
                            last = mm(o, a_lo[:, k, rows], wh, start=False, stop=(k == KT - 1))
                    else:
                        pe.wait_ge(w_lo_ready, 2 * u + j + 1)
                        s = (2 * u + j) % 4
                        for k in range(KT):
                            if j == 0:
                                tile_ready(k)
                            mm(o, w_hi[:, s, k, :], a_hi[:, k, :], start=(k == 0), stop=False)
                            mm(o, w_hi[:, s, k, :], a_lo[:, k, :], start=False, stop=False)
                            last = mm(o, w_lo[:, s, k, :], a_hi[:, k, :], start=False, stop=(k == KT - 1))
                        if j == 0:
                            last.then_inc(w_done, 1)
                            if between:
                                between()
                last.then_inc(w_done, 2 if name in BY_TOKEN else 1)

            pe.wait_ge(consts, 2)
            transposes(xin, 0)
            pe.wait_ge(ld_prm, 16 * 8)
            nc.tensor.transpose(ps[:, 3, 0:120], prow[0:120, :], ident[0:120, 0:120])
            nc.tensor.transpose(ps[:, 3, 120:136], prow2[:, :], ident[0:16, 0:16]).then_inc(prm_psum, 1)
            pe.wait_ge(prm_ready, 1)
            inverse_rows(0)
            project("xbc", 0, A_, (a_lo_ready, SPLIT["u"], 2))
            pe.wait_ge(ld_mem, 16)
            transposes(memin, 1)
            for n in range(1, 4):
                project("xbc", n, A_)
            project("xbc", 4, A_)
            pe.wait_ge(normed, 1)
            inverse_rows(1)
            for n in range(5, 8):
                project("xbc", n, A_)
            pe.wait_ge(ld_small, 16 * 7)
            pe.wait_ge(normed, 1)
            pe.wait_ge(tr_copied, 8)
            for k in range(KT):
                last = mm(ps[0:24, 4, 0:S], wdf[:, k, :], uT[:, k, :], start=(k == 0), stop=(k == KT - 1))
            last.then_inc(dft_psum, 1)
            project("z", 0, A_)
            pe.wait_ge(dft_ready, 1)
            for tb in range(TB):
                last = nc.tensor.transpose(ps[:, 5, 32 * tb:32 * tb + 24], dfT[:, tb * P:(tb + 1) * P], ident[0:24, 0:24])
            last.then_inc(df_psum, 1)
            project("z", 1, A_)
            pe.wait_ge(df_raw, 1)
            for j in range(4):
                tb, half = j // 2, j % 2
                pe.wait_ge(xc_ready, 4 * (half + 1))
                for c in range(4):
                    last = nc.tensor.transpose(ps[:, 4 + j, c * P:(c + 1) * P],
                                               xc[:, 4 * half + c, tb * P:(tb + 1) * P], idn)
                last.then_inc(xdt_psum, 1)
            project("z", 2, A_)
            pe.wait_ge(consts, 11)
            pe.wait_ge(df_ready, 1)
            pe.wait_ge(normed, 2)
            mm(ps[:, 3, 64:88], tri[:, 0:P], af[:, 0, :], start=True, stop=True)
            mm(ps[:, 3, 96:120], tri[:, P:2 * P], af[:, 0, :], start=True, stop=False)
            mm(ps[:, 3, 96:120], tri[:, 0:P], af[:, 1, :], start=False, stop=True)
            mm(ps[0:24, 3, 256:512], af[:, 0, :], tri[:, 0:S], start=True, stop=False)
            mm(ps[0:24, 3, 256 + P:512], af[:, 1, :], tri[:, 0:P], start=False, stop=True).then_inc(cum_psum, 1)
            pe.wait_ge(xc_ready, 16)
            for g in range(SSD_G):
                pe.wait_ge(xdt_ready, g + 1)
                mm(ps[:, 4 + g, 0:S], xc[:, 8 + g, 0:P], xc[:, 12 + g, :], start=True, stop=True)
                mm(ps[:, 4 + g, S:384], xc[:, 8 + g, P:S], xc[:, 12 + g, P:S], start=True, stop=True).then_inc(cb_psum, 1)
            project("z", 3, A_)
            pe.wait_ge(cum_ready, 3)

            def running_sum(bank, r):
                row = ident_r[0:24, r:r + 1].to_broadcast([24, P])
                mm(ps[:, bank, 0:S], row, acT[0][:, :], start=True, stop=False)
                return mm(ps[:, bank, 0:S], row, acT[1][:, :], start=False, stop=True)

            for h in range(SSD_H + 2):
                if h < SSD_H:
                    if h < 2:
                        pe.wait_ge(cb_ready, h + 1)
                    else:
                        pe.wait_ge(s_diff, 2 * (h - 1))
                    running_sum(4 + h % 2, h).then_inc(sb_psum, 1)
                if h in SSD_FILL:
                    project(*SSD_FILL[h], A_)
                if h >= 3 and h % 2 == 1:
                    c = (h - 3) // 2
                    if c < 2:
                        pe.wait_ge(cb_ready, SSD_G)
                    else:
                        pe.wait_ge(y_read, c - 1)
                    for keys in range(TB):
                        for y in (2 * c, 2 * c + 1):
                            if keys == 0:
                                pe.wait_ge(s_mt, y + 1)
                            o = ps[(y % 2) * 64:(y % 2) * 64 + 64, 6 + c % 2, :]
                            x_y = xdt[:, keys, y * 64:(y + 1) * 64]
                            if keys == 0:
                                mm(o[:, 0:S], x_y, dm[y % 4][:, 0:S], start=True, stop=False)
                            else:
                                mm(o[:, P:S], x_y, dm[y % 4][:, S:384], start=False, stop=True).then_inc(sy_psum, 1)

            def scores(h):
                if h >= 1:
                    pe.wait_ge(f_score, 4 * h)
                running_sum(4, SSD_H + h)
                mm(ps[:, 6 + h % 2, 0:P], qT[:, h, 0:P], kT[:, h, 0:P], start=True, stop=True)
                mm(ps[:, 6 + h % 2, P:384], qT[:, h, P:S], kT[:, h, :], start=True, stop=True).then_inc(f_psum, 1)

            pe.wait_ge(s_diff, 2 * SSD_H)
            pe.wait_ge(y_read, 7)
            pe.wait_ge(dve_drained, drained(unit("k", 3))[1])
            pe.wait_ge(act_drained, drained(unit("q", 3))[1])
            scores(0)
            project("gate", 0, A_)
            pe.wait_ge(gsq, KT)
            for tb in range(TB):
                for g in range(SSD_G):
                    for j in range(2):
                        last = mm(ps[:, 5, 4 * tb + g:4 * tb + g + 1], sq[:, 2 * g + j, tb * P:(tb + 1) * P],
                                  c_g[:, 0:1], start=(j == 0), stop=(j == 1))
            last.then_inc(gms_psum, 1)
            project("gate", 1, A_)
            pe.wait_ge(y_read, 8)
            scores(1)
            pe.wait_ge(gst_ready, 1)
            for g in range(SSD_G):
                for tb in range(TB):
                    at = (g % 2) * S + tb * P
                    last = mm(ps[:, 3 + 2 * (g // 2), at:at + P], gst[:, tb, g:g + 1].to_broadcast([P, P]), idn,
                              start=True, stop=True)
            last.then_inc(g_rows, 1)
            for h in range(1, FOX_H + 1):
                if FOX_FILL[h][0] == "gate":
                    project(*FOX_FILL[h], A_)
                else:
                    project(*FOX_FILL[h], B_, (a_lo_ready, SPLIT["yssd"], 2))
                if h == 1:
                    pe.wait_ge(y_normed, KT)
                y = h - 1
                pe.wait_ge(f_norm, 2 * h)
                for j in range(3):
                    last = nc.tensor.transpose(ps[:, 3, j * P:(j + 1) * P], ft[y % 2][:, j * P:(j + 1) * P], idn)
                last.then_inc(pt_psum, 1)
                if h + 1 < FOX_H:
                    scores(h + 1)
                pe.wait_ge(pt_copied, y + 1)
                if y >= 1:
                    pe.wait_ge(yf_lo, y)
                o = ps[:, 5, 0:S]
                mm(o, V[:, 0, y * P:(y + 1) * P], PT[:, 0:S], start=True, stop=False)
                mm(o[:, P:S], V[:, 1, y * P:(y + 1) * P], PT[:, S:384], start=False, stop=True).then_inc(fo_psum, 1)
            for n in range(2, 4):
                project("ssd", n, B_)
            project("fox", 0, C_, (yf_lo, 0, 1))
            for n in range(1, 4):
                project("fox", n, C_)
            project("ck", 0, B_, (a_lo_ready, SPLIT["mu"], 2))
            project("out", 0, A_, (a_lo_ready, SPLIT["merged"], 2))
            for n in range(1, 4):
                project("out", n, A_)
            project("ck", 1, B_, between=lambda: mean_squares(squared, 0, 1))
            inverse_rows(2)
            project("ck", 2, B_)
            project("ck", 3, B_)
            project("cq", 0, C_, (a_lo_ready, SPLIT["u2"], 2))
            for n in range(1, 4):
                project("cq", n, C_)
            for h in range(X_H + 1):
                if h < X_H:
                    if h == 0:
                        pe.wait_ge(dve_drained, drained(unit("ck", 3))[1])
                    if h >= 2:
                        pe.wait_ge(x_exp, 2 * (h - 1))
                    pe.wait_ge(act_drained, drained(unit("cq", h))[1])
                    for b in range(TB):
                        for j in range(2):
                            last = mm(ps[:, 6 + h % 2, b * S:(b + 1) * S], qx[:, 2 * h + j, b * P:(b + 1) * P],
                                      kxT[:, 2 * h + j, :], start=(j == 0), stop=(j == 1))
                    last.then_inc(x_psum, 1)
                y = h - 1
                if h >= 1:
                    pe.wait_ge(x_norm, 2 * h)
                    for m in range(TB):
                        for b in range(TB):
                            at = m * S + b * P
                            last = nc.tensor.transpose(ps[:, 3, at:at + P],
                                                       xp[y % 2][:, b * S + m * P:b * S + (m + 1) * P], idn)
                    last.then_inc(xpt_psum, 1)
                if h < X_H:
                    project("cv", h, B_)
                if h >= 1:
                    pe.wait_ge(dve_drained, drained(unit("cv", y))[1])
                    pe.wait_ge(xpt_copied, y + 1)
                    if y >= 2:
                        pe.wait_ge(ox_lo, y - 1)
                    for j in range(2):
                        for m in range(TB):
                            last = mm(ps[:, 4 + y % 2, j * S:(j + 1) * S],
                                      Vx[:, m, (2 * y + j) * P:(2 * y + j + 1) * P],
                                      xPT[:, m * S:(m + 1) * S], start=(m == 0), stop=(m == TB - 1))
                    last.then_inc(xo_psum, 1)
            def logits(n):
                for c in (2 * n, 2 * n + 1):
                    last = mm(ps[0:NE, 0, 0:S], wrt[:, c, :], hT[:, c, :], start=(c == 0), stop=(c == KT - 1))
                return last

            def by_token(c):
                for tb in range(TB):
                    last = mm(ps[:, 4 + 2 * tb + c // 4, (c % 4) * P:(c % 4 + 1) * P],
                              hT[:, c, tb * P:(tb + 1) * P], idn, start=(c % 4 == 0), stop=False,
                              skip_group_check=True)
                    if c % 4 == 3:
                        last.then_inc(tok_psum, 1)

            def pair(n):
                pe.wait_ge(dve_drained, drained(unit("co", n))[1])
                if n == 1:
                    pe.wait_ge(wrt_ready, 1)
                    logits(0)
                if n >= 1:
                    logits(n)
                by_token(2 * n)
                by_token(2 * n + 1)

            project("co", 0, A_, (ox_lo, 0, 2))
            project("co", 1, A_)
            pair(0)
            project("co", 2, A_)
            pair(1)
            project("co", 3, A_)
            pair(2)
            pe.wait_ge(dve_drained, drained(unit("co", 3))[1])
            logits(3).then_inc(lgt_psum, 1)
            mean_squares(squared, 4, 2)
            by_token(6)
            pe.wait_ge(lgt_ready, 1)
            for tb in range(TB):
                last = nc.tensor.transpose(ps[:, 1, NE * tb:NE * (tb + 1)], lgT[:, tb * P:(tb + 1) * P], ident[0:NE, 0:NE])
            last.then_inc(lg_psum, 1)
            by_token(7)
            def keep_clock(bank, n):
                for _ in range(n):
                    mm(ps[:, bank, 0:S], idn, tri[:, 0:S], start=True, stop=True)

            keep_clock(0, 8)
            pe.wait_ge(msk_ready, 1)
            mm(ps[0:NE, 2, 0:1], msk[:, 0, :], tri[:, P:P + 1], start=True, stop=False)
            mm(ps[0:NE, 2, 0:1], msk[:, 1, :], tri[:, P:P + 1], start=False, stop=True).then_inc(cnt_psum, 1)
            mm(ps[:, 0, 0:NE], tri[:, 0:P], msk[:, 0, :], start=True, stop=True)
            mm(ps[:, 0, NE:2 * NE], tri[:, P:2 * P], msk[:, 0, :], start=True, stop=False)
            mm(ps[:, 0, NE:2 * NE], tri[:, 0:P], msk[:, 1, :], start=False, stop=True).then_inc(pos_psum, 1)
            pe.wait_ge(extra_ready, 1)
            mm(ps[0:NE, 1, 0:1], tri[0:NE, 0:NE], ec[:, 1:2], start=True, stop=True)
            mm(ps[0:1, 1, 1:2], tri[0:NE, P:P + 1], ec[:, 1:2], start=True, stop=True).then_inc(off_psum, 1)
            pe.wait_ge(posm_ready, 1)
            for tb in range(TB):
                last = nc.tensor.transpose(ps[0:NE, 2, tb * P:(tb + 1) * P], posm[:, tb, :], idn)
            last.then_inc(ptr_psum, 1)
            keep_clock(0, 1)
            pe.wait_ge(gt_ready, 1)
            for tb in range(TB):
                last = nc.tensor.transpose(ps[0:NE, 3, tb * P:(tb + 1) * P], gt[:, tb, :], idn)
            last.then_inc(ptr_psum, 1)
            keep_clock(0, 3)
            pe.wait_ge(table_ready, 1)
            pe.wait_ge(ptr_ready, 1)
            for tb in range(TB):
                mm(ps[:, 0, 128 + NI * tb:128 + NI * (tb + 1)], posT[:, tb * P:(tb + 1) * P], pe1[:, :], start=True, stop=False)
                last = mm(ps[:, 0, 128 + NI * tb:128 + NI * (tb + 1)], c_s[0:NE, :], pb2[:, :], start=False, stop=True)
            last.then_inc(item_psum, 1)
            pe.wait_ge(ptr_ready, 2)
            for tb in range(TB):
                mm(ps[:, 1, 256 + NI * tb:256 + NI * (tb + 1)], gtT[:, tb * P:(tb + 1) * P], pe1[:, :], start=True, stop=True)
            mm(ps[0:1, 1, 384:384 + NI], rowf[0:NE, :], pe1[:, :], start=True, stop=True).then_inc(item_psum, 1)
            xg_cols = xgT.rearrange("p (m a j) -> p m a j", m=4, a=2)
            at_cols = actT.rearrange("p (m a j) -> p m a j", m=4, a=2)

            def gather(i1):
                pe.wait_ge(sel_ready, 2 * i1)
                for tb in range(TB):
                    for half in range(2):
                        last = mm(ps[64 * half:64 * (half + 1), 2, :], sel[:, 64 * tb:64 * (tb + 1)],
                                  xtok[:, tb, 512 * half:512 * (half + 1)], start=(tb == 0), stop=(tb == TB - 1))
                last.then_inc(xg_psum, 1)

            def gathered_transposes(i1):
                pe.wait_ge(xg_copied, i1)
                for m in range(4):
                    last = nc.tensor.transpose(ps[:, 2, m * P:(m + 1) * P], xgs[:, m * P:(m + 1) * P], idn)
                last.then_inc(xgt_psum, 1)

            def scatter(each=None):
                for tb in range(TB):
                    for half in range(2):
                        rows = slice(64 * half, 64 * (half + 1))
                        last = mm(ps[:, 4 + 2 * tb + half, :], sgT[rows, tb * P:(tb + 1) * P], ys[rows, :],
                                  start=False, stop=bool(each), skip_group_check=True)
                    if each:
                        last.then_inc(each, 1)
                return last

            gather(1)
            keep_clock(3, 2)
            gathered_transposes(1)
            keep_clock(3, 2)
            pe.wait_ge(ld_b1, 16)
            pe.wait_ge(tok_ready, 4)
            pe.wait_ge(item_ready, 2)
            pe.wait_ge(meta_ready, 1)
            n_items = pe.value_load(meta[0:1, NI:NI + 1], min_val=NE, max_val=MAX_ITEMS)

            def item(i, outside, loads):
                pe.wait_ge(xgt_ready, i + 1)
                for s in range(8):
                    if s < XN:
                        pe.wait_ge((x_loaded if outside else e_loaded)[s], loads)
                    else:
                        pe.wait_ge(e_loaded[s], 16 * i + 16)
                    for b in range(2):
                        for half in range(2):
                            last = mm(ps[64 * half:64 * (half + 1), b, :], xg_cols[:, s % 4, s // 4, :],
                                      e_slot(s, outside)[:, b * DE + 512 * half:b * DE + 512 * (half + 1)],
                                      start=(s == 0), stop=(s == 7))
                    last.then_inc(h_psum if s == 7 else e_used, 2 if s == 0 else 1)
                    if s == 3:
                        pe.wait_ge(selb_ready, i + 1)
                        for b in range(2):
                            for half in range(2):
                                mm(ps[64 * half:64 * (half + 1), b, :], selb[0:NE, :],
                                   b1[0:NE, b * DE + 512 * half:b * DE + 512 * (half + 1)], start=False, stop=False)
                pe.wait_ge(y_ready, i + 1)
                pe.wait_ge(sgt_ready, i + 1)
                scatter().then_inc(e_used, 1)
                gather(i + 2)
                pe.wait_ge(sg_ready, 2 * i + 2)
                for tb in range(TB):
                    last = nc.tensor.transpose(ps[:, 3, tb * P:(tb + 1) * P], sg[:, tb * P:(tb + 1) * P], idn)
                last.then_inc(sgt_psum, 1)
                gathered_transposes(i + 2)
                pe.wait_ge(act_ready, i + 1)
                for m in range(4):
                    last = nc.tensor.transpose(ps[:, 0, m * P:(m + 1) * P], lin[:, m * P:(m + 1) * P], idn)
                last.then_inc(at_psum, 1)
                pe.wait_ge(at_ready, i + 1)
                pe.wait_ge(sgt_ready, i + 2)
                for s in range(8, 12):
                    pe.wait_ge(e_loaded[s], 16 * i + 16)
                    for c in range(2):
                        k = 2 * (s - 8) + c
                        for half in range(2):
                            last = mm(ps[64 * half:64 * (half + 1), 3, :], at_cols[:, k % 4, k // 4, :],
                                      e_slot(s)[:, c, 512 * half:512 * (half + 1)],
                                      start=(k == 0), stop=(k == 7))
                    last.then_inc(e_used if s < 11 else y_psum, 1)

            def two_items(pair):
                item(2 * pair, False, 16 * pair + 16)
                item(2 * pair + 1, True, 16 * pair + 16)

            with pe.Fori(0, NE // 4) as pair:
                two_items(pair)
            pe.wait_ge(ld_b2, 16)
            for j in range(4):
                mm(ps[:, 4 + j, :], gtT[:, (j // 2) * P:(j // 2 + 1) * P], b2[0:NE, (j % 2) * 512:(j % 2 + 1) * 512],
                   start=False, stop=False, skip_group_check=True)
            with pe.Fori(NE // 4, NE // 2) as pair:
                two_items(pair)
            with pe.If(n_items > NE):
                with pe.Fori(NE, n_items) as i:
                    item(i, False, 16 * i - 16 * (NE // 2 - 1))
            pe.wait_ge(y_ready, n_items + 1)
            scatter(acc_done)

        @block.scalar
        def _(act):
            A = nc.scalar.activation
            done = [0]

            def link(ins):
                done[0] += 1
                ins.then_inc(act_chain, 1)
                act.wait_ge(act_chain, done[0])

            def squares(n, src):
                for tb in range(TB):
                    A(page(21, D, D * tb), src[:, tb, :], ACT.Square, accum_out=smal[:, tb, 2:3]).then_inc(tr_squared, 1)

            def root(n):
                act.wait_ge(*((tr_squared, 2 * n + 2) if n < 2 else (ms_psum, n - 1)))
                if n:
                    act.wait_ge(st_ready, n)
                    act.wait_ge(ms_rows, n)
                if n < 2:
                    A(st[:, :], smal[:, :, 2], ACT.Sqrt, scale=1.0 / D, bias=eps[:, :]).then_inc(ms_root, 1)
                else:
                    A(st[:, :], ps[:, 3, 508:508 + TB], ACT.Sqrt, bias=eps[:, :]).then_inc(ms_root, 1)

            def split_weights(u):
                if u == NU:
                    return
                act.wait_ge(w_loaded[u % 2], 16 * (u // 2 + 1))
                for j in range(2):
                    p = 2 * u + j
                    if p >= 4:
                        act.wait_ge(w_done, p - 3)
                    A(w_hi[:, p % 4, :, :], raw_w[u % 2][:, :, j * P:(j + 1) * P], ACT.Copy).then_inc(w_hi_ready, 1)

            def split_act(name, src, dst, ready, count, step):
                for j in range(4):
                    act.wait_ge(ready, count + step * (j + 1))
                    A(dst[0][:, 2 * j:2 * j + 2, :], src[:, 2 * j:2 * j + 2, :], ACT.Copy).then_inc(a_hi_ready, 1)

            def silu(n):
                for c in (2 * n, 2 * n + 1):
                    act.wait_ge(conved, c + 1)
                    A(xc[:, c, :], xc[:, c, :], ACT.Silu, bias=prm[:, CB + c:CB + c + 1]).then_inc(xc_ready, 1)

            def step(name, n):
                split_weights(unit(name, n) + 1)
                drain(name, n)

            def drain(name, n):
                u = unit(name, n)
                if name not in ON_ACT:
                    return
                act.wait_ge(w_done, 2 * u + 2)
                bank = ps[:, u % PJ, :]
                two = bank.rearrange("p (a b) -> p a b", a=2)
                if name == "xbc":
                    ins = A(xb[:, 2 * n:2 * n + 2, 4:4 + S], two, ACT.Copy)
                elif name == "z":
                    ins = A(zs[:, 2 * n:2 * n + 2, :], two, ACT.Silu)
                elif name == "q":
                    ins = A(qT[:, 2 * n:2 * n + 2, :], two, ACT.Copy, scale=FOX_SCALE)
                elif name == "cq":
                    ins = A(qx[:, 2 * n:2 * n + 2, :], two, ACT.Copy, scale=X_SCALE)
                else:
                    for j in range(2):
                        c = 2 * n + j
                        ins = A(gate[:, c, :], bank[:, j * S:(j + 1) * S], ACT.Identity,
                                bias=prm[:, B_GATE + c:B_GATE + c + 1])
                ins.then_inc(act_drained, 1)

            act.wait_ge(consts, 3)
            A(warm, eps[:, :], ACT.Square)
            for half in range(2):
                act.wait_ge(ld_xs[half], 16)
            squares(0, xin)
            root(0)
            split_weights(0)
            split_act("u", uT, A_, normed_tiles, 0, 1)
            act.wait_ge(consts, 12)
            for n in range(8):
                step("xbc", n)
                if n == 1:
                    act.wait_ge(ld_mem, 16)
                    act.wait_ge(ms_root, 1)
                    squares(1, memin)
                if n == 3:
                    root(1)
                act.wait_ge(act_drained, n + 1)
                for c in (2 * n, 2 * n + 1):
                    A(xc[:, c, :], xb[:, c, 1:1 + S], ACT.Copy, scale=prm[:, CW + c:CW + c + 1]).then_inc(conv_begun, 1)
                if n >= 2:
                    silu(n - 2)
            split_weights(unit("z", 1))
            silu(6)
            silu(7)
            drain("z", 0)
            split_weights(unit("z", 2))
            act.wait_ge(df_raw, 1)
            link(A(sp[:, :, :], raw[:, :, :], ACT.Abs))
            link(A(sp[:, :, :], sp[:, :, :], ACT.Exp, scale=-1.0))
            A(alog[:, :], alog[:, :], ACT.Exp).then_inc(df_soft, 1)
            A(sp[:, :, :], sp[:, :, :], ACT.Ln, bias=1.0).then_inc(df_soft, 1)
            drain("z", 1)
            step("z", 2)
            step("z", 3)
            for h in range(SSD_H + 3):
                if h < SSD_H:
                    act.wait_ge(s_diff, 2 * h + 2)
                    A(dm[h % 4], dm[h % 4], ACT.Exp).then_inc(s_exp, 1)
                if h in SSD_FILL:
                    step(*SSD_FILL[h])
                if h >= 3 and h % 2 == 1:
                    c = (h - 3) // 2
                    act.wait_ge(gated, c + 1)
                    A(sq[:, c, :], zs[:, c, :], ACT.Square).then_inc(gsq, 1)

            def exps(h):
                act.wait_ge(f_score, 4 * h + 4)
                t = ft[h % 2]
                A(t[:, 0:P], t[:, 0:P], ACT.Exp, bias=mx[:, h % 2, 0:1], accum_out=rsum[:, h % 2, 0:1]).then_inc(f_exp, 1)
                A(t[:, P:384], t[:, P:384], ACT.Exp, bias=mx[:, h % 2, 1:2], accum_out=rsum[:, h % 2, 1:2]).then_inc(f_exp, 1)

            split_weights(unit("gate", 1))
            exps(0)
            drain("gate", 0)
            act.wait_ge(gms_psum, 1)
            A(gst[:, :, :], ps[:, 5, 0:TB * SSD_G].rearrange("p (a b) -> p a b", a=TB), ACT.Sqrt, bias=eps[:, :]).then_inc(g_root, 1)
            step("gate", 1)

            def gate_sigmoid(branch):
                tiles_ = slice(8 * branch, 8 * branch + 8)
                A(gate[:, tiles_, :], gate[:, tiles_, :], ACT.Sigmoid).then_inc(gate_sig, 1)

            for h in range(1, FOX_H + 1):
                split_weights(unit(*FOX_FILL[h]) + 1)
                if h < FOX_H:
                    exps(h)
                if h == 1:
                    split_act("yssd", zs, B_, y_normed, 0, 2)
                y = h - 1
                act.wait_ge(pt_psum, y + 1)
                if y >= 1:
                    act.wait_ge(fo_psum, y)
                A(PT, ps[:, 3, 0:384], ACT.Copy).then_inc(pt_copied, 1)
                drain(*FOX_FILL[h])
                act.wait_ge(fo_psum, y + 1)
                if y == 0:
                    act.wait_ge(a_lo_ready, SPLIT["yssd"] + 4)
                A(C_[0][:, y, :], ps[:, 5, 0:S], ACT.Copy).then_inc(yf_hi, 1)
                if h == 7:
                    act.wait_ge(act_drained, drained(unit("gate", 7))[1])
                    gate_sigmoid(0)
            gate_sigmoid(1)
            for n in range(2, 4):
                step("ssd", n)
            for n in range(4):
                step("fox", n)
                if n == 0:
                    act.wait_ge(w_done, 2 * unit("ssd", 3) + 2)
                    split_act("mu", muT, B_, normed, 2, 0)
                act.wait_ge(merge_made, n + 1)
                A(A_[0][:, 2 * n:2 * n + 2, :], merged[:, 2 * n:2 * n + 2, :], ACT.Copy).then_inc(a_hi_ready, 1)
            step("ck", 0)
            def pair_square(name, n):
                act.wait_ge(dve_drained, drained(unit(name, n))[1])
                A(sq[:, 2 * n:2 * n + 2, :], hT[:, 2 * n:2 * n + 2, :], ACT.Square).then_inc(squared, 1)

            for n in range(4):
                step("out", n)
                if n:
                    pair_square("out", n - 1)
            pair_square("out", 3)
            step("ck", 1)
            root(2)
            step("ck", 2)
            split_act("u2", uT, C_, normed_tiles, 4, 1)
            step("ck", 3)
            for n in range(4):
                step("cq", n)
            for h in range(X_H + 1):
                y = h - 1
                if h < X_H:
                    act.wait_ge(x_max, h + 1)
                    if h >= 2:
                        act.wait_ge(xpt_psum, h - 1)
                    for b in range(TB):
                        A(xp[h % 2][:, S * b:S * (b + 1)], ps[:, 6 + h % 2, S * b:S * (b + 1)], ACT.Exp,
                          bias=mx[:, h % 2, b:b + 1], accum_out=rsum[:, h % 2, b:b + 1]).then_inc(x_exp, 1)
                if h >= 1:
                    act.wait_ge(xpt_psum, y + 1)
                    if y >= 1:
                        act.wait_ge(xo_psum, y)
                    A(xPT, ps[:, 3, :], ACT.Copy).then_inc(xpt_copied, 1)
                if h < X_H:
                    step("cv", h)
                if h >= 1:
                    act.wait_ge(xo_psum, y + 1)
                    A(A_[0][:, 2 * y:2 * y + 2, :].rearrange("p a b -> p (a b)"), ps[:, 4 + y % 2, :], ACT.Copy).then_inc(ox_hi, 1)
            step("co", 0)
            for n in range(4):
                if n < 3:
                    step("co", n + 1)
                pair_square("co", n)
            root(3)

            def tokens(tb):
                for half in range(2):
                    act.wait_ge(tok_psum, 2 * half + 2)
                    A(xtok[:, tb, 512 * half:512 * (half + 1)], ps[:, 4 + 2 * tb + half, :], ACT.Copy,
                      scale=st[:, tb:tb + 1]).then_inc(tok_ready, 1)

            act.wait_ge(st_ready, 4)
            tokens(0)
            act.wait_ge(top_ready, 1)
            for tb in range(TB):
                A(em[:, tb, :], lg[:, tb, :], ACT.Exp, bias=smal[:, tb, 0:1]).then_inc(ex_ready, 1)
            tokens(1)
            act.wait_ge(ptr_psum, 1)
            A(posT[:, :], ps[0:NE, 2, 0:S], ACT.Copy).then_inc(ptr_ready, 1)
            act.wait_ge(ptr_psum, 2)
            A(gtT[:, :], ps[0:NE, 3, 0:S], ACT.Copy).then_inc(ptr_ready, 1)

            def gathered_copy(i1):
                act.wait_ge(xg_psum, i1)
                A(xgs, ps[:, 2, :], ACT.Copy).then_inc(xg_copied, 1)

            gathered_copy(1)
            act.wait_ge(meta_ready, 1)
            n_items = act.value_load(meta[0:1, NI:NI + 1], min_val=NE, max_val=MAX_ITEMS)
            with act.Fori(0, n_items) as i:
                act.wait_ge(glu_ready, i + 1)
                A(sig, glu, ACT.Sigmoid, scale=ALPHA).then_inc(sig_ready, 1)
                gathered_copy(i + 2)
                act.wait_ge(sgt_psum, i + 1)
                A(sgT, ps[:, 3, 0:S], ACT.Copy).then_inc(sgt_ready, 1)
                act.wait_ge(at_psum, i + 1)
                A(actT, ps[:, 0, :], ACT.Copy).then_inc(at_ready, 1)
                act.wait_ge(y_psum, i + 1)
                A(ys, ps[:, 3, :], ACT.Copy).then_inc(y_ready, 1)
            A(warm, eps[:, :], ACT.Sqrt)
            for tb in range(TB):
                act.wait_ge(acc_done, tb + 1)
                A(outsb[:, tb, :], ps[:, 4 + 2 * tb:6 + 2 * tb, :].rearrange("p a b -> p (a b)"), ACT.Square,
                  accum_out=smal[:, tb, 2:3]).then_inc(f_sq, 1)
                act.wait_ge(f_sq, tb + 1)
                A(smal[:, tb, 3:4], smal[:, tb, 2:3], ACT.Sqrt, scale=1.0 / D, bias=eps[:, :]).then_inc(f_root, 1)

        @block.vector
        def _(dve):
            V_ = nc.vector
            done = [0]

            def link(ins):
                done[0] += 1
                ins.then_inc(dve_chain, 1)
                dve.wait_ge(dve_chain, done[0])

            def inverse(n):
                dve.wait_ge(ms_root, n + 1)
                V_.reciprocal(st[:, :], st[:, :]).then_inc(st_ready, 1)

            def split_act(name, src, dst, j):
                dve.wait_ge(a_hi_ready, SPLIT[name] + j + 1)
                pair = slice(2 * j, 2 * j + 2)
                V_.tensor_tensor(dst[1][:, pair, :], src[:, pair, :], dst[0][:, pair, :].bitcast(f32),
                                 ALU.subtract).then_inc(a_lo_ready, 1)

            def apply_norm(n, src, dst, gain, name=None, pair=None):
                dve.wait_ge(ms_rows, n + 1)
                for c in range(KT):
                    ins = V_.scalar_tensor_tensor(out=dst[:, c, :], in0=src[:, c, :],
                                                  scalar=prm[:, gain + c:gain + c + 1], in1=ps[:, 3, 0:S],
                                                  op0=ALU.mult, op1=ALU.mult)
                    if name and c % 2 == 1 and c < KT - 1:
                        ins.then_inc(normed_tiles, 1)
                        if c >= 3:
                            split_act(name, dst, pair, c // 2 - 1)
                ins.then_inc(normed, 1)
                if name:
                    dve.wait_ge(normed, n + 1)
                    V_.engine_nop().then_inc(normed_tiles, 1)
                    split_act(name, dst, pair, 2)
                    split_act(name, dst, pair, 3)

            def copies(n, dst):
                for j in range(4):
                    dve.wait_ge(tr_psum, 4 * n + j + 1)
                    V_.tensor_copy(dst[:, 2 * j:2 * j + 2, :].rearrange("p a b -> p (a b)"), ps[:, 4 + j, :]).then_inc(tr_copied, 1)

            def split_weights(u):
                if u == NU:
                    return
                for j in range(2):
                    p = 2 * u + j
                    dve.wait_ge(w_hi_ready, p + 1)
                    V_.tensor_tensor(w_lo[:, p % 4, :, :], raw_w[u % 2][:, :, j * P:(j + 1) * P],
                                     w_hi[:, p % 4, :, :].bitcast(f32), ALU.subtract).then_inc(w_lo_ready, 1)

            def step(name, n):
                split_weights(unit(name, n) + 1)
                drain(name, n)

            def drain(name, n):
                u = unit(name, n)
                if name in ON_ACT:
                    return
                dve.wait_ge(w_done, 2 * u + 2)
                bank = ps[:, u % PJ, :]
                two = bank.rearrange("p (a b) -> p a b", a=2)
                pair = slice(2 * n, 2 * n + 2)
                if name == "k":
                    ins = V_.tensor_copy(kT[:, pair, :], two)
                elif name == "ck":
                    ins = V_.tensor_copy(kxT[:, pair, :], two)
                elif name == "v":
                    ins = V_.tensor_copy(V[:, :, 256 * n:256 * (n + 1)], two)
                elif name == "cv":
                    ins = V_.tensor_copy(Vx[:, :, 256 * n:256 * (n + 1)], two)
                elif name == "ssd":
                    ins = V_.tensor_tensor(merged[:, pair, :], two, gate[:, pair, :], ALU.mult)
                elif name == "fox":
                    link(V_.tensor_tensor(mtmp[:, pair, :], two, gate[:, 8 + 2 * n:10 + 2 * n, :], ALU.mult))
                    ins = V_.tensor_tensor(merged[:, pair, :], merged[:, pair, :], mtmp[:, pair, :], ALU.add)
                else:
                    ins = V_.tensor_tensor(hT[:, pair, :], hT[:, pair, :], two, ALU.add)
                ins.then_inc(dve_drained, 1)
                if name == "fox":
                    dve.wait_ge(dve_drained, drained(u)[1])
                    V_.engine_nop().then_inc(merge_made, 1)

            copies(0, hT)
            inverse(0)
            dve.wait_ge(prm_psum, 1)
            V_.tensor_copy(prm[:, 0:136], ps[:, 3, 0:136]).then_inc(prm_ready, 1)
            dve.wait_ge(prm_ready, 1)
            dve.wait_ge(tr_copied, 4)
            split_weights(0)
            apply_norm(0, hT, uT, G_MIX, "u", A_)

            def conv(n):
                pair = (2 * n, 2 * n + 1)
                for tap in range(1, 4):
                    for c in pair:
                        if tap == 1:
                            dve.wait_ge(conv_begun, c + 1)
                        else:
                            dve.wait_ge(dve_chain, done[0] - 1 if tap == 2 or c == pair[0] else done[0])
                        ins = V_.scalar_tensor_tensor(out=xc[:, c, :], in0=xb[:, c, 1 + tap:1 + tap + S],
                                                      scalar=prm[:, CW + 16 * tap + c:CW + 16 * tap + c + 1],
                                                      in1=xc[:, c, :], op0=ALU.mult, op1=ALU.add)
                        if tap < 3:
                            ins.then_inc(dve_chain, 1)
                            done[0] += 1
                        else:
                            ins.then_inc(conved, 1)

            for n in range(8):
                if n == 4:
                    inverse(1)
                step("xbc", n)
                if n == 0:
                    copies(1, muT)
                else:
                    conv(n - 1)
            step("z", 0)
            conv(7)
            dve.wait_ge(dft_psum, 1)
            V_.tensor_copy(dfT, ps[0:24, 4, 0:S]).then_inc(dft_ready, 1)
            apply_norm(1, muT, muT, G_MEM)
            dve.wait_ge(df_psum, 1)
            for tb in range(TB):
                last = V_.tensor_tensor(raw[:, tb, :], ps[:, 5, 32 * tb:32 * tb + 24], bdf[:, :], ALU.add)
            last.then_inc(df_raw, 1)
            dve.wait_ge(df_raw, 1)
            step("z", 1)
            dve.wait_ge(df_soft, 2)
            link(V_.scalar_tensor_tensor(out=dt[:, :, :], in0=raw[:, :, 0:16], scalar=0.0, in1=sp[:, :, 0:16],
                                         op0=ALU.max, op1=ALU.add))
            for tb in range(TB):
                V_.scalar_tensor_tensor(out=af[:, tb, 0:16], in0=dt[:, tb, :], scalar=-1.0, in1=alog[:, :],
                                        op0=ALU.mult, op1=ALU.mult)
            V_.scalar_tensor_tensor(out=af[:, :, 16:24], in0=raw[:, :, 16:24], scalar=0.0, in1=sp[:, :, 16:24],
                                    op0=ALU.min, op1=ALU.subtract).then_inc(df_ready, 1)
            for j in range(4):
                tb, half = j // 2, j % 2
                dve.wait_ge(xdt_psum, j + 1)
                V_.tensor_tensor(xdt[:, tb, 512 * half:512 * (half + 1)].rearrange("p (h e) -> p h e", e=64),
                                 ps[:, 4 + j, :].rearrange("p (h e) -> p h e", e=64),
                                 dt[:, tb, 8 * half:8 * half + 8].unsqueeze(2).to_broadcast([P, 8, 64]),
                                 ALU.mult).then_inc(xdt_ready, 1)
            step("z", 2)
            dve.wait_ge(cum_psum, 1)
            V_.tensor_copy(actok[:, :, :], ps[:, 3, 64:128].rearrange("p (a b) -> p a b", a=2)[:, :, 0:24]).then_inc(cum_ready, 1)
            link(V_.tensor_copy(acT[0][:, :], ps[0:24, 3, 256:512]))
            V_.tensor_tensor(acT[1][:, :], ps[0:24, 3, 256:512], acT[0][:, :].bitcast(f32), ALU.subtract).then_inc(cum_ready, 1)
            for g in range(SSD_G):
                dve.wait_ge(cb_psum, g + 1)
                V_.tensor_tensor(cbm[:, g, :], ps[:, 4 + g, 0:384], tri[:, :], ALU.mult).then_inc(cb_ready, 1)
            step("z", 3)
            dve.wait_ge(cum_ready, 2)
            dve.wait_ge(dsk_ready, 2)
            V_.tensor_copy(ident_r[:, :], ident[0:24, 0:24]).then_inc(cum_ready, 1)
            for h in range(SSD_H + 3):
                if h < SSD_H:
                    dve.wait_ge(sb_psum, h + 1)
                    if h >= 4:
                        dve.wait_ge(sy_psum, h - 3)
                    V_.tensor_scalar(dm[h % 4][:, 0:S], ps[:, 4 + h % 2, 0:S], actok[:, 0, h:h + 1], 0.0,
                                     ALU.subtract, ALU.min).then_inc(s_diff, 1)
                    V_.tensor_scalar(dm[h % 4][:, S:384], ps[:, 4 + h % 2, P:S], actok[:, 1, h:h + 1], 0.0,
                                     ALU.subtract, ALU.min).then_inc(s_diff, 1)
                if h in SSD_FILL:
                    step(*SSD_FILL[h])
                if h >= 3 and h % 2 == 1:
                    c = (h - 3) // 2
                    dve.wait_ge(sy_psum, 2 * c + 2)
                    V_.scalar_tensor_tensor(out=ytmp[c % 2], in0=xc[:, c, :], scalar=dsk[:, c:c + 1],
                                            in1=ps[:, 6 + c % 2, 0:S], op0=ALU.mult, op1=ALU.add).then_inc(y_read, 1)
                    dve.wait_ge(y_read, c + 1)
                    V_.tensor_tensor(zs[:, c, :], ytmp[c % 2], zs[:, c, :], ALU.mult).then_inc(gated, 1)

            def scores(h):
                cp, sc, t = ps[:, 4, :], ps[:, 6 + h % 2, :], ft[h % 2]
                dve.wait_ge(f_psum, h + 1)
                if h >= 2:
                    dve.wait_ge(pt_psum, h - 1)
                V_.scalar_tensor_tensor(out=negc[:, 0:P], in0=cp[:, 0:P], scalar=-1.0, in1=fmask[:, 0:P],
                                        op0=ALU.mult, op1=ALU.add)
                link(V_.scalar_tensor_tensor(out=negc[:, P:384], in0=cp[:, 0:S], scalar=-1.0, in1=fmask[:, P:384],
                                             op0=ALU.mult, op1=ALU.add))
                r = SSD_H + h
                V_.scalar_tensor_tensor(out=t[:, 0:P], in0=sc[:, 0:P], scalar=actok[:, 0, r:r + 1], in1=negc[:, 0:P],
                                        op0=ALU.add, op1=ALU.add).then_inc(f_score, 1)
                V_.scalar_tensor_tensor(out=t[:, P:384], in0=sc[:, P:384], scalar=actok[:, 1, r:r + 1],
                                        in1=negc[:, P:384], op0=ALU.add, op1=ALU.add).then_inc(f_score, 1)
                dve.wait_ge(f_score, 4 * h + 2)
                V_.reduce_max(mx[:, h % 2, 0:1], t[:, 0:P], AX.X, negate=True).then_inc(f_score, 1)
                V_.reduce_max(mx[:, h % 2, 1:2], t[:, P:384], AX.X, negate=True).then_inc(f_score, 1)

            def probabilities(h):
                t = ft[h % 2]
                dve.wait_ge(f_exp, 2 * h + 2)
                link(V_.reciprocal(rinv[:, h % 2, :], rsum[:, h % 2, :]))
                V_.tensor_scalar(t[:, 0:P], t[:, 0:P], rinv[:, h % 2, 0:1], None, ALU.mult).then_inc(f_norm, 1)
                V_.tensor_scalar(t[:, P:384], t[:, P:384], rinv[:, h % 2, 1:2], None, ALU.mult).then_inc(f_norm, 1)

            split_weights(unit("gate", 1))
            dve.wait_ge(s_mt, SSD_H)
            scores(0)
            probabilities(0)
            dve.wait_ge(g_root, 1)
            V_.reciprocal(gst[:, :, :], gst[:, :, :]).then_inc(gst_ready, 1)
            split_weights(unit("gate", 2))
            scores(1)
            dve.wait_ge(g_rows, 1)
            for c in range(KT):
                g = c // 2
                V_.scalar_tensor_tensor(out=zs[:, c, :], in0=zs[:, c, :], scalar=prm[:, G_SSD + c:G_SSD + c + 1],
                                        in1=ps[:, 3 + 2 * (g // 2), (g % 2) * S:(g % 2) * S + S],
                                        op0=ALU.mult, op1=ALU.mult).then_inc(y_normed, 1)
            for h in range(1, FOX_H + 1):
                if 1 < h < FOX_H:
                    scores(h)
                split_weights(unit(*FOX_FILL[h]) + 1)
                if h < FOX_H:
                    probabilities(h)
                if h == 1:
                    for j in range(4):
                        split_act("yssd", zs, B_, j)
                if h == 8:
                    dve.wait_ge(gate_sig, 1)
                    drain("ssd", 0)
                y = h - 1
                dve.wait_ge(yf_hi, h)
                V_.tensor_tensor(C_[1][:, y, :], ps[:, 5, 0:S], C_[0][:, y, :].bitcast(f32), ALU.subtract).then_inc(yf_lo, 1)
            drain("ssd", 1)
            for n in range(2, 4):
                step("ssd", n)
            dve.wait_ge(gate_sig, 2)
            for n in range(4):
                split_weights(unit("fox", n) + 1)
                if n == 0:
                    for j in range(4):
                        split_act("mu", muT, B_, j)
                drain("fox", n)
                if n:
                    split_act("merged", merged, A_, n - 1)
            split_act("merged", merged, A_, 3)
            step("ck", 0)
            for n in range(4):
                step("out", n)
            split_weights(unit("ck", 2))
            inverse(2)
            drain("ck", 1)
            dve.wait_ge(ms_rows, 3)

            def norm_pair(j):
                for c in (2 * j, 2 * j + 1):
                    ins = V_.scalar_tensor_tensor(out=uT[:, c, :], in0=hT[:, c, :], scalar=prm[:, G_CROSS + c:G_CROSS + c + 1],
                                                  in1=ps[:, 3, 0:S], op0=ALU.mult, op1=ALU.mult)
                ins.then_inc(normed_tiles, 1)

            norm_pair(0)
            norm_pair(1)
            split_weights(unit("ck", 3))
            norm_pair(2)
            norm_pair(3)
            for j in range(2):
                split_act("u2", uT, C_, j)
            drain("ck", 2)
            split_weights(unit("cq", 0))
            for j in range(2, 4):
                split_act("u2", uT, C_, j)
            drain("ck", 3)
            for n in range(4):
                step("cq", n)
            for h in range(X_H + 1):
                if h < X_H:
                    dve.wait_ge(x_psum, h + 1)
                    V_.tensor_reduce(mx[:, h % 2, :], ps[:, 6 + h % 2, :].rearrange("p (a b) -> p a b", a=2), AX.X,
                                     ALU.max, negate=True).then_inc(x_max, 1)
                    dve.wait_ge(x_exp, 2 * h + 2)
                    link(V_.reciprocal(rinv[:, h % 2, :], rsum[:, h % 2, :]))
                    for b in range(TB):
                        t = xp[h % 2][:, S * b:S * (b + 1)]
                        V_.tensor_scalar(t, t, rinv[:, h % 2, b:b + 1], None, ALU.mult).then_inc(x_norm, 1)
                    step("cv", h)
                if h >= 1:
                    y = h - 1
                    dve.wait_ge(ox_hi, h)
                    V_.tensor_tensor(A_[1][:, 2 * y:2 * y + 2, :].rearrange("p a b -> p (a b)"), ps[:, 4 + y % 2, :],
                                     A_[0][:, 2 * y:2 * y + 2, :].rearrange("p a b -> p (a b)").bitcast(f32),
                                     ALU.subtract).then_inc(ox_lo, 1)
            for n in range(4):
                step("co", n)
            dve.wait_ge(lgt_psum, 1)
            V_.tensor_copy(lgT[:, :], ps[0:NE, 0, 0:S]).then_inc(lgt_ready, 1)
            inverse(3)
            dve.wait_ge(lg_psum, 1)
            dve.wait_ge(st_ready, 4)
            for tb in range(TB):
                last = V_.scalar_tensor_tensor(out=lg[:, tb, :], in0=ps[:, 1, NE * tb:NE * (tb + 1)], scalar=st[:, tb:tb + 1],
                                               in1=brt[:, :], op0=ALU.mult, op1=ALU.add)
            link(last)
            for tb in range(TB):
                last = V_.max(v8[:, tb, :], lg[:, tb, :])
            link(last)
            V_.tensor_scalar(smal[:, :, 0], v8[:, :, 0], -1.0, None, ALU.mult).then_inc(top_ready, 1)
            for tb in range(TB):
                last = V_.max_index(i8[:, tb, :], v8[:, tb, :], lg[:, tb, :])
            link(last)
            link(V_.tensor_copy(i8f[:, :, :], i8[:, :, :]))
            for tb in range(TB):
                last = V_.tensor_tensor(chosen[:, tb, :, :], iota[:, 0, 0:NE].unsqueeze(1).to_broadcast([P, TOPK, NE]),
                                        i8f[:, tb, 0:TOPK].unsqueeze(2).to_broadcast([P, TOPK, NE]), ALU.is_equal)
            link(last)
            for tb in range(TB):
                last = V_.tensor_reduce(msk[:, tb, :], chosen[:, tb, :, :].rearrange("p k e -> p e k"), AX.X, ALU.add)
            last.then_inc(msk_ready, 1)
            dve.wait_ge(cnt_psum, 1)
            link(V_.tensor_copy(ec[:, 0:1], ps[0:NE, 2, 0:1]))
            V_.scalar_tensor_tensor(out=ec[:, 4:4 + MAX_EXTRA], in0=fulls[:, :], scalar=ec[:, 0:1], in1=tri[0:NE, P:P + MAX_EXTRA],
                                    op0=ALU.is_lt, op1=ALU.mult, accum_out=ec[:, 1:2]).then_inc(extra_ready, 1)
            dve.wait_ge(pos_psum, 1)
            dve.wait_ge(msk_ready, 1)
            V_.scalar_tensor_tensor(out=posm[:, :, :], in0=msk[:, :, :], scalar=-(NO_SLOT + 1.0),
                                    in1=ps[:, 0, 0:2 * NE].rearrange("p (a b) -> p a b", a=2),
                                    op0=ALU.mult, op1=ALU.add).then_inc(posm_ready, 1)
            dve.wait_ge(ex_ready, 2)
            for tb in range(TB):
                last = V_.scalar_tensor_tensor(out=gt[:, tb, :], in0=em[:, tb, :], scalar=1.0, in1=msk[:, tb, :],
                                               op0=ALU.mult, op1=ALU.mult, accum_out=smal[:, tb, 1:2])
            link(last)
            link(V_.reciprocal(smal[:, :, 1], smal[:, :, 1]))
            for tb in range(TB):
                last = V_.tensor_scalar(gt[:, tb, :], gt[:, tb, :], smal[:, tb, 1:2], None, ALU.mult)
            last.then_inc(gt_ready, 1)
            dve.wait_ge(extra_ready, 1)
            dve.wait_ge(off_psum, 1)
            V_.tensor_scalar(meta[0:1, NI:NI + 1], ps[0:1, 1, 1:2], float(NE), None, ALU.add)
            V_.tensor_copy(ec[:, 3:4], ps[0:NE, 1, 0:1])
            link(V_.tensor_tensor(ec[:, 2:3], ps[0:NE, 1, 0:1], ec[:, 1:2], ALU.subtract))
            link(V_.tensor_scalar(pe2[:, :], ifurther[:, 0, :], ec[:, 3:4], None, ALU.is_lt))
            link(V_.scalar_tensor_tensor(out=pe2[:, :], in0=ifurther[:, 0, :], scalar=ec[:, 2:3], in1=pe2[:, :],
                                         op0=ALU.is_ge, op1=ALU.mult))
            V_.scalar_tensor_tensor(out=pb2[:, :], in0=ifurther[:, 1, :], scalar=ec[:, 2:3], in1=pe2[:, :],
                                    op0=ALU.subtract, op1=ALU.mult)
            V_.tensor_tensor(pe1[:, :], pe2[:, :], ident[0:NE, 0:NI], ALU.add).then_inc(table_ready, 1)
            dve.wait_ge(item_psum, 1)
            V_.tensor_copy(ipos[:, :, :], ps[:, 0, 128:256].rearrange("p (a b) -> p a b", a=2)).then_inc(item_ready, 1)
            dve.wait_ge(item_ready, 1)
            dve.wait_ge(table_ready, 1)

            def selection(i, i1):
                for tb in range(TB):
                    V_.tensor_scalar(sel[:, 64 * tb:64 * (tb + 1)], islot[:, 0, :], ipos[:, tb, bass.ds(i, 1)], None,
                                     ALU.is_equal).then_inc(sel_ready, 1)

            def bias_row(i):
                V_.tensor_copy(selb[0:NE, :], pe1[:, bass.ds(i, 1)].to_broadcast([NE, SLOTS])).then_inc(selb_ready, 1)

            def gathered_columns(i1):
                dve.wait_ge(xgt_psum, i1)
                V_.tensor_tensor(xgT.rearrange("p (m a j) -> p m a j", m=4, a=2),
                                 ps[:, 2, :].rearrange("p (m a j) -> p m a j", m=4, a=2),
                                 prm[:, G_FFN:G_FFN + KT].rearrange("p (a m) -> p m a", a=2).unsqueeze(3).to_broadcast([P, 4, 2, SLOTS]),
                                 ALU.mult).then_inc(xgt_ready, 1)

            selection(0, 1)
            bias_row(0)
            dve.wait_ge(item_psum, 2)
            V_.tensor_copy(igate[:, :, :], ps[:, 1, 256:384].rearrange("p (a b) -> p a b", a=2)).then_inc(item_ready, 1)
            V_.tensor_copy(meta[0:1, 0:NI], ps[0:1, 1, 384:384 + NI]).then_inc(meta_ready, 1)
            dve.wait_ge(meta_ready, 1)
            gathered_columns(1)
            n_items = dve.value_load(meta[0:1, NI:NI + 1], min_val=NE, max_val=MAX_ITEMS)
            with dve.Fori(0, n_items) as i:
                dve.wait_ge(xg_psum, i + 1)
                selection(i + 1, i + 2)
                for tb in range(TB):
                    V_.tensor_scalar(sg[:, P * tb:P * (tb + 1)], islot[:, :, :].rearrange("p a b -> p (a b)"),
                                     ipos[:, tb, bass.ds(i, 1)], igate[:, tb, bass.ds(i, 1)],
                                     ALU.is_equal, ALU.mult).then_inc(sg_ready, 1)
                dve.wait_ge(h_psum, i + 1)
                V_.tensor_scalar(glu, ps[:, 0, :], LIMIT, None, ALU.min).then_inc(glu_ready, 1)
                V_.tensor_scalar(lin, ps[:, 1, :], LIMIT, -LIMIT, ALU.min, ALU.max).then_inc(dve_chain, 1)
                dve.wait_ge(dve_chain, 2 * i + (done[0] + 1))
                V_.scalar_tensor_tensor(out=lin, in0=lin, scalar=1.0, in1=glu, op0=ALU.add, op1=ALU.mult).then_inc(dve_chain, 1)
                dve.wait_ge(dve_chain, 2 * i + (done[0] + 2))
                dve.wait_ge(sig_ready, i + 1)
                V_.tensor_tensor(lin, lin, sig, ALU.mult).then_inc(act_ready, 1)
                bias_row(i + 1)
                gathered_columns(i + 2)
            dve.wait_ge(ld_g, 16)
            for tb in range(TB):
                dve.wait_ge(f_root, tb + 1)
                V_.reciprocal(smal[:, tb, 1:2], smal[:, tb, 3:4]).then_inc(f_inverse, 1)
                dve.wait_ge(f_inverse, tb + 1)
                for half in range(2):
                    cols = slice(512 * half, 512 * (half + 1))
                    V_.scalar_tensor_tensor(out=outsb[:, tb, cols], in0=ps[:, 4 + 2 * tb + half, :], scalar=smal[:, tb, 1:2],
                                            in1=gfin[:, cols], op0=ALU.mult, op1=ALU.mult).then_inc(out_ready, 1)


INPUTS = ["x", "mem", "norm_mix_g", "w_in", "conv_w", "conv_b", "dt_bias", "a_log", "d_skip", "ssd_norm_g",
          "w_ssd_branch", "b_forget", "w_fox_branch", "b_gates", "w_out", "norm_cross_g", "norm_mem_g",
          "w_cross_q", "w_cross_kv", "w_cross_o", "norm_ffn_g", "w_router", "b_router", "w_expert_in",
          "b_expert_in", "w_expert_out", "b_expert_out", "norm_final_g"]


def kernel(**inputs):
    import concourse.bacc as bacc
    from concourse.bass_utils import run_bass_kernel_spmd

    nc = bacc.Bacc("TRN2", target_bir_lowering=False, num_devices=1)
    arrays, args = {}, []
    for name in INPUTS:
        a = np.ascontiguousarray(inputs[name])
        arrays[f"in_{name}"] = a
        args.append(nc.dram_tensor(f"in_{name}", a.shape, mybir.dt.from_np(a.dtype), kind="ExternalInput").ap())
    args.append(nc.dram_tensor("out_h", (1, S, D), mybir.dt.float32, kind="ExternalOutput").ap())
    layer_program(nc, *args)
    result = run_bass_kernel_spmd(nc, [arrays], core_ids=[0])
    return result.results[0]["out_h"]
```
